# Optimizing a Trainium2 kernel written in Bass

```python
import math
import jax, jax.numpy as jnp
from jax import lax
import numpy as np

D_MODEL = 1024
BATCH = 1
SEQ = 512
DEPTH = 1

N_META = 16
GLA_H = 4
GLA_DK = D_MODEL // 2 // GLA_H
GLA_DV = D_MODEL // GLA_H
GLA_LR = 16
GLA_TAU = 16.0
GLA_CHUNK = 64
DSA_H = 16
DSA_DH = D_MODEL // DSA_H
DSA_Q_LORA = D_MODEL // 4
DSA_KV_LAT = D_MODEL // 8
IDX_H = 8
IDX_D = 64
TOPK_MAX = 256
QBLK = 128
ML_H = 4
ML_DK = D_MODEL // 2 // ML_H
ML_DV = D_MODEL // ML_H
ML_CONV = 4
ML_CHUNK = 64
T5_BUCKETS = 32
T5_MAX_DIST = 128
D_FF = 4 * D_MODEL
EPS = 1e-6
NEG = -1e30

COL_SPLITS = (
    GLA_H * GLA_DK, GLA_H * GLA_DK, GLA_H * GLA_DV, GLA_H * GLA_DV, GLA_LR,
    DSA_Q_LORA, DSA_KV_LAT, IDX_D, IDX_H,
    ML_H * ML_DK, ML_H * ML_DK, ML_H * ML_DV, ML_H * ML_DV, ML_H, ML_H,
    D_MODEL, D_MODEL, D_MODEL,
)
N_COLS = sum(COL_SPLITS)

kernel_name = "hybrid_gla_dsa_mlstm_trunk"

def rms_norm(x, g):
    x32 = x.astype(jnp.float32)
    y = x32 * lax.rsqrt(jnp.mean(x32 * x32, axis=-1, keepdims=True) + EPS)
    return (y * g.astype(jnp.float32)).astype(x.dtype)

def layer_norm(x, g, b):
    x32 = x.astype(jnp.float32)
    mu = jnp.mean(x32, axis=-1, keepdims=True)
    var = jnp.mean(jnp.square(x32 - mu), axis=-1, keepdims=True)
    y = (x32 - mu) * lax.rsqrt(var + EPS) * g.astype(jnp.float32) + b.astype(jnp.float32)
    return y.astype(x.dtype)

def to_chunks(a, chunk):
    front = (-a.shape[1]) % chunk
    a = jnp.pad(a, [(0, 0), (front, 0)] + [(0, 0)] * (a.ndim - 2))
    b, tp = a.shape[:2]
    a = a.reshape(b, tp // chunk, chunk, *a.shape[2:])
    perm = (1, 0, 3, 2) + tuple(range(4, a.ndim))
    return a.transpose(perm), front

def from_chunks(a, front):
    a = a.transpose(1, 0, 3, 2, 4)
    b, nc, c, h, d = a.shape
    return a.reshape(b, nc * c, h, d)[:, front:]

def causal_dwconv(x, w):
    return lax.conv_general_dilated(
        x, w[:, None, :].astype(x.dtype), window_strides=(1,), padding=[(ML_CONV - 1, 0)],
        dimension_numbers=("NWC", "WIO", "NWC"), feature_group_count=x.shape[-1])

def t5_bucket(rel):
    n = jnp.maximum(rel, 0)
    max_exact = T5_BUCKETS // 2
    nf = jnp.maximum(n, 1).astype(jnp.float32)
    large = max_exact + (jnp.log(nf / max_exact) / math.log(T5_MAX_DIST / max_exact)
                         * (T5_BUCKETS - max_exact)).astype(jnp.int32)
    large = jnp.minimum(large, T5_BUCKETS - 1)
    return jnp.where(n < max_exact, n, large)

def gla_chunk_step(S, xs):
    q, k, v, g = xs
    C = q.shape[2]
    G = jnp.cumsum(g, axis=2)
    causal = jnp.tril(jnp.ones((C, C), bool))
    diff = G[:, :, :, None, :] - G[:, :, None, :, :]
    decay = jnp.exp(jnp.where(causal[None, None, :, :, None], diff, -jnp.inf))
    A = jnp.einsum("bhtk,bhtsk,bhsk->bhts", q, decay, k)
    o = jnp.einsum("bhtk,bhkv->bhtv", q * jnp.exp(G), S) + jnp.einsum("bhts,bhsv->bhtv", A, v)
    G_last = G[:, :, -1:, :]
    S_new = jnp.exp(G_last[:, :, 0, :])[..., None] * S + jnp.einsum(
        "bhsk,bhsv->bhkv", k * jnp.exp(G_last - G), v)
    return S_new, o

def gla_branch(q, k, v, r, a_lr, p):
    B, T = q.shape[:2]
    q = q.reshape(B, T, GLA_H, GLA_DK) * GLA_DK ** -0.5
    k = k.reshape(B, T, GLA_H, GLA_DK)
    v = v.reshape(B, T, GLA_H, GLA_DV)
    g = jax.nn.log_sigmoid((a_lr @ p["w_gla_a2"] + p["b_gla_a"]).astype(jnp.float32)) / GLA_TAU
    g = g.reshape(B, T, GLA_H, GLA_DK)
    qc, front = to_chunks(q, GLA_CHUNK)
    kc, _ = to_chunks(k, GLA_CHUNK)
    vc, _ = to_chunks(v, GLA_CHUNK)
    gc, _ = to_chunks(g, GLA_CHUNK)
    s0 = jnp.zeros((B, GLA_H, GLA_DK, GLA_DV), jnp.float32)
    _, oc = lax.scan(gla_chunk_step, s0, (qc, kc, vc, gc))
    o = from_chunks(oc, front)
    o = rms_norm(o, p["g_gla_head"]) * jax.nn.silu(r.reshape(B, T, GLA_H, GLA_DV))
    return o.reshape(B, T, GLA_H * GLA_DV).astype(v.dtype)

def dsa_branch(c_q, c_kv, k_idx, w_idx, p, t5_table):
    B, T = c_q.shape[:2]
    topk = min(TOPK_MAX, (T - N_META) // 4)
    cq = rms_norm(c_q, p["g_dsa_q"])
    q = (cq @ p["w_dsa_uq"]).reshape(B, T, DSA_H, DSA_KV_LAT) * DSA_KV_LAT ** -0.5
    qi = (cq @ p["w_idx_q"]).reshape(B, T, IDX_H, IDX_D) * IDX_D ** -0.5
    wi = w_idx * IDX_H ** -0.5
    kv = rms_norm(c_kv, p["g_dsa_kv"])
    ki = layer_norm(k_idx, p["idx_ln_g"], p["idx_ln_b"])

    front = (-T) % QBLK
    nblk = (T + front) // QBLK

    def blk(a):
        a = jnp.pad(a, [(0, 0), (front, 0)] + [(0, 0)] * (a.ndim - 2))
        return a.reshape(B, nblk, QBLK, *a.shape[2:]).swapaxes(0, 1)

    qpos = (jnp.arange(T + front, dtype=jnp.int32) - front).reshape(nblk, QBLK)
    kpos = jnp.arange(T, dtype=jnp.int32)

    def attend_block(args):
        qb, qib, wb, pb = args
        score = jnp.einsum("bqh,bqhs->bqs", wb,
                           jax.nn.relu(jnp.einsum("bqhd,bsd->bqhs", qib, ki))).astype(jnp.float32)
        score = jnp.where(kpos[None, None, :] <= pb[None, :, None], score, NEG)
        _, idx = lax.top_k(score, topk)
        kv_sel = jax.vmap(lambda kv_b, i_b: kv_b[i_b])(kv, idx)
        bias = t5_table[t5_bucket(pb[None, :, None] - idx)]
        logits = (jnp.einsum("bqhc,bqkc->bhqk", qb, kv_sel).astype(jnp.float32)
                  + bias.transpose(0, 3, 1, 2).astype(jnp.float32))
        logits = jnp.where((idx <= pb[None, :, None])[:, None], logits, NEG)
        prob = jax.nn.softmax(logits, axis=-1).astype(kv_sel.dtype)
        return jnp.einsum("bhqk,bqkc->bqhc", prob, kv_sel)

    o_lat = lax.map(attend_block, (blk(q), blk(qi), blk(wi), qpos))
    o_lat = o_lat.swapaxes(0, 1).reshape(B, nblk * QBLK, DSA_H, DSA_KV_LAT)[:, front:]
    o = jnp.einsum("bthc,hcd->bthd", o_lat, p["w_dsa_uv"])
    return o.reshape(B, T, DSA_H * DSA_DH)

def mlstm_chunk_step(carry, xs):
    Cs, ns, ms = carry
    q, k, v, li, lf = xs
    C = q.shape[2]
    causal = jnp.tril(jnp.ones((C, C), bool))
    b = jnp.cumsum(lf, axis=-1)
    D = jnp.where(causal, b[..., :, None] - b[..., None, :] + li[..., None, :], -jnp.inf)
    m_inter = b + ms[..., None]
    m = jnp.maximum(m_inter, jnp.max(D, axis=-1))
    w_inter = jnp.exp(m_inter - m)
    P = jnp.exp(D - m[..., None]) * jnp.einsum("bhtk,bhsk->bhts", q, k)
    num = w_inter[..., None] * jnp.einsum("bhtk,bhkv->bhtv", q, Cs) + jnp.einsum("bhts,bhsv->bhtv", P, v)
    den = w_inter * jnp.einsum("bhtk,bhk->bht", q, ns) + jnp.sum(P, axis=-1)
    h = num / jnp.maximum(jnp.abs(den), jnp.exp(-m))[..., None]
    b_last = b[..., -1]
    dec = b_last[..., None] - b + li
    m_new = jnp.maximum(b_last + ms, jnp.max(dec, axis=-1))
    w_old = jnp.exp(b_last + ms - m_new)
    w_new = jnp.exp(dec - m_new[..., None])
    Cs_new = w_old[..., None, None] * Cs + jnp.einsum("bhs,bhsk,bhsv->bhkv", w_new, k, v)
    ns_new = w_old[..., None] * ns + jnp.einsum("bhs,bhsk->bhk", w_new, k)
    return (Cs_new, ns_new, m_new), h

def mlstm_branch(q, k, v, o_pre, i_pre, f_pre, p):
    B, T = q.shape[:2]
    qk = jax.nn.silu(causal_dwconv(jnp.concatenate([q, k], axis=-1), p["ml_conv"]))
    q, k = jnp.split(qk, 2, axis=-1)
    q = q.reshape(B, T, ML_H, ML_DK) * ML_DK ** -0.5
    k = k.reshape(B, T, ML_H, ML_DK)
    v = v.reshape(B, T, ML_H, ML_DV)
    li = i_pre.astype(jnp.float32)
    lf = jax.nn.log_sigmoid(f_pre.astype(jnp.float32) + p["ml_f_bias"].astype(jnp.float32))
    qc, front = to_chunks(q, ML_CHUNK)
    kc, _ = to_chunks(k, ML_CHUNK)
    vc, _ = to_chunks(v, ML_CHUNK)
    lic, _ = to_chunks(li, ML_CHUNK)
    lfc, _ = to_chunks(lf, ML_CHUNK)
    init = (jnp.zeros((B, ML_H, ML_DK, ML_DV), jnp.float32),
            jnp.zeros((B, ML_H, ML_DK), jnp.float32),
            jnp.zeros((B, ML_H), jnp.float32))
    _, hc = lax.scan(mlstm_chunk_step, init, (qc, kc, vc, lic, lfc))
    h = from_chunks(hc, front)
    h = rms_norm(h, p["g_ml_head"]) * jax.nn.sigmoid(o_pre).reshape(B, T, ML_H, ML_DV)
    return h.reshape(B, T, ML_H * ML_DV).astype(v.dtype)

def hybrid_layer(h, p, t5_table):
    xn = rms_norm(h, p["g_pre_mix"])
    z = xn @ p["w_in"] + p["b_in"]
    (gla_q, gla_k, gla_v, gla_r, gla_a, dsa_cq, dsa_ckv, idx_k, idx_w,
     ml_q, ml_k, ml_v, ml_o, ml_i, ml_f, gate_a, gate_b, gate_c) = jnp.split(
        z, np.cumsum(COL_SPLITS)[:-1].tolist(), axis=-1)
    y_a = gla_branch(gla_q, gla_k, gla_v, gla_r, gla_a, p) @ p["w_br_gla"]
    y_b = dsa_branch(dsa_cq, dsa_ckv, idx_k, idx_w, p, t5_table) @ p["w_br_dsa"]
    y_c = mlstm_branch(ml_q, ml_k, ml_v, ml_o, ml_i, ml_f, p) @ p["w_br_ml"]
    mix = jax.nn.sigmoid(gate_a) * y_a + jax.nn.sigmoid(gate_b) * y_b + jax.nn.sigmoid(gate_c) * y_c
    h = h + rms_norm(mix @ p["w_out"], p["g_post_mix"])
    xn = rms_norm(h, p["g_pre_mlp"])
    u = jnp.square(jax.nn.relu(xn @ p["w_up"]))
    return h + rms_norm(u @ p["w_down"], p["g_post_mlp"])

def setup_inputs(seed: int = 0) -> dict:
    key = jax.random.key(seed)
    ks = jax.random.split(key, 32)
    f32 = jnp.float32
    L = DEPTH

    def nrm(k, shape, scale):
        return scale * jax.random.normal(k, shape, f32)

    def gain(k, shape):
        return 1.0 + 0.05 * jax.random.normal(k, shape, f32)

    return {
        "x": nrm(ks[0], (BATCH, SEQ, D_MODEL), 1.0),
        "meta_tokens": nrm(ks[1], (N_META, D_MODEL), 1.0),
        "t5_bias": nrm(ks[2], (T5_BUCKETS, DSA_H), 0.5),
        "g_pre_mix": gain(ks[3], (L, D_MODEL)),
        "w_in": nrm(ks[4], (L, D_MODEL, N_COLS), D_MODEL ** -0.5),
        "b_in": nrm(ks[5], (L, N_COLS), 0.01),
        "w_gla_a2": nrm(ks[6], (L, GLA_LR, GLA_H * GLA_DK), GLA_LR ** -0.5),
        "b_gla_a": nrm(ks[7], (L, GLA_H * GLA_DK), 0.1),
        "g_gla_head": gain(ks[8], (L, GLA_DV)),
        "w_br_gla": nrm(ks[9], (L, GLA_H * GLA_DV, D_MODEL), (GLA_H * GLA_DV) ** -0.5),
        "g_dsa_q": gain(ks[10], (L, DSA_Q_LORA)),
        "w_dsa_uq": nrm(ks[11], (L, DSA_Q_LORA, DSA_H * DSA_KV_LAT), DSA_Q_LORA ** -0.5),
        "w_idx_q": nrm(ks[12], (L, DSA_Q_LORA, IDX_H * IDX_D), DSA_Q_LORA ** -0.5),
        "g_dsa_kv": gain(ks[13], (L, DSA_KV_LAT)),
        "w_dsa_uv": nrm(ks[14], (L, DSA_H, DSA_KV_LAT, DSA_DH), DSA_KV_LAT ** -0.5),
        "idx_ln_g": gain(ks[15], (L, IDX_D)),
        "idx_ln_b": nrm(ks[16], (L, IDX_D), 0.01),
        "w_br_dsa": nrm(ks[17], (L, DSA_H * DSA_DH, D_MODEL), (DSA_H * DSA_DH) ** -0.5),
        "ml_conv": nrm(ks[18], (L, ML_CONV, 2 * ML_H * ML_DK), ML_CONV ** -0.5),
        "ml_f_bias": jnp.linspace(3.0, 6.0, ML_H, dtype=f32)[None, :] + nrm(ks[19], (L, ML_H), 0.1),
        "g_ml_head": gain(ks[20], (L, ML_DV)),
        "w_br_ml": nrm(ks[21], (L, ML_H * ML_DV, D_MODEL), (ML_H * ML_DV) ** -0.5),
        "w_out": nrm(ks[22], (L, D_MODEL, D_MODEL), D_MODEL ** -0.5),
        "g_post_mix": gain(ks[23], (L, D_MODEL)),
        "g_pre_mlp": gain(ks[24], (L, D_MODEL)),
        "w_up": nrm(ks[25], (L, D_MODEL, D_FF), D_MODEL ** -0.5),
        "w_down": nrm(ks[26], (L, D_FF, D_MODEL), D_FF ** -0.5),
        "g_post_mlp": gain(ks[27], (L, D_MODEL)),
    }

def reference(x, meta_tokens, t5_bias, g_pre_mix, w_in, b_in, w_gla_a2, b_gla_a, g_gla_head,
              w_br_gla, g_dsa_q, w_dsa_uq, w_idx_q, g_dsa_kv, w_dsa_uv, idx_ln_g, idx_ln_b,
              w_br_dsa, ml_conv, ml_f_bias, g_ml_head, w_br_ml, w_out, g_post_mix, g_pre_mlp,
              w_up, w_down, g_post_mlp):
    B = x.shape[0]
    meta = jnp.broadcast_to(meta_tokens.astype(x.dtype)[None], (B, N_META, x.shape[-1]))
    h = jnp.concatenate([meta, x], axis=1)
    for l in range(DEPTH):
        p = {
            "g_pre_mix": g_pre_mix[l], "w_in": w_in[l], "b_in": b_in[l],
            "w_gla_a2": w_gla_a2[l], "b_gla_a": b_gla_a[l], "g_gla_head": g_gla_head[l],
            "w_br_gla": w_br_gla[l],
            "g_dsa_q": g_dsa_q[l], "w_dsa_uq": w_dsa_uq[l], "w_idx_q": w_idx_q[l],
            "g_dsa_kv": g_dsa_kv[l], "w_dsa_uv": w_dsa_uv[l], "idx_ln_g": idx_ln_g[l],
            "idx_ln_b": idx_ln_b[l], "w_br_dsa": w_br_dsa[l],
            "ml_conv": ml_conv[l], "ml_f_bias": ml_f_bias[l], "g_ml_head": g_ml_head[l],
            "w_br_ml": w_br_ml[l],
            "w_out": w_out[l], "g_post_mix": g_post_mix[l], "g_pre_mlp": g_pre_mlp[l],
            "w_up": w_up[l], "w_down": w_down[l], "g_post_mlp": g_post_mlp[l],
        }
        h = hybrid_layer(h, p, t5_bias)
    return h[:, N_META:]


_drawn_inputs = setup_inputs


def setup_inputs(seed=0):
    import zlib

    import numpy as np

    out = dict(_drawn_inputs(seed))
    spreads = {}
    factors = {'g_dsa_kv': 4.233,
     'idx_ln_g': 2.724,
     'idx_ln_b': 5.459,
     'w_gla_a2': 3.667,
     'b_gla_a': 8.0,
     'g_gla_head': 7.783,
     'g_ml_head': 8.0}
    for name, (base, spread) in spreads.items():
        noise = np.random.default_rng([zlib.crc32(name.encode()), seed]).standard_normal(out[name].shape)
        drawn = base * np.exp(spread * noise) if base else spread * noise
        out[name] = __import__('jax').numpy.asarray(drawn.astype(out[name].dtype))
    for name, factor in factors.items():
        out[name] = (out[name] * factor).astype(out[name].dtype)
    return out
```

```python
import concourse.bass as bass
from concourse import mybir
from contextlib import ExitStack

FP32 = mybir.dt.float32
F32R = mybir.dt.float32r
BF16 = mybir.dt.bfloat16
U32 = mybir.dt.uint32
ACT = mybir.ActivationFunctionType
ALU = mybir.AluOpType

D = 1024
SEQ = 512
META = 16
ALL = META + SEQ
HALF = ALL // 2
P = 128
KT = D // P
QT = SEQ // P
HEADS = 4
DK = D // 2 // HEADS
DV = D // HEADS
DSA_H = 16
IDX_H = 8
TOPK = 128
FF = 4 * D
FT = FF // P
BUCKETS = 32
LINE = 655
LPITCH = 656
EPS = 1e-6
BIG = 1e30
MARK = -3e38
LEVELS = [64, 32, 16, 8, 4, 2, 1]
NRAW = 3
NHL = 4
CH = 1024

C_GQ, C_GK, C_GV, C_GR, C_GA = 0, 512, 1024, 2048, 3072
C_CQ, C_CKV, C_IK, C_IW = 3088, 3344, 3472, 3536
C_MQ, C_MK, C_MV, C_MO, C_MI, C_MF = 3544, 4056, 4568, 5592, 6616, 6620
C_GATE = 6624

ROWS = {}
ROW_LIST = []


def _rows():
    at = 0
    for name, n, src in [
        ("gq", 4, "b_in"), ("gk", 4, "b_in"), ("gr", 8, "b_in"), ("cq", 2, "b_in"), ("ckv", 1, "b_in"),
        ("ik", 1, "b_in"), ("mq", 4, "b_in"), ("mk", 4, "b_in"), ("mo", 8, "b_in"), ("gate", 24, "b_in"),
        ("ga", 1, "b_in"), ("mi", 1, "b_in"), ("mf", 1, "b_in"), ("a2", 4, "b_gla_a"), ("hg", 2, "g_gla_head"),
        ("hm", 2, "g_ml_head"), ("dq", 2, "g_dsa_q"), ("dkv", 1, "g_dsa_kv"), ("ig", 1, "idx_ln_g"),
        ("ib", 1, "idx_ln_b"), ("fb", 1, "ml_f_bias"), ("cv", 32, "ml_conv"),
    ]:
        ROWS[name] = at
        ROW_LIST.append((name, n, src))
        at += n
    return at


NROW = _rows()
COLUMNS = {"gq": C_GQ, "gk": C_GK, "gr": C_GR, "cq": C_CQ, "ckv": C_CKV, "ik": C_IK, "mq": C_MQ, "mk": C_MK,
           "mo": C_MO, "gate": C_GATE, "ga": C_GA, "mi": C_MI, "mf": C_MF}
WIDTHS = {"ga": 16, "mi": HEADS, "mf": HEADS, "fb": HEADS, "ik": 64, "ig": 64, "ib": 64}


def row_sources(a, name, count, src):
    w = WIDTHS.get(name, P)
    if src == "ml_conv":
        return [((8 * k, 0), a[src][0, k:k + 1, :].rearrange("k (t p) -> (k t) p", p=P)) for k in range(4)]
    c0 = COLUMNS.get(name, 0)
    part = a[src][0, c0:c0 + count * w].rearrange("(t p) -> t p", p=w)
    if w == 64:
        return [((0, 0), part), ((0, 64), part)]
    return [((0, 0), part)]


NROWDMA = 21 + 4 + 3


class Tile:

    def __init__(self, kind, m=P, kt=KT, both=False, rhs="x", off=0, width=P):
        self.kind, self.m, self.kt, self.both, self.rhs, self.off, self.width = kind, m, kt, both, rhs, off, width


def plan():
    chunks, tiles = [], {}
    state = {"done": 0, "slot": 0, "freed": [0, 0]}

    def tile(name, use, new=0, kind="F", **k):
        t = Tile(kind, **k)
        t.chunks = list(use)
        t.slot = state["slot"]
        state["slot"] ^= 1
        t.need = state["freed"][t.slot]
        state["freed"][t.slot] += 1
        t.freed = state["freed"][t.slot]
        state["done"] += 1
        t.val = state["done"]
        tiles[name] = t
        for c in t.chunks[:new]:
            chunks[c]["end"] = t.val
        return t

    def chunk(src, c0, ncol, kt=KT, k0=0, twice=False):
        chunks.append(dict(src=src, c0=c0, n=ncol, kt=kt, k0=k0, twice=twice, end=None))
        return len(chunks) - 1

    def feature(name, src, c0, m=P, kt=KT, both=False, twice=False, rhs="x"):
        c = chunk(src, c0, m, kt, twice=twice)
        tile(name, [c], 1, kind="F", m=m * (2 if twice else 1), kt=kt, both=both, rhs=rhs, off=0,
             width=m * (2 if twice else 1))

    def values(name, c0):
        c = [chunk("w_in", c0, P), chunk("w_in", c0 + P, P)]
        assert c[0] % 2 == 0
        tile(name + "A", c, 0, kind="V")
        tile(name + "M", c, 2, kind="VM")

    def pad():
        if len(chunks) % 2:
            chunks.append(None)

    feature("cq0", "w_in", C_CQ)
    feature("cq1", "w_in", C_CQ + P)
    feature("ckv", "w_in", C_CKV, both=True)
    feature("ik", "w_in", C_IK, 64, both=True, twice=True)
    c = chunk("w_in", C_IW, IDX_H)
    tile("iw", [c], 1, kind="W")
    c = chunk("w_idx_q", 0, 512, 2)
    for m in range(4):
        tile(f"iq{m}", [c], int(m == 3), kind="F", m=P, kt=2, both=False, rhs="cq", off=m * P, width=512)
    for n in range(4):
        c = chunk("w_dsa_uq", n * 512, 512, 2)
        for m in range(4):
            tile(f"uq{4 * n + m}", [c], int(m == 3), kind="F", m=P, kt=2, both=False, rhs="cq", off=m * P,
                 width=512)
    for m in range(8):
        feature(f"gb{m}", "w_in", C_GATE + D + m * P)
    for m in range(8):
        feature(f"yb{m}", "w_br_dsa", m * P, rhs="y")
    feature("ga", "w_in", C_GA, 16, both=True)
    for h in range(HEADS):
        feature(f"gq{h}", "w_in", C_GQ + h * DK)
        feature(f"gk{h}", "w_in", C_GK + h * DK, both=True)
        tile(f"gg{h}", [], 0, kind="G")
        pad()
        values(f"gv{h}", C_GV + h * DV)
        if h:
            for v in range(2):
                feature(f"gr{2 * (h - 1) + v}", "w_in", C_GR + (2 * (h - 1) + v) * P)
    for v in range(2):
        feature(f"gr{6 + v}", "w_in", C_GR + (6 + v) * P)
    for m in range(8):
        feature(f"ta{m}", "w_in", C_GATE + m * P)
        feature(f"ya{m}", "w_br_gla", m * P, rhs="y")
    feature("mi", "w_in", C_MI, HEADS, both=True)
    feature("mf", "w_in", C_MF, HEADS, both=True)
    for h in range(HEADS):
        feature(f"mq{h}", "w_in", C_MQ + h * DK, both=True)
        feature(f"mk{h}", "w_in", C_MK + h * DK, both=True)
        pad()
        values(f"mv{h}", C_MV + h * DV)
        if h:
            for v in range(2):
                feature(f"mo{2 * (h - 1) + v}", "w_in", C_MO + (2 * (h - 1) + v) * P)
    for v in range(2):
        feature(f"mo{6 + v}", "w_in", C_MO + (6 + v) * P)
    for m in range(8):
        feature(f"tc{m}", "w_in", C_GATE + 2 * D + m * P)
        feature(f"yc{m}", "w_br_ml", m * P, rhs="y")
    for hf in range(2):
        for n in range(4):
            c = chunk("w_out", hf * 512, 512, 2, 2 * n)
            tile(f"out{hf}_{n}", [c], 1, kind="O")
            state["slot"] ^= 1
            state["freed"][tiles[f"out{hf}_{n}"].slot] -= 1
    for m in range(FT):
        feature(f"up{m}", "w_up", m * P, rhs="n")
    for hf in range(2):
        for n in range(FT // 2):
            c = chunk("w_down", hf * 512, 512, 2, 2 * n)
            tile(f"down{hf}_{n}", [c], 1, kind="O")
            state["slot"] ^= 1
            state["freed"][tiles[f"down{hf}_{n}"].slot] -= 1
    real, held = [], [None] * NHL
    for n, c in enumerate(chunks):
        if c is None:
            continue
        c["r"] = len(real)
        c["raw"] = c["r"] % NRAW
        c["hl"] = n % NHL
        c["after"] = held[c["hl"]]
        held[c["hl"]] = c["end"]
        real.append(c)
    total = [0] * NRAW
    for c in real:
        total[c["raw"]] += 32 if c["twice"] else 16
        c["load"] = total[c["raw"]]
    return chunks, real, tiles



def build(nc, a, scratch, out):
    chunks, real, tl = plan()
    ctx = ExitStack()
    with ctx:
        def sb(name, shape, dt=FP32):
            return ctx.enter_context(nc.sbuf_tensor(name, shape, dt))

        def sem(name):
            return ctx.enter_context(nc.semaphore(name))

        def region(offset, specs):
            with ExitStack() as r:
                if offset:
                    r.enter_context(nc.sbuf_tensor(f"below_{specs[0][0]}", [P, offset // 4], FP32))
                return [r.enter_context(nc.sbuf_tensor(n, sh, dt)) for n, sh, dt in specs]

        wraw = sb("wraw", [P, NRAW, CH])
        whi = sb("whi", [P, NHL, CH], F32R)
        wlo = sb("wlo", [P, NHL, CH], F32R)
        ident = sb("ident", [P, P])
        identb = sb("identb", [P, P], BF16)
        ones = sb("ones", [P, P])
        later_neg = sb("later_neg", [P, P])
        later_big = sb("later_big", [P, P], BF16)
        later_bigT = sb("later_bigT", [P, P])
        col = sb("col", [P, NROW])
        eps = sb("eps", [P, 1])
        lm = sb("lm", [P, len(LEVELS), 64])

        XO = 0
        MIXO = XO + 2 * KT * ALL * 4
        YO = MIXO + KT * SEQ * 4
        LO = YO + DSA_H * ALL * 4
        PTO = LO + 4 * ALL * 4
        KVO = PTO + 2 * (QT + 1) * 2 * P * 4
        xh, xl, mix = region(XO, [("xh", [P, KT, ALL], F32R), ("xl", [P, KT, ALL], F32R), ("mix", [P, KT, SEQ], FP32)])
        rline, oh, t5 = region(MIXO, [("rline", [P, 2, LPITCH], FP32), ("oh", [BUCKETS, LINE], FP32),
                                      ("t5", [BUCKETS, DSA_H], FP32)])
        (table, L, PT, PTm, kvT, kvn, kvm, keep, low, psm, prec, qlat, S, top8, rl, kn, wi, bw) = region(YO, [
            ("table", [P, DSA_H, ALL], FP32), ("L", [P, 4, ALL], FP32), ("PT", [P, 2, QT, 2 * P], FP32),
            ("PTm", [META, 2, 2 * P], FP32), ("kvT", [P, ALL], FP32), ("kvn", [P, QT, P], FP32),
            ("kvm", [META, P], FP32), ("keep", [P, QT, ALL], BF16), ("low", [P, 64], FP32), ("psm", [P, 64], FP32),
            ("prec", [P, 64], FP32), ("qlat", [P, DSA_H, SEQ], FP32), ("S", [P, QT, ALL], FP32),
            ("top8", [P, 2, 8], FP32), ("rl", [P, 2, ALL], FP32), ("kn", [P, ALL], FP32), ("wi", [P, QT, IDX_H], FP32),
            ("bw", [P, IDX_H], FP32)])
        QO = KVO + (ALL + QT * P + P) * 4 + QT * ALL * 2 + 3 * 64 * 4
        SO = QO + DSA_H * SEQ * 4
        (uvp,) = region(SO, [("uvp", [P, DSA_H, P], FP32)])
        cq, sq = region(LO, [("cq", [P, 2, SEQ], FP32), ("sq", [P, 2, SEQ], FP32)])
        cqh, cql = region(PTO, [("cqh", [P, 2, SEQ], F32R), ("cql", [P, 2, SEQ], F32R)])
        (qi,) = region(QO, [("qi", [P, 4, SEQ], FP32)])
        rk, ckv, ki, sqk = region(SO, [("rk", [P, ALL], FP32), ("ckv", [P, ALL], FP32), ("ki", [P, ALL], FP32),
                                       ("sqk", [P, ALL], FP32)])
        rq, xc = region(SO + QT * ALL * 4 + 64, [("rq", [P, SEQ], FP32), ("xc", [P, ALL], FP32)])
        X, Xm, gbc, junk, brow, ss = region(QO, [
            ("X", [P, QT, D], FP32), ("Xm", [META, D], FP32), ("gbc", [P, D], FP32), ("junk", [P, D], FP32),
            ("brow", [NROW, P], FP32), ("ss", [P, QT + 1], FP32)])
        yh, yl = region(YO, [("yh", [P, KT, SEQ], F32R), ("yl", [P, KT, SEQ], F32R)])
        AO = YO + 2 * KT * SEQ * 4
        (sgate, gtmp, vb, qh, kh, vh, vm, AT, ATm, sqo, rso, on, sgr) = region(AO, [
            ("sgate", [P, 2, SEQ], FP32), ("gtmp", [P, 2, SEQ], FP32), ("vb", [P, D], FP32),
            ("qh", [P, 2, SEQ], FP32), ("kh", [P, 2, ALL], FP32), ("vh", [P, 2, QT, DV], FP32),
            ("vm", [META, 2, DV], FP32), ("AT", [P, QT, SEQ], FP32), ("ATm", [META, SEQ], FP32),
            ("sqo", [P, 2, SEQ], FP32), ("rso", [P, SEQ], FP32), ("on", [P, 2, SEQ], FP32), ("sgr", [P, SEQ], FP32)])
        BO = AO + (2 * SEQ * 2 + D + 2 * SEQ + 2 * ALL + 2 * QT * DV + 2 * DV + QT * SEQ + SEQ + 2 * SEQ + SEQ + 2 * SEQ + SEQ) * 4
        (aT, a2, G, E, QL, KL, QQ, KHt, gt, gf, gch) = region(BO, [
            ("aT", [META, ALL], FP32), ("a2", [META, HEADS * DK], FP32),
            ("G", [P, 2, ALL], FP32), ("E", [P, SEQ], FP32), ("QL", [P, 2, SEQ // 2], FP32), ("KL", [P, 2, SEQ], FP32),
            ("QQ", [P, SEQ], FP32), ("KHt", [P, ALL - P], FP32), ("gt", [P, QT + 1], FP32), ("gf", [P, QT + 1], FP32),
            ("gch", [P, ALL], FP32)])
        (zc, cv, sgc, u, lf, bcum, uT, uTm, M, fbias, Mb, Md, Wd, Wm, emn) = region(BO, [
            ("zc", [P, ALL + 3], FP32), ("cv", [P, ALL], FP32), ("sgc", [P, ALL], FP32), ("u", [HEADS, ALL], FP32),
            ("lf", [HEADS, ALL], FP32), ("bcum", [HEADS, ALL], FP32),
            ("uT", [P, QT, HEADS], FP32), ("uTm", [META, HEADS], FP32), ("M", [HEADS, ALL], FP32),
            ("fbias", [HEADS, 1], FP32), ("Mb", [P, SEQ], FP32), ("Md", [P, SEQ], FP32), ("Wd", [P, SEQ], FP32),
            ("Wm", [META, SEQ], FP32), ("emn", [P, SEQ], FP32)])
        (hres,) = region(0, [("hres", [P, QT, D], FP32)])
        nh, nl = region(QT * D * 4, [("nh", [P, KT, SEQ], F32R), ("nl", [P, KT, SEQ], F32R)])
        UO = QT * D * 4 + 2 * KT * SEQ * 4
        (U,) = region(UO, [("U", [P, FT, SEQ], FP32)])
        (gains, uh, ul, xn, jk, ssf) = region(UO + FT * SEQ * 4, [
            ("gains", [P, 3, D], FP32), ("uh", [P, 4, SEQ], F32R), ("ul", [P, 4, SEQ], F32R), ("xn", [P, QT, D], FP32),
            ("jk", [P, SEQ], FP32), ("ssf", [P, 3, QT, 2], FP32)])

        GP = [ctx.enter_context(nc.psum_tensor(f"GP{i}", [P, 1024], FP32)) for i in range(2)]
        PA = [ctx.enter_context(nc.psum_tensor(f"PA{i}", [P, 1024], FP32)) for i in range(2)]

        def bank(i):
            return PA[i // 2][:, (i % 2) * SEQ:(i % 2 + 1) * SEQ]

        def halves(ps, n=P):
            return ps[0:n, :].rearrange("p (a b) -> p a b", a=2)[:, :, 0:HALF]

        def two(t, n=P):
            return t[0:n, 0:ALL].rearrange("p (a b) -> p a b", a=2)

        def accumulators(name, hf, t):
            pair = GP if (name == "out") == (hf == 0) else PA
            return pair[t // 2][:, (t % 2) * SEQ:(t % 2 + 1) * SEQ]

        def cc(name, k=0, n=P):
            return col[0:n, ROWS[name] + k:ROWS[name] + k + 1]

        raw_in = [sem(f"raw_in{i}") for i in range(NRAW)]
        hi_done, split_done, gemm_done = sem("hi_done"), sem("split_done"), sem("gemm_done")
        gfree = [sem(f"gfree{i}") for i in range(2)]
        act_c, dve_c, pool_c = sem("act_chain"), sem("dve_chain"), sem("pool_chain")
        row_zero, ld_rows, ld_x, ld_line = sem("row_zero"), sem("ld_rows"), sem("ld_x"), sem("ld_line")
        masks = sem("masks")
        col_ps, col_ok, ss_zero, rs_ok, xn_ok = sem("col_ps"), sem("col_ok"), sem("ss_zero"), sem("rs_ok"), sem("xn_ok")
        xt_ps, xh_ok, xl_ok = sem("xt_ps"), sem("xh_ok"), sem("xl_ok")
        line_ps, line_ok, table_in = sem("line_ps"), sem("line_ok"), sem("table_in")
        line_out = [sem(f"line_out{i}") for i in range(2)]
        cqsq, kvsq, kisq, xcsq, ssq_ps = sem("cqsq"), sem("kvsq"), sem("kisq"), sem("xcsq"), sem("ssq_ps")
        rq_ok, rk_ok, xc_ok = sem("rq_ok"), sem("rk_ok"), sem("xc_ok")
        cqs_ok, kvT_ok, kn_ok, kvn_ps, kvn_ok = sem("cqs_ok"), sem("kvT_ok"), sem("kn_ok"), sem("kvn_ps"), sem("kvn_ok")
        sc_ps, sc_rl, sc_acc, keep_ok = sem("sc_ps"), sem("sc_rl"), sem("sc_acc"), sem("keep_ok")
        lg_ps, lg_mn, p_exp, p_nrm = sem("lg_ps"), sem("lg_mn"), sem("p_exp"), sem("p_nrm")
        pt_ps, pt_a, pt_d, pv_ps, ol_ev = sem("pt_ps"), sem("pt_a"), sem("pt_d"), sem("pv_ps"), sem("ol_ev")
        uv_zero, ld_uv, uv_ps, yh_b, yl_b = sem("uv_zero"), sem("ld_uv"), sem("uv_ps"), sem("yh_b"), sem("yl_b")
        ld_a, gla_c, aT_ok, gg_a, gg_l, G_ok = sem("ld_a"), sem("gla_consts"), sem("aT_ok"), sem("gg_a"), sem("gg_l"), sem("G_ok")
        lv_w, lv_e, lv_qk, lv_ps, lv_sel = sem("lv_w"), sem("lv_e"), sem("lv_qk"), sem("lv_ps"), sem("lv_sel")
        od_e, od_q, od_ps, od_ev = sem("od_e"), sem("od_q"), sem("od_ps"), sem("od_ev")
        av_ps, av_sq, av_ss, av_rs, on_ok = sem("av_ps"), sem("av_sq"), sem("av_ss"), sem("av_rs"), sem("on_ok")
        sg_ok, y_ok, gate_ok, mix_ok = sem("sg_ok"), sem("y_ok"), sem("gate_ok"), sem("mix_ok")
        ld_v, zpad, z_ok, cv_ok, cs_ok, qk_ok = sem("ld_v"), sem("zpad"), sem("z_ok"), sem("cv_ok"), sem("cs_ok"), sem("qk_ok")
        fa_ok, fl_ok, u_ok, M_ok, uT_ps, uT_ok = sem("fa_ok"), sem("fl_ok"), sem("u_ok"), sem("M_ok"), sem("uT_ps"), sem("uT_ok")
        mb_ps, mb_ok, md_ok, em_ok = sem("mb_ps"), sem("mb_ok"), sem("md_ok"), sem("em_ok")
        s_ps, w_ok, at_ok, num_ok = sem("s_ps"), sem("w_ok"), sem("at_ok"), sem("num_ok")
        ms_ok, ms_d = sem("ms_ok"), sem("ms_d")
        ld_h, ld_g, out_s, o_ss, h_ok, h_rs, n_ok = sem("ld_h"), sem("ld_g"), sem("out_s"), sem("o_ss"), sem("h_ok"), sem("h_rs"), sem("n_ok")
        nt_ps, nh_ok, nl_ok = sem("nt_ps"), sem("nh_ok"), sem("nl_ok")
        u_r, U_ok, uh_ok, ul_ok, fin_ss, fin, out_done = sem("u_r"), sem("U_ok"), sem("uh_ok"), sem("ul_ok"), sem("fin_ss"), sem("fin"), sem("out_done")

        block = ctx.enter_context(nc.Block())
        NHEADS2 = DSA_H // 2
        GROUPS = QT * NHEADS2

        def pt_d_after(g):
            return g + 1 + max(g + 1 - 2 * NHEADS2, 0)

        @block.sync
        def _(sp):
            sp.wait_ge(row_zero, 1)
            n = 0
            for name, count, src in ROW_LIST:
                r = ROWS[name]
                for dst, part in row_sources(a, name, count, src):
                    sp.dma_start(brow[r + dst[0]:r + dst[0] + part.shape[0], dst[1]:dst[1] + part.shape[1]],
                                 part).then_inc(ld_rows, 16)
                    n += 1
            assert n == NROWDMA, n
            for c in real:
                if c["r"] >= NRAW:
                    sp.wait_ge(split_done, c["r"] - NRAW + 1)
                src = a[c["src"]][0, c["k0"] * P:(c["k0"] + c["kt"]) * P, c["c0"]:c["c0"] + c["n"]]
                src = src.rearrange("(k p) n -> p k n", p=P)
                w = c["n"] * (2 if c["twice"] else 1)
                dst = wraw[:, c["raw"], 0:c["kt"] * w].rearrange("p (k n) -> p k n", n=w)
                for rep in range(w // c["n"]):
                    sp.dma_start(dst[:, :, rep * c["n"]:(rep + 1) * c["n"]], src).then_inc(raw_in[c["raw"]], 16)

        @block.gpsimd
        def _(pool):
            nc.gpsimd.memset(ident[:, :], 0.0).then_inc(pool_c, 1)
            nc.gpsimd.memset(later_neg[:, :], 0.0).then_inc(pool_c, 1)
            nc.gpsimd.memset(later_bigT[:, :], 0.0).then_inc(pool_c, 1)
            pool.wait_ge(pool_c, 3)
            nc.gpsimd.affine_select(out=ident[:, :], in_=ident[:, :], compare_op=ALU.not_equal, fill=1.0, base=0,
                                    pattern=[[-1, P]], channel_multiplier=1).then_inc(pool_c, 1)
            nc.gpsimd.affine_select(out=later_neg[:, :], in_=later_neg[:, :], compare_op=ALU.is_ge, fill=-BIG, base=0,
                                    pattern=[[-1, P]], channel_multiplier=1).then_inc(pool_c, 1)
            nc.gpsimd.affine_select(out=later_bigT[:, :], in_=later_bigT[:, :], compare_op=ALU.is_ge, fill=BIG, base=0,
                                    pattern=[[1, P]], channel_multiplier=-1).then_inc(pool_c, 1)
            pool.wait_ge(pool_c, 6)
            nc.gpsimd.tensor_copy(identb[:, :], ident[:, :]).then_inc(masks, 1)
            nc.gpsimd.tensor_scalar(later_big[:, :], later_neg[:, :], -1.0, 1.0, ALU.mult, ALU.mult).then_inc(masks, 1)
            nc.gpsimd.memset(lm[:, :, :], 1.0).then_inc(pool_c, 1)
            pool.wait_ge(pool_c, 7)
            for l, B in enumerate(LEVELS):
                v = lm[:, l, :].rearrange("p (n b) -> p n b", b=B)
                nc.gpsimd.affine_select(out=v, in_=v, compare_op=ALU.is_ge, fill=0.0, base=0,
                                        pattern=[[-2 * B, 64 // B], [0, B]], channel_multiplier=1).then_inc(pool_c, 1)
                pool.wait_ge(pool_c, 8 + l)
            for l, B in enumerate(LEVELS):
                v = lm[:, l, :].rearrange("p (n b) -> p n b", b=B)
                nc.gpsimd.affine_select(out=v, in_=v, compare_op=ALU.is_ge, fill=0.0, base=B - 1,
                                        pattern=[[2 * B, 64 // B], [0, B]], channel_multiplier=-1).then_inc(masks, 1)
            pool.wait_ge(masks, 2 + len(LEVELS))
            for c in real:
                n = c["kt"] * c["n"] * (2 if c["twice"] else 1)
                src, hi, lo = wraw[:, c["raw"], 0:n], whi[:, c["hl"], 0:n], wlo[:, c["hl"], 0:n]
                pool.wait_ge(raw_in[c["raw"]], c["load"])
                if c["after"]:
                    pool.wait_ge(gemm_done, c["after"])
                nc.gpsimd.tensor_scalar(hi, src, 1.0, 1.0, ALU.mult, ALU.mult).then_inc(hi_done, 1)
                pool.wait_ge(hi_done, c["r"] + 1)
                nc.gpsimd.tensor_tensor(lo, src, hi.bitcast(FP32), ALU.subtract).then_inc(split_done, 1)

        @block.scalar
        def _(act):
            n = [0]

            def seq(ins):
                n[0] += 1
                ins.then_inc(act_c, 1)
                act.wait_ge(act_c, n[0])

            def lnexp():
                nc.scalar.preload_act_table_set("natural_log_exp_and_others")

            def inv_root(t, src, width):
                seq(nc.scalar.activation(t, src, ACT.Ln, bias=eps[0:t.shape[0], :], scale=1.0 / width))
                return nc.scalar.activation(t, t, ACT.Exp, scale=-0.5)

            def ready(name):
                t = tl[name]
                act.wait_ge(gemm_done, t.val)
                return GP[t.slot]

            def whole(name):
                act.wait_ge(gfree[tl[name].slot], tl[name].freed)

            act.dma_start(X[:, :, :], a["x"][0].rearrange("(t p) d -> p t d", p=P)).then_inc(ld_x, 16)
            act.dma_start(Xm[:, :], a["meta_tokens"]).then_inc(ld_x, 16)
            act.dma_start(gbc[:, :], a["g_pre_mix"].broadcast_to([P, D])).then_inc(ld_x, 16)
            act.dma_start(oh[:, :], a["onehot"]).then_inc(ld_line, 16)
            act.dma_start(t5[:, :], a["t5_bias"]).then_inc(ld_line, 16)
            act.dma_start(bw[:, :], a["b_in"][0:1, C_IW:C_IW + IDX_H].broadcast_to([P, IDX_H])).then_inc(ld_line, 16)
            lnexp()
            act.wait_ge(ld_x, 48)
            act.wait_ge(ss_zero, 1)
            seq(nc.scalar.activation(junk[0:META, :], Xm[:, :], ACT.Square, accum_out=ss[0:META, QT:QT + 1]))
            for t in range(QT):
                seq(nc.scalar.activation(junk[:, :], X[:, t, :], ACT.Square, accum_out=ss[:, t:t + 1]))
            inv_root(ss[:, :], ss[:, :], D).then_inc(rs_ok, 1)
            for f in range(KT):
                act.wait_ge(xt_ps, f + 1)
                nc.scalar.activation(xh[:, f, META:ALL], bank(f % 4), ACT.Copy).then_inc(xh_ok, 1)
            act.wait_ge(xt_ps, KT + 1)
            nc.scalar.activation(xh[:, :, 0:META], GP[1][:, 0:KT * META].rearrange("p (k m) -> p k m", m=META),
                                 ACT.Copy).then_inc(xh_ok, 1)
            for h in range(DSA_H):
                act.wait_ge(line_ps, h + 1)
                if h >= 2:
                    act.wait_ge(line_out[h % 2], 16 * (h // 2))
                nc.scalar.activation(rline[:, h % 2, 0:LINE], GP[h % 2][:, 0:LINE], ACT.Copy, scale=-1.0).then_inc(line_ok, 1)
                act.wait_ge(line_ok, h + 1)
                act.dma_start(scratch[:, h, 0:LINE], rline[:, h % 2, 0:LINE]).then_inc(line_out[h % 2], 16)
            act.wait_ge(line_out[0], 8 * DSA_H)
            act.wait_ge(line_out[1], 8 * DSA_H)
            act.dma_start(table[:, :, :], bass.AP(tensor=scratch.tensor, offset=P - 1,
                                                  ap=[[DSA_H * LPITCH - 1, P], [LPITCH, DSA_H], [1, ALL]])).then_inc(table_in, 16)
            act.wait_ge(col_ok, 1)
            act.wait_ge(xl_ok, KT + 1)
            for k in range(2):
                nc.scalar.activation(cq[:, k, :], ready(f"cq{k}")[:, 0:SEQ], ACT.Identity, bias=cc("cq", k)).then_inc(gfree[tl[f"cq{k}"].slot], 1)
            whole("cq0")
            whole("cq1")
            nc.scalar.activation(sq[:, :, :], cq[:, :, :], ACT.Square).then_inc(cqsq, 1)
            nc.scalar.activation(two(ckv), halves(ready("ckv")), ACT.Identity, bias=cc("ckv")).then_inc(gfree[tl["ckv"].slot], 1)
            whole("ckv")
            nc.scalar.activation(sqk[:, :], ckv[:, :], ACT.Square).then_inc(kvsq, 1)
            nc.scalar.activation(two(ki), halves(ready("ik")), ACT.Identity, bias=cc("ik")).then_inc(gfree[tl["ik"].slot], 1)
            act.wait_ge(ssq_ps, 1)
            inv_root(rq[:, :], PA[0][:, 0:SEQ], 2 * P).then_inc(rq_ok, 1)
            act.wait_ge(ssq_ps, 2)
            inv_root(two(rk), halves(PA[1]), P).then_inc(rk_ok, 1)
            act.wait_ge(xc_ok, 1)
            act.wait_ge(rk_ok, 1)
            nc.scalar.activation(sqk[:, :], xc[:, :], ACT.Square).then_inc(xcsq, 1)
            act.wait_ge(kvT_ok, 1)
            act.wait_ge(ssq_ps, 4)
            inv_root(two(rk), halves(PA[1]), P).then_inc(rk_ok, 1)
            act.wait_ge(kvn_ps, 1)
            nc.scalar.activation(kvn[:, :, :], PA[0][:, 0:QT * P].rearrange("p (t c) -> p t c", t=QT), ACT.Copy).then_inc(kvn_ok, 1)
            nc.scalar.activation(kvm[:, :], PA[0][0:META, QT * P:(QT + 1) * P], ACT.Copy).then_inc(kvn_ok, 1)
            for m in range(4):
                nc.scalar.activation(qi[:, m, :], ready(f"iq{m}")[:, 0:SEQ], ACT.Copy, scale=0.125).then_inc(gfree[tl[f"iq{m}"].slot], 1)
            for v in range(QT * IDX_H):
                w = META + P * (v // IDX_H + 1)
                act.wait_ge(sc_ps, v + 1)
                if v >= 2:
                    act.wait_ge(sc_acc, v - 1)
                nc.scalar.activation(rl[:, v % 2, 0:w], PA[v % 2][:, 0:w], ACT.Relu).then_inc(sc_rl, 1)
            for h in range(DSA_H):
                nc.scalar.activation(qlat[:, h, :], ready(f"uq{h}")[:, 0:SEQ], ACT.Copy, scale=-float(P) ** -0.5).then_inc(gfree[tl[f"uq{h}"].slot], 1)
            act.wait_ge(table_in, 16)
            for m in range(KT):
                nc.scalar.activation(mix[:, m, :], ready(f"gb{m}")[:, 0:SEQ], ACT.Sigmoid, bias=cc("gate", 8 + m)).then_inc(gfree[tl[f"gb{m}"].slot], 1)
            lnexp()

            def exps(v):
                i = v // DSA_H
                w = META + P * (i + 1)
                act.wait_ge(lg_mn, v + 1)
                nc.scalar.activation(L[:, v % 4, 0:w], L[:, v % 4, 0:w], ACT.Exp, bias=low[:, v:v + 1], scale=-1.0,
                                     accum_out=psm[:, v:v + 1]).then_inc(p_exp, 1)

            exps(0)
            exps(1)
            for g in range(GROUPS):
                i, h = g // NHEADS2, 2 * (g % NHEADS2)
                if g + 1 < GROUPS:
                    exps(2 * g + 2)
                    exps(2 * g + 3)
                act.wait_ge(pt_ps, g + 1)
                if g >= 2:
                    act.wait_ge(pv_ps, g - 1)
                w = min(i + 1, 2)
                nc.scalar.activation(PT[:, g % 2, 0:w, :], GP[0][:, 0:w * 2 * P].rearrange("p (j n) -> p j n", j=w),
                                     ACT.Copy).then_inc(pt_a, 1)
                act.wait_ge(pv_ps, g + 1)
                nc.scalar.activation(qlat[:, h:h + 2, i * P:(i + 1) * P],
                                     GP[1][:, SEQ + (g % 2) * 2 * P:SEQ + (g % 2 + 1) * 2 * P].rearrange("p (h n) -> p h n", h=2),
                                     ACT.Copy).then_inc(ol_ev, 1)
                if g == 0:
                    act.wait_ge(uv_zero, 1)
                    act.dma_start(uvp[:, 0::2, 0:64], a["w_dsa_uv"][0, 0::2].rearrange("h c d -> c h d")).then_inc(ld_uv, 16)
                    act.dma_start(uvp[:, 1::2, 64:P], a["w_dsa_uv"][0, 1::2].rearrange("h c d -> c h d")).then_inc(ld_uv, 16)
            for m in range(KT):
                act.wait_ge(uv_ps, m + 1)
                nc.scalar.activation(yh[:, m, :], PA[m % 2][:, 0:SEQ], ACT.Copy).then_inc(yh_b, 1)
            act.wait_ge(yl_b, KT)
            act.dma_start(a2[:, :], a["w_gla_a2"][0]).then_inc(ld_a, 16)
            act.dma_start(vb[:, :], a["b_in"][0:1, C_GV:C_GV + D].broadcast_to([P, D])).then_inc(ld_a, 16)
            nc.scalar.activation(two(aT, META), halves(ready("ga"), META), ACT.Identity, bias=cc("ga", 0, META)).then_inc(gfree[tl["ga"].slot], 1)

            def gate_of(h):
                ps = ready(f"gg{h}")
                if h:
                    act.wait_ge(gg_l, h)
                    act.wait_ge(G_ok, h)
                nc.scalar.activation(two(gch), halves(ps), ACT.Abs, bias=cc("a2", h)).then_inc(gg_a, 1)
                act.wait_ge(gg_a, h + 1)
                seq(nc.scalar.activation(gch[:, :], gch[:, :], ACT.Exp, scale=-1.0))
                nc.scalar.activation(gch[:, :], gch[:, :], ACT.Ln, bias=1.0).then_inc(gg_l, 1)

            def level(h, l):
                k = len(LEVELS) * h + l
                act.wait_ge(lv_w, k + 1)
                nc.scalar.activation(E[:, :], E[:, :], ACT.Exp, scale=1.0 / 16.0).then_inc(lv_e, 1)

            def off(h):
                g0 = G[:, h % 2, :]
                if h:
                    act.wait_ge(od_q, 4 * h)
                    act.wait_ge(od_ps, 4 * h)
                nc.scalar.activation(QQ[:, :], g0[:, META:ALL], ACT.Exp, scale=1.0 / 16.0).then_inc(od_e, 1)
                nc.scalar.activation(gf[:, :], g0[:, META - 1::P], ACT.Exp, scale=1.0 / 16.0).then_inc(od_e, 1)
                seq(nc.scalar.activation(gt[:, :], g0[:, META - 1::P], ACT.Copy, scale=1.0 / 16.0))
                nc.scalar.activation(KHt[:, 0:META], g0[:, 0:META], ACT.Exp, bias=gt[:, 0:1], scale=-1.0 / 16.0).then_inc(od_e, 1)
                for j in range(3):
                    nc.scalar.activation(KHt[:, META + j * P:META + (j + 1) * P], g0[:, META + j * P:META + (j + 1) * P],
                                         ACT.Exp, bias=gt[:, j + 1:j + 2], scale=-1.0 / 16.0).then_inc(od_e, 1)
                if h:
                    act.wait_ge(av_ps, h)
                for q, j in enumerate([2, 1, 0]):
                    act.wait_ge(od_ps, 4 * h + q + 1)
                    w = SEQ - P * (j + 1)
                    nc.scalar.activation(AT[:, j, P:P + w], bank(q)[:, 0:w], ACT.Copy).then_inc(od_ev, 1)
                act.wait_ge(od_ps, 4 * h + 4)
                nc.scalar.activation(ATm[:, :], bank(3)[0:META, :], ACT.Copy).then_inc(od_ev, 1)

            def head_norm(k, src):
                nc.scalar.activation(sqo[:, :, :], src, ACT.Square).then_inc(av_sq, 1)
                act.wait_ge(av_ss, k + 1)
                inv_root(rso[:, :], bank(2), DV).then_inc(av_rs, 1)

            order = [("evac", 0)]
            for h in range(HEADS):
                order += [("mixed", h), ("off", h), ("pv", h), ("r", h)]
            for what, h in order:
                if what == "evac":
                    gate_of(0)
                elif what == "mixed":
                    for l in range(4):
                        level(h, l)
                    if h + 1 < HEADS:
                        gate_of(h + 1)
                    for l in range(4, 7):
                        level(h, l)
                elif what == "off":
                    off(h)
                elif what == "pv":
                    act.wait_ge(av_ps, h + 1)
                    head_norm(h, PA[0][:, :].rearrange("p (a b) -> p a b", a=2))
                else:
                    for v in range(2):
                        m = 2 * h + v
                        ps = ready(f"gr{m}")
                        if m:
                            act.wait_ge(y_ok, m)
                        nc.scalar.activation(sgr[:, :], ps[:, 0:SEQ], ACT.Sigmoid, bias=cc("gr", m)).then_inc(sg_ok, 1)
                        act.wait_ge(y_ok, m + 1)
                        nc.scalar.activation(yh[:, m, :], on[:, v, :], ACT.Copy).then_inc(ms_ok, 1)
                    lnexp()

            def gates(branch, name, at):
                for m in range(KT):
                    k = 8 * branch + m
                    ps = ready(f"{name}{m}")
                    if k >= 2:
                        act.wait_ge(mix_ok, k - 1)
                    nc.scalar.activation(sgate[:, m % 2, :], ps[:, 0:SEQ], ACT.Sigmoid, bias=cc("gate", at + m)).then_inc(gfree[tl[f"{name}{m}"].slot], 1)

            gates(0, "ta", 0)
            lnexp()
            act.wait_ge(mix_ok, KT)
            act.dma_start(vb[:, :], a["b_in"][0:1, C_MV:C_MV + D].broadcast_to([P, D])).then_inc(ld_v, 16)
            act.wait_ge(ms_d, 1)
            nc.scalar.activation(two(lf, HEADS), halves(ready("mf"), HEADS), ACT.Abs, bias=fbias[:, :]).then_inc(fa_ok, 1)
            act.wait_ge(fa_ok, 1)
            seq(nc.scalar.activation(lf[:, :], lf[:, :], ACT.Exp, scale=-1.0))
            nc.scalar.activation(lf[:, :], lf[:, :], ACT.Ln, bias=1.0).then_inc(fl_ok, 1)

            def conv_in(h, q):
                k = 2 * h + q
                ps = ready(f"m{'qk'[q]}{h}")
                act.wait_ge(zpad, 1)
                if k:
                    act.wait_ge(cv_ok, k)
                nc.scalar.activation(zc[:, 3:3 + ALL].rearrange("p (a b) -> p a b", a=2), halves(ps), ACT.Identity,
                                     bias=cc(f"m{'qk'[q]}", h)).then_inc(gfree[tl[f"m{'qk'[q]}{h}"].slot], 1)
                act.wait_ge(cv_ok, k + 1)
                if k:
                    act.wait_ge(qk_ok, k)
                nc.scalar.activation(sgc[:, :], cv[:, :], ACT.Sigmoid).then_inc(cs_ok, 1)

            def mlstm(h):
                lnexp()
                if h:
                    act.wait_ge(md_ok, h)
                    act.wait_ge(at_ok, 5 * h)
                act.wait_ge(mb_ps, 2 * h + 1)
                nc.scalar.activation(Mb[:, :], bank(0), ACT.Copy).then_inc(mb_ok, 1)
                act.wait_ge(mb_ps, 2 * h + 2)
                if h:
                    act.wait_ge(num_ok, 2 * h)
                nc.scalar.activation(emn[:, :], bank(1), ACT.Exp).then_inc(em_ok, 1)
                act.wait_ge(mb_ok, h + 1)
                act.wait_ge(uT_ok, 2)
                act.wait_ge(md_ok, h + 1)
                nc.scalar.activation(Wm[:, :], Mb[0:META, :], ACT.Exp, bias=uTm[:, h:h + 1], scale=-1.0).then_inc(w_ok, 1)
                for j in range(QT):
                    if j:
                        act.wait_ge(at_ok, 5 * h + j + 1)
                    nc.scalar.activation(Wd[:, 0:P], Md[:, j * P:(j + 1) * P], ACT.Exp, bias=uT[:, j, h:h + 1], scale=-1.0).then_inc(w_ok, 1)
                    if j < QT - 1:
                        nc.scalar.activation(Wd[:, P:SEQ - j * P], Mb[:, (j + 1) * P:SEQ], ACT.Exp, bias=uT[:, j, h:h + 1],
                                             scale=-1.0).then_inc(w_ok, 1)
                act.wait_ge(num_ok, 2 * h + 2)
                head_norm(HEADS + h, on[:, :, :])

            def m_out(h):
                for v in range(2):
                    m = 2 * h + v
                    ps = ready(f"mo{m}")
                    act.wait_ge(y_ok, 8 + m)
                    nc.scalar.activation(sgr[:, :], ps[:, 0:SEQ], ACT.Sigmoid, bias=cc("mo", m)).then_inc(gfree[tl[f"mo{m}"].slot], 1)
                    act.wait_ge(y_ok, 8 + m + 1)
                    nc.scalar.activation(yh[:, m, :], on[:, v, :], ACT.Copy).then_inc(ms_ok, 1)

            conv_in(0, 0)
            conv_in(0, 1)
            for h in range(HEADS):
                if h + 1 < HEADS:
                    conv_in(h + 1, 0)
                    conv_in(h + 1, 1)
                mlstm(h)
                m_out(h)
            gates(1, "tc", 16)
            lnexp()
            act.wait_ge(gemm_done, tl["tc7"].val)
            act.dma_start(hres[:, :, :], a["x"][0].rearrange("(t p) d -> p t d", p=P)).then_inc(ld_h, 16)
            act.wait_ge(gemm_done, tl["yc7"].val)
            for m in range(KT):
                act.wait_ge(mix_ok, KT + m + 1)
                nc.scalar.activation(yh[:, m, :], mix[:, m, :], ACT.Copy).then_inc(ms_ok, 1)
            act.wait_ge(ms_ok, 3 * KT)
            for n_, g_ in enumerate(["g_post_mix", "g_pre_mlp", "g_post_mlp"]):
                act.dma_start(gains[:, n_, :], a[g_].broadcast_to([P, D])).then_inc(ld_g, 16)

            def out_sums(k, base, name, stop):
                for hf in range(2):
                    act.wait_ge(gemm_done, tl[f"{name}{hf}_{stop}"].val)
                    for t in range(QT):
                        seq(nc.scalar.activation(jk[:, :], acc(name, hf, t), ACT.Square, accum_out=ssf[:, k, t, hf:hf + 1]))

            acc = accumulators
            out_sums(0, 0, "out", 3)
            nc.scalar.activation(jk[:, 0:1], eps[:, :], ACT.Copy).then_inc(out_s, 1)
            act.wait_ge(h_rs, 1)
            inv_root(ssf[:, 0, :, 0], ssf[:, 0, :, 0], D).then_inc(o_ss, 1)
            for t in range(QT):
                act.wait_ge(h_ok, t + 1)
                for hf in range(2):
                    seq(nc.scalar.activation(jk[:, :], hres[:, t, hf * SEQ:(hf + 1) * SEQ], ACT.Square, accum_out=ssf[:, 1, t, hf:hf + 1]))
            nc.scalar.activation(jk[:, 0:1], eps[:, :], ACT.Copy).then_inc(o_ss, 1)
            act.wait_ge(h_rs, 2)
            inv_root(ssf[:, 1, :, 0], ssf[:, 1, :, 0], D).then_inc(o_ss, 1)
            for f in range(KT):
                act.wait_ge(nt_ps, f + 1)
                nc.scalar.activation(nh[:, f, :], bank(f % 4), ACT.Copy).then_inc(nh_ok, 1)
            for m in range(FT):
                ps = ready(f"up{m}")
                nc.scalar.activation(U[:, m, :], ps[:, 0:SEQ], ACT.Relu).then_inc(gfree[tl[f"up{m}"].slot], 1)
            for k in range(2 * FT):
                act.wait_ge(U_ok, k % FT + 1)
                if k >= 4:
                    act.wait_ge(gemm_done, tl[f"down{(k - 4) // FT}_{(k - 4) % FT // 2}"].val)
                nc.scalar.activation(uh[:, k % 4, :], U[:, k % FT, :], ACT.Copy).then_inc(uh_ok, 1)
                if k == 2 * FT - 1:
                    break
                if k == FT + 3:
                    for t in range(QT):
                        seq(nc.scalar.activation(jk[:, :], acc("down", 0, t), ACT.Square, accum_out=ssf[:, 2, t, 0:1]))
            act.wait_ge(gemm_done, tl[f"down1_{FT // 2 - 1}"].val)
            for t in range(QT):
                seq(nc.scalar.activation(jk[:, :], acc("down", 1, t), ACT.Square, accum_out=ssf[:, 2, t, 1:2]))
            nc.scalar.activation(jk[:, 0:1], eps[:, :], ACT.Copy).then_inc(o_ss, 1)
            act.wait_ge(h_rs, 3)
            inv_root(ssf[:, 2, :, 0], ssf[:, 2, :, 0], D).then_inc(o_ss, 1)
            for t in range(QT):
                act.wait_ge(fin, t + 1)
                act.dma_start(out[0, t * P:(t + 1) * P, :], hres[:, t, :]).then_inc(out_done, 16)
            act.wait_ge(out_done, 16 * QT)

        @block.vector
        def _(dve):
            n = [0]

            def seq(ins):
                n[0] += 1
                ins.then_inc(dve_c, 1)
                dve.wait_ge(dve_c, n[0])

            def ready(name):
                t = tl[name]
                dve.wait_ge(gemm_done, t.val)
                return GP[t.slot]

            def whole(name):
                dve.wait_ge(gfree[tl[name].slot], tl[name].freed)

            tt, ts, stt = nc.vector.tensor_tensor, nc.vector.tensor_scalar, nc.vector.scalar_tensor_tensor
            nc.vector.memset(brow[:, :], 0.0).then_inc(row_zero, 1)
            nc.vector.memset(ones[:, :], 1.0)
            nc.vector.memset(eps[:, :], EPS)
            nc.vector.memset(ss[:, :], 1.0).then_inc(ss_zero, 1)
            dve.wait_ge(rs_ok, 1)
            dve.wait_ge(ld_x, 48)
            stt(Xm[:, :], Xm[:, :], ss[0:META, QT:QT + 1], gbc[0:META, :], ALU.mult, ALU.mult).then_inc(xn_ok, 1)
            for t in range(QT):
                stt(X[:, t, :], X[:, t, :], ss[:, t:t + 1], gbc[:, :], ALU.mult, ALU.mult).then_inc(xn_ok, 1)
            dve.wait_ge(col_ps, 1)
            nc.vector.tensor_copy(col[:, :], GP[0][:, 0:NROW]).then_inc(col_ok, 1)
            for f in range(KT):
                dve.wait_ge(xh_ok, f + 1)
                tt(xl[:, f, META:ALL], bank(f % 4), xh[:, f, META:ALL].bitcast(FP32), ALU.subtract).then_inc(xl_ok, 1)
            dve.wait_ge(xh_ok, KT + 1)
            tt(xl[:, :, 0:META], GP[1][:, 0:KT * META].rearrange("p (k m) -> p k m", m=META),
               xh[:, :, 0:META].bitcast(FP32), ALU.subtract).then_inc(xl_ok, 1)
            dve.wait_ge(col_ok, 1)
            dve.wait_ge(rq_ok, 1)
            for k in range(2):
                seq(stt(cq[:, k, :], cq[:, k, :], cc("dq", k), rq[:, :], ALU.mult, ALU.mult))
            seq(nc.vector.tensor_copy(cqh[:, :, :], cq[:, :, :]))
            tt(cql[:, :, :], cq[:, :, :], cqh[:, :, :].bitcast(FP32), ALU.subtract).then_inc(cqs_ok, 1)
            dve.wait_ge(ssq_ps, 3)
            whole("ik")
            stt(two(xc), halves(PA[0]), -1.0 / P, two(ki), ALU.mult, ALU.add).then_inc(xc_ok, 1)
            dve.wait_ge(rk_ok, 1)
            stt(kvT[:, :], ckv[:, :], cc("dkv"), rk[:, :], ALU.mult, ALU.mult).then_inc(kvT_ok, 1)
            dve.wait_ge(rk_ok, 2)
            dve.wait_ge(xc_ok, 1)
            seq(stt(kn[:, :], xc[:, :], cc("ig"), rk[:, :], ALU.mult, ALU.mult))
            ts(kn[:, :], kn[:, :], cc("ib"), None, ALU.add).then_inc(kn_ok, 1)
            dve.wait_ge(ld_line, 48)
            seq(tt(wi[:, :, :], ready("iw")[:, 0:QT * IDX_H].rearrange("p (t h) -> p t h", h=IDX_H),
                   bw[:, :].unsqueeze(1).broadcast_to([P, QT, IDX_H]), ALU.add))
            ts(wi[:, :, :], wi[:, :, :], IDX_H ** -0.5, None, ALU.mult).then_inc(gfree[tl["iw"].slot], 1)
            whole("iw")
            dve.wait_ge(masks, 2)
            for v in range(QT * IDX_H):
                i, h = v // IDX_H, v % IDX_H
                w = META + P * (i + 1)
                dve.wait_ge(sc_rl, v + 1)
                if h == 0:
                    ts(S[:, i, 0:w], rl[:, v % 2, 0:w], wi[:, i, h:h + 1], None, ALU.mult).then_inc(sc_acc, 1)
                else:
                    dve.wait_ge(sc_acc, v)
                    stt(S[:, i, 0:w], rl[:, v % 2, 0:w], wi[:, i, h:h + 1], S[:, i, 0:w], ALU.mult, ALU.add).then_inc(sc_acc, 1)
            dve.wait_ge(sc_acc, QT * IDX_H)
            for i in range(QT):
                w = META + P * (i + 1)
                seq(tt(S[:, i, w - P:w], S[:, i, w - P:w], later_neg[:, :], ALU.add))
                for r in range(TOPK // 8):
                    seq(nc.vector.max(top8[:, 0, :], S[:, i, 0:w]))
                    seq(nc.vector.match_replace(S[:, i, 0:w], top8[:, 0, :], S[:, i, 0:w], MARK))
                seq(ts(keep[:, i, 0:w], S[:, i, 0:w], MARK / 2, BIG, ALU.is_gt, ALU.mult))
                tt(keep[:, i, w - P:w], keep[:, i, w - P:w], later_big[:, :], ALU.max).then_inc(keep_ok, 1)
            dve.wait_ge(keep_ok, QT)
            nc.vector.memset(uvp[:, :, :], 0.0).then_inc(uv_zero, 1)
            dve.wait_ge(table_in, 16)

            def logits(v):
                i, h = v // DSA_H, v % DSA_H
                w = META + P * (i + 1)
                dve.wait_ge(lg_ps, v + 1)
                if v >= 4:
                    dve.wait_ge(pt_ps, v // 2 - 1)
                nc.vector.tensor_tensor_reduce(out=L[:, v % 4, 0:w], in0=PA[v % 2][:, 0:w],
                                               in1=table[:, h, (QT - 1 - i) * P:(QT - 1 - i) * P + w], scale=1.0,
                                               scalar=3e38, op0=ALU.add, op1=ALU.min, accum_out=low[:, v:v + 1]).then_inc(lg_mn, 1)

            logits(0)
            logits(1)
            for g in range(GROUPS):
                i = g // NHEADS2
                w = META + P * (i + 1)
                if g + 1 < GROUPS:
                    logits(2 * g + 2)
                    logits(2 * g + 3)
                for v in (2 * g, 2 * g + 1):
                    dve.wait_ge(p_exp, v + 1)
                    seq(nc.vector.reciprocal(prec[:, v:v + 1], psm[:, v:v + 1]))
                    ts(L[:, v % 4, 0:w], L[:, v % 4, 0:w], prec[:, v:v + 1], None, ALU.mult).then_inc(p_nrm, 1)
                dve.wait_ge(pt_ps, g + 1)
                if g >= 2:
                    dve.wait_ge(pv_ps, g - 1)
                if i >= 2:
                    nc.vector.tensor_copy(PT[:, g % 2, 2:i + 1, :],
                                          GP[0][:, SEQ:SEQ + (i - 1) * 2 * P].rearrange("p (j n) -> p j n", j=i - 1)).then_inc(pt_d, 1)
                nc.vector.tensor_copy(PTm[:, g % 2, :], GP[1][0:META, (g % 2) * 2 * P:(g % 2 + 1) * 2 * P]).then_inc(pt_d, 1)
            for m in range(KT):
                dve.wait_ge(yh_b, m + 1)
                tt(yl[:, m, :], PA[m % 2][:, 0:SEQ], yh[:, m, :].bitcast(FP32), ALU.subtract).then_inc(yl_b, 1)
            for m in range(KT):
                whole(f"gb{m}")
                tt(mix[:, m, :], mix[:, m, :], ready(f"yb{m}")[:, 0:SEQ], ALU.mult).then_inc(gfree[tl[f"yb{m}"].slot], 1)
            nc.vector.memset(AT[:, :, :], 0.0)
            nc.vector.memset(KL[:, :, :], 0.0)
            nc.vector.memset(KHt[:, :], 0.0).then_inc(gla_c, 1)
            dve.wait_ge(gla_c, 1)
            dve.wait_ge(ld_a, 32)

            def values(name, h):
                ps = ready(f"{name}{h}A")
                nc.vector.tensor_tensor(vh[:, h % 2, :, :], ps[:, :].rearrange("p (t n) -> p t n", t=QT),
                                        vb[:, h * DV:(h + 1) * DV].unsqueeze(1).broadcast_to([P, QT, DV]),
                                        ALU.add).then_inc(gfree[tl[f"{name}{h}A"].slot], 1)
                ps = ready(f"{name}{h}M")
                tt(vm[:, h % 2, :], ps[0:META, 0:DV], vb[0:META, h * DV:(h + 1) * DV], ALU.add).then_inc(gfree[tl[f"{name}{h}M"].slot], 1)

            def qk(h):
                ts(qh[:, h % 2, :], ready(f"gq{h}")[:, 0:SEQ], cc("gq", h), DK ** -0.5, ALU.add, ALU.mult).then_inc(gfree[tl[f"gq{h}"].slot], 1)
                ts(two(kh[:, h % 2, :]), halves(ready(f"gk{h}")), cc("gk", h), None, ALU.add).then_inc(gfree[tl[f"gk{h}"].slot], 1)

            def forget(h):
                ps = ready(f"gg{h}")
                g0 = G[:, h % 2, :]
                dve.wait_ge(gg_l, h + 1)
                ts(two(g0), halves(ps), cc("a2", h), 0.0, ALU.add, ALU.min).then_inc(gfree[tl[f"gg{h}"].slot], 1)
                whole(f"gg{h}")
                seq(tt(gch[:, :], g0, gch[:, :], ALU.subtract))
                nc.vector.tensor_tensor_scan(g0[:, 0:META], ones[:, 0:META], gch[:, 0:META], 0.0, ALU.mult, ALU.add)
                for i in range(QT):
                    s0 = slice(META + i * P, META + (i + 1) * P)
                    ins = nc.vector.tensor_tensor_scan(g0[:, s0], ones[:, :], gch[:, s0], 0.0, ALU.mult, ALU.add)
                ins.then_inc(G_ok, 1)

            def parts(t, B):
                v = t.rearrange("p (n two b) -> p n two b", two=2, b=B)
                return v[:, :, 0, :], v[:, :, 1, :]

            def lv_write(h, l):
                B = LEVELS[l]
                lo_, up = parts(G[:, h % 2, META:ALL], B)
                N = SEQ // (2 * B)
                mid = lo_[:, :, B - 1:B].broadcast_to([P, N, B])
                k = len(LEVELS) * h + l
                if k:
                    dve.wait_ge(lv_qk, k)
                dve.wait_ge(G_ok, h + 1)
                tt(E[:, 0:SEQ // 2].rearrange("p (n b) -> p n b", b=B), up, mid, ALU.subtract)
                tt(E[:, SEQ // 2:SEQ].rearrange("p (n b) -> p n b", b=B), mid, lo_, ALU.subtract).then_inc(lv_w, 1)

            def lv_mul(h, l):
                B = LEVELS[l]
                k = len(LEVELS) * h + l
                dve.wait_ge(lv_e, k + 1)
                if k >= 2:
                    dve.wait_ge(lv_ps, 8 * ((k - 2) // 7) + (k - 2) % 7 + 1)
                _, uq = parts(qh[:, h % 2, :], B)
                lk, _ = parts(kh[:, h % 2, META:ALL], B)
                lo_, _ = parts(KL[:, k % 2, :], B)
                tt(QL[:, k % 2, :].rearrange("p (n b) -> p n b", b=B), uq, E[:, 0:SEQ // 2].rearrange("p (n b) -> p n b", b=B), ALU.mult)
                if k:
                    dve.wait_ge(lv_qk, k)
                tt(lo_, lk, E[:, SEQ // 2:SEQ].rearrange("p (n b) -> p n b", b=B), ALU.mult).then_inc(lv_qk, 1)

            def lv_select(h, l):
                k = 8 * h + l
                dve.wait_ge(lv_ps, k + 1)
                if k == 8 * h and h:
                    dve.wait_ge(av_ps, h)
                if k:
                    dve.wait_ge(lv_sel, k)
                if l < len(LEVELS):
                    B = LEVELS[l]
                    o_ = AT[:, :, 0:P].rearrange("p t (n two b) -> p t n two b", two=2, b=B)[:, :, :, 1, :]
                    m_ = lm[:, l, :].rearrange("p (n b) -> p n b", b=B).unsqueeze(1).broadcast_to([P, QT, 64 // B, B])
                    d_ = bank(k % 4)[:, 0:QT * 64].rearrange("p (t n b) -> p t n b", t=QT, b=B)
                    nc.vector.copy_predicated(o_, m_.bitcast(U32), d_).then_inc(lv_sel, 1)
                else:
                    m_ = ident[:, :].unsqueeze(1).broadcast_to([P, QT, P])
                    nc.vector.copy_predicated(AT[:, :, 0:P], m_.bitcast(U32),
                                              bank(k % 4).rearrange("p (t n) -> p t n", t=QT)).then_inc(lv_sel, 1)

            def off(h):
                dve.wait_ge(od_e, 6 * h + 6)
                seq(tt(KHt[:, :], KHt[:, :], kh[:, h % 2, 0:ALL - P], ALU.mult))
                tt(QQ[:, :], QQ[:, :], qh[:, h % 2, :], ALU.mult).then_inc(od_q, 1)
                for q, j in enumerate([2, 1, 0]):
                    dve.wait_ge(od_ps, 4 * h + q + 1)
                    dve.wait_ge(od_q, 4 * h + q + 1)
                    ts(QQ[:, (j + 1) * P:SEQ], QQ[:, (j + 1) * P:SEQ], gf[:, j + 1:j + 2], None, ALU.mult).then_inc(od_q, 1)

            def scaled(k, gname, src):
                dve.wait_ge(av_rs, k + 1)
                for v in range(2):
                    stt(on[:, v, :], src(v), cc(gname, v), rso[:, :], ALU.mult, ALU.mult).then_inc(on_ok, 1)

            def steps(h):
                lv_write(h, 0)
                for l in range(7):
                    lv_mul(h, l)
                    if l < 6:
                        lv_write(h, l + 1)
                    if l == 3 and h + 1 < HEADS:
                        qk(h + 1)
                        forget(h + 1)
                    if l:
                        lv_select(h, l - 1)
                lv_select(h, 6)
                lv_select(h, 7)
                if h + 1 < HEADS:
                    values("gv", h + 1)

            qk(0)
            forget(0)
            values("gv", 0)
            for h in range(HEADS):
                steps(h)
                off(h)
                if h:
                    dve.wait_ge(ms_ok, 2 * h)
                scaled(h, "hg", lambda v: bank(v))
                for v in range(2):
                    m = 2 * h + v
                    dve.wait_ge(sg_ok, m + 1)
                    stt(sgr[:, :], ready(f"gr{m}")[:, 0:SEQ], cc("gr", m), sgr[:, :], ALU.add, ALU.mult).then_inc(gfree[tl[f"gr{m}"].slot], 1)
                    whole(f"gr{m}")
                    dve.wait_ge(on_ok, 2 * h + 2)
                    tt(on[:, v, :], on[:, v, :], sgr[:, :], ALU.mult).then_inc(y_ok, 1)
                    dve.wait_ge(ms_ok, m + 1)
                    tt(yl[:, m, :], on[:, v, :], yh[:, m, :].bitcast(FP32), ALU.subtract).then_inc(yl_b, 1)

            def mixing(branch, gate, name):
                for m in range(KT):
                    k = 8 * branch + m
                    dve.wait_ge(gfree[tl[f"{gate}{m}"].slot], tl[f"{gate}{m}"].freed)
                    if k >= 2:
                        dve.wait_ge(mix_ok, k - 1)
                    tt(gtmp[:, m % 2, :], ready(f"{name}{m}")[:, 0:SEQ], sgate[:, m % 2, :], ALU.mult).then_inc(gfree[tl[f"{name}{m}"].slot], 1)
                    whole(f"{name}{m}")
                    tt(mix[:, m, :], mix[:, m, :], gtmp[:, m % 2, :], ALU.add).then_inc(mix_ok, 1)

            mixing(0, "ta", "ya")
            nc.vector.memset(zc[:, 0:3], 0.0).then_inc(zpad, 1)
            dve.wait_ge(mix_ok, KT)
            tt(fbias[:, :], cc("mf", 0, HEADS), cc("fb", 0, HEADS), ALU.add).then_inc(ms_d, 1)
            dve.wait_ge(ms_d, 1)
            ts(two(u, HEADS), halves(ready("mi"), HEADS), cc("mi", 0, HEADS), None, ALU.add).then_inc(gfree[tl["mi"].slot], 1)
            dve.wait_ge(fl_ok, 1)
            ts(two(bcum, HEADS), halves(ready("mf"), HEADS), fbias[:, :], 0.0, ALU.add, ALU.min).then_inc(gfree[tl["mf"].slot], 1)
            whole("mf")
            whole("mi")
            seq(tt(lf[:, :], bcum[:, :], lf[:, :], ALU.subtract))
            seq(nc.vector.memset(M[:, :], 1.0))
            seq(nc.vector.tensor_tensor_scan(bcum[:, :], M[:, :], lf[:, :], 0.0, ALU.mult, ALU.add))
            tt(u[:, :], u[:, :], bcum[:, :], ALU.subtract).then_inc(u_ok, 1)
            dve.wait_ge(u_ok, 1)
            seq(nc.vector.tensor_tensor_scan(M[:, :], u[:, :], u[:, :], 0.0, ALU.max, ALU.max))
            stt(bcum[:, :], bcum[:, :], -1.0, M[:, :], ALU.mult, ALU.subtract).then_inc(M_ok, 1)
            dve.wait_ge(uT_ps, 1)
            nc.vector.tensor_copy(uT[:, :, :], bank(0)[:, 0:QT * HEADS].rearrange("p (t h) -> p t h", h=HEADS)).then_inc(uT_ok, 1)
            nc.vector.tensor_copy(uTm[:, :], bank(0)[0:META, QT * HEADS:(QT + 1) * HEADS]).then_inc(uT_ok, 1)
            dve.wait_ge(ld_v, 16)

            def conv(h, q):
                k = 2 * h + q
                dve.wait_ge(zpad, 1)
                whole(f"m{'qk'[q]}{h}")
                if k:
                    dve.wait_ge(qk_ok, k)
                w = lambda tap: cc("cv", tap * 8 + q * 4 + h)
                seq(ts(cv[:, :], zc[:, 0:ALL], w(0), None, ALU.mult))
                for tap in range(1, 4):
                    ins = stt(cv[:, :], zc[:, tap:tap + ALL], w(tap), cv[:, :], ALU.mult, ALU.add)
                    if tap < 3:
                        seq(ins)
                ins.then_inc(cv_ok, 1)
                dve.wait_ge(cs_ok, k + 1)
                dve.wait_ge(cv_ok, k + 1)
                if q == 0:
                    stt(qh[:, h % 2, :], cv[:, META:ALL], DK ** -0.5, sgc[:, META:ALL], ALU.mult, ALU.mult).then_inc(qk_ok, 1)
                else:
                    tt(kh[:, h % 2, :], cv[:, :], sgc[:, :], ALU.mult).then_inc(qk_ok, 1)

            def mlstm(h):
                dve.wait_ge(mb_ok, h + 1)
                tt(Md[:, :].rearrange("p (t n) -> p t n", t=QT), Mb[:, :].rearrange("p (t n) -> p t n", t=QT),
                   later_bigT[:, :].unsqueeze(1).broadcast_to([P, QT, P]), ALU.add).then_inc(md_ok, 1)
                if h:
                    dve.wait_ge(av_ps, HEADS + h)
                for q in range(5):
                    dve.wait_ge(s_ps, 5 * h + q + 1)
                    b = bank((2 + q) % 4)
                    if q == 0:
                        dve.wait_ge(w_ok, 8 * h + 1)
                        tt(ATm[:, :], b[0:META, :], Wm[:, :], ALU.mult).then_inc(at_ok, 1)
                    else:
                        j = q - 1
                        dve.wait_ge(w_ok, 8 * h + min(2 * q + 1, 8))
                        tt(AT[:, j, 0:SEQ - j * P], b[:, 0:SEQ - j * P], Wd[:, 0:SEQ - j * P], ALU.mult).then_inc(at_ok, 1)
                dve.wait_ge(av_ps, HEADS + h + 1)
                dve.wait_ge(em_ok, h + 1)
                if h:
                    dve.wait_ge(y_ok, 8 + 2 * h)
                    dve.wait_ge(ms_ok, 8 + 2 * h)
                seq(tt(gtmp[:, 0, :], bank(3), emn[:, :], ALU.max))
                seq(stt(gtmp[:, 0, :], bank(3), -1.0, gtmp[:, 0, :], ALU.mult, ALU.max))
                seq(nc.vector.reciprocal(gtmp[:, 1, :], gtmp[:, 0, :]))
                for v in range(2):
                    tt(on[:, v, :], bank(v), gtmp[:, 1, :], ALU.mult).then_inc(num_ok, 1)
                dve.wait_ge(num_ok, 2 * h + 2)
                scaled(HEADS + h, "hm", lambda v: on[:, v, :])

            def m_out(h):
                for v in range(2):
                    m = 2 * h + v
                    whole(f"mo{m}")
                    dve.wait_ge(on_ok, 8 + 2 * h + 2)
                    tt(on[:, v, :], on[:, v, :], sgr[:, :], ALU.mult).then_inc(y_ok, 1)
                    dve.wait_ge(ms_ok, 8 + m + 1)
                    tt(yl[:, m, :], on[:, v, :], yh[:, m, :].bitcast(FP32), ALU.subtract).then_inc(yl_b, 1)

            conv(0, 0)
            conv(0, 1)
            values("mv", 0)
            for h in range(HEADS):
                if h + 1 < HEADS:
                    conv(h + 1, 0)
                    conv(h + 1, 1)
                    values("mv", h + 1)
                mlstm(h)
                m_out(h)
            mixing(1, "tc", "yc")
            for m in range(KT):
                dve.wait_ge(ms_ok, 16 + m + 1)
                tt(yl[:, m, :], mix[:, m, :], yh[:, m, :].bitcast(FP32), ALU.subtract).then_inc(yl_b, 1)
            dve.wait_ge(out_s, 1)
            tt(ssf[:, 0, :, 0], ssf[:, 0, :, 0], ssf[:, 0, :, 1], ALU.add).then_inc(h_rs, 1)
            dve.wait_ge(o_ss, 1)
            dve.wait_ge(ld_h, 16)
            dve.wait_ge(ld_g, 48)
            for t in range(QT):
                for hf in range(2):
                    seq(stt(xn[:, t, hf * SEQ:(hf + 1) * SEQ], accumulators("out", hf, t), ssf[:, 0, t, 0:1],
                            gains[:, 0, hf * SEQ:(hf + 1) * SEQ], ALU.mult, ALU.mult))
                tt(hres[:, t, :], hres[:, t, :], xn[:, t, :], ALU.add).then_inc(h_ok, 1)
            dve.wait_ge(o_ss, 2)
            tt(ssf[:, 1, :, 0], ssf[:, 1, :, 0], ssf[:, 1, :, 1], ALU.add).then_inc(h_rs, 1)
            dve.wait_ge(o_ss, 3)
            dve.wait_ge(h_ok, QT)
            for t in range(QT):
                stt(xn[:, t, :], hres[:, t, :], ssf[:, 1, t, 0:1], gains[:, 1, :], ALU.mult, ALU.mult).then_inc(n_ok, 1)
            for f in range(KT):
                dve.wait_ge(nh_ok, f + 1)
                tt(nl[:, f, :], bank(f % 4), nh[:, f, :].bitcast(FP32), ALU.subtract).then_inc(nl_ok, 1)
            for m in range(FT):
                whole(f"up{m}")
                tt(U[:, m, :], U[:, m, :], U[:, m, :], ALU.mult).then_inc(U_ok, 1)
            for k in range(2 * FT):
                dve.wait_ge(U_ok, k % FT + 1)
                dve.wait_ge(uh_ok, k + 1)
                tt(ul[:, k % 4, :], U[:, k % FT, :], uh[:, k % 4, :].bitcast(FP32), ALU.subtract).then_inc(ul_ok, 1)
            dve.wait_ge(o_ss, 4)
            tt(ssf[:, 2, :, 0], ssf[:, 2, :, 0], ssf[:, 2, :, 1], ALU.add).then_inc(h_rs, 1)
            dve.wait_ge(o_ss, 5)
            for t in range(QT):
                for hf in range(2):
                    seq(stt(xn[:, t, hf * SEQ:(hf + 1) * SEQ], accumulators("down", hf, t), ssf[:, 2, t, 0:1],
                            gains[:, 2, hf * SEQ:(hf + 1) * SEQ], ALU.mult, ALU.mult))
                tt(hres[:, t, :], hres[:, t, :], xn[:, t, :], ALU.add).then_inc(fin, 1)

        @block.tensor
        def _(pe):
            mm = nc.tensor.matmul

            def rhs(kind, k):
                if kind == "x":
                    return xh[:, k, META:ALL], xl[:, k, META:ALL]
                h_, l_ = {"cq": (cqh, cql), "y": (yh, yl), "n": (nh, nl)}[kind]
                return h_[:, k, :], l_[:, k, :]

            def gemm(name):
                t = tl[name]
                if t.need:
                    pe.wait_ge(gfree[t.slot], t.need)
                for c in t.chunks:
                    pe.wait_ge(split_done, chunks[c]["r"] + 1)
                ps = GP[t.slot]
                if t.kind == "F":
                    s0 = chunks[t.chunks[0]]["hl"]
                    for k in range(t.kt):
                        w = slice(k * t.width + t.off, k * t.width + t.off + t.m)
                        ah, al = rhs(t.rhs, k)
                        for p_, (wt, av, hx) in enumerate([(whi, ah, xh), (whi, al, xl), (wlo, ah, xh)]):
                            st, sp_ = (k == 0 and p_ == 0), (k == t.kt - 1 and p_ == 2)
                            if t.both:
                                for b in range(2):
                                    ins = mm(ps[0:t.m, b * SEQ:b * SEQ + HALF], wt[:, s0, w],
                                             hx[:, k, b * HALF:(b + 1) * HALF], start=st, stop=sp_)
                            else:
                                ins = mm(ps[0:t.m, 0:SEQ], wt[:, s0, w], av, start=st, stop=sp_)
                elif t.kind in ("V", "VM"):
                    s0 = chunks[t.chunks[0]]["hl"]
                    for i in range(QT if t.kind == "V" else 1):
                        tok = slice(META + i * P, META + (i + 1) * P) if t.kind == "V" else slice(0, META)
                        o_ = ps[:, i * DV:(i + 1) * DV] if t.kind == "V" else ps[0:META, 0:DV]
                        for k in range(KT):
                            for p_, (at_, wt) in enumerate([(xh, whi), (xh, wlo), (xl, whi)]):
                                ins = mm(o_, at_[:, k, tok], wt[:, s0:s0 + 2, k * P:(k + 1) * P],
                                         start=(k == 0 and p_ == 0), stop=(k == KT - 1 and p_ == 2))
                elif t.kind == "W":
                    s0 = chunks[t.chunks[0]]["hl"]
                    for i in range(QT):
                        tok = slice(META + i * P, META + (i + 1) * P)
                        for k in range(KT):
                            for p_, (at_, wt) in enumerate([(xh, whi), (xh, wlo), (xl, whi)]):
                                ins = mm(ps[:, i * IDX_H:(i + 1) * IDX_H], at_[:, k, tok], wt[:, s0, k * IDX_H:(k + 1) * IDX_H],
                                         start=(k == 0 and p_ == 0), stop=(k == KT - 1 and p_ == 2))
                else:
                    h = int(name[2:])
                    for b in range(2):
                        ins = mm(ps[:, b * SEQ:b * SEQ + HALF], a2[:, h * DK:(h + 1) * DK], aT[:, b * HALF:(b + 1) * HALF],
                                 start=True, stop=True)
                ins.then_inc(gemm_done, 1)

            def token_gemm(name, n, hf, last, parts):
                t = tl[f"{name}{hf}_{n}"]
                c = chunks[t.chunks[0]]
                pe.wait_ge(split_done, c["r"] + 1)
                for k in range(2):
                    ah, al = parts(k)
                    for i in range(QT):
                        for p_, (av, wt) in enumerate([(ah, whi), (ah, wlo), (al, whi)]):
                            ins = mm(accumulators(name, hf, i), av[:, i * P:(i + 1) * P], wt[:, c["hl"], k * SEQ:(k + 1) * SEQ],
                                     start=(n == 0 and k == 0 and p_ == 0), stop=(last and k == 1 and p_ == 2))
                ins.then_inc(gemm_done, 1)

            pe.wait_ge(masks, 1)
            pe.wait_ge(pool_c, 7 + len(LEVELS))
            pe.wait_ge(ld_rows, 16 * NROWDMA)
            nc.tensor.transpose(GP[0][:, 0:NROW], brow[:, :], ident[0:NROW, 0:NROW]).then_inc(col_ps, 1)
            pe.wait_ge(xn_ok, QT + 1)
            for f in range(KT):
                if f >= 4:
                    pe.wait_ge(xl_ok, f - 3)
                for t in range(QT):
                    ins = nc.tensor.transpose(bank(f % 4)[:, t * P:(t + 1) * P], X[:, t, f * P:(f + 1) * P], ident[:, :])
                ins.then_inc(xt_ps, 1)
            for f in range(KT):
                ins = nc.tensor.transpose(GP[1][:, f * META:(f + 1) * META], Xm[:, f * P:(f + 1) * P], ident[0:META, 0:META])
            ins.then_inc(xt_ps, 1)
            pe.wait_ge(ld_line, 48)
            pe.wait_ge(col_ok, 1)
            pe.wait_ge(xl_ok, KT + 1)
            for h in range(DSA_H):
                if h >= 2:
                    pe.wait_ge(line_ok, h - 1)
                for c0, c1 in ((0, SEQ), (SEQ, LINE)):
                    ins = mm(GP[h % 2][:, c0:c1], t5[:, h:h + 1].broadcast_to([BUCKETS, P]), oh[:, c0:c1], start=True, stop=True)
                ins.then_inc(line_ps, 1)
            pe.wait_ge(line_ok, DSA_H)
            gemm("cq0")
            gemm("cq1")
            gemm("ckv")
            pe.wait_ge(cqsq, 1)
            for k in range(2):
                ins = mm(PA[0][:, 0:SEQ], ones[:, :], sq[:, k, :], start=(k == 0), stop=(k == 1))
            ins.then_inc(ssq_ps, 1)

            def summed(ps, src):
                for b in range(2):
                    ins = mm(ps[:, b * SEQ:b * SEQ + HALF], ones[:, :], src[:, b * HALF:(b + 1) * HALF], start=True, stop=True)
                ins.then_inc(ssq_ps, 1)

            pe.wait_ge(kvsq, 1)
            summed(PA[1], sqk)
            gemm("ik")
            pe.wait_ge(rq_ok, 1)
            pe.wait_ge(gfree[tl["ik"].slot], tl["ik"].freed)
            summed(PA[0], ki)
            gemm("iw")
            pe.wait_ge(xcsq, 1)
            pe.wait_ge(rk_ok, 1)
            summed(PA[1], sqk)
            pe.wait_ge(kvT_ok, 1)
            pe.wait_ge(xc_ok, 1)
            for t in range(QT):
                nc.tensor.transpose(PA[0][:, t * P:(t + 1) * P], kvT[:, META + t * P:META + (t + 1) * P], ident[:, :])
            nc.tensor.transpose(PA[0][0:META, QT * P:(QT + 1) * P], kvT[:, 0:META], ident[:, :]).then_inc(kvn_ps, 1)
            pe.wait_ge(cqs_ok, 1)
            for m in range(4):
                gemm(f"iq{m}")
            pe.wait_ge(kn_ok, 1)
            pe.wait_ge(kvn_ok, 2)
            for m in range(4):
                pe.wait_ge(gfree[tl[f"iq{m}"].slot], tl[f"iq{m}"].freed)
            for v in range(QT * IDX_H):
                i, h = v // IDX_H, v % IDX_H
                w = META + P * (i + 1)
                if v >= 2:
                    pe.wait_ge(sc_rl, v - 1)
                r = slice(64 * (h % 2), 64 * (h % 2) + 64)
                for c0 in range(0, w, SEQ):
                    ins = mm(PA[v % 2][:, c0:min(c0 + SEQ, w)], qi[r, h // 2, i * P:(i + 1) * P], kn[r, c0:min(c0 + SEQ, w)],
                             start=True, stop=True)
                ins.then_inc(sc_ps, 1)
            for h in range(DSA_H):
                gemm(f"uq{h}")
            for m in range(KT):
                gemm(f"gb{m}")
            for nm in ("uq15", "uq14", "gb7", "gb6"):
                pe.wait_ge(gfree[tl[nm].slot], tl[nm].freed)
            pe.wait_ge(sc_rl, QT * IDX_H)

            def logits(v):
                i, h = v // DSA_H, v % DSA_H
                w = META + P * (i + 1)
                pe.wait_ge(keep_ok, i + 1)
                if v >= 2:
                    pe.wait_ge(lg_mn, v - 1)
                for c0 in range(0, w, SEQ):
                    c = slice(c0, min(c0 + SEQ, w))
                    mm(PA[v % 2][:, c], qlat[:, h, i * P:(i + 1) * P], kvT[:, c], start=True, stop=False)
                    ins = mm(PA[v % 2][:, c], identb[:, :], keep[:, i, c], start=False, stop=True)
                ins.then_inc(lg_ps, 1)

            logits(0)
            logits(1)
            for g in range(GROUPS):
                i = g // NHEADS2
                if g + 1 < GROUPS:
                    logits(2 * g + 2)
                    logits(2 * g + 3)
                pe.wait_ge(p_nrm, 2 * g + 2)
                if g:
                    pe.wait_ge(pt_a, g)
                    pe.wait_ge(pt_d, pt_d_after(g - 1))
                for s_ in range(2):
                    v = (2 * g + s_) % 4
                    for j in range(i + 1):
                        nc.tensor.transpose(GP[0][:, (2 * j + s_) * P:(2 * j + s_ + 1) * P],
                                            L[:, v, META + j * P:META + (j + 1) * P], ident[:, :])
                    ins = nc.tensor.transpose(GP[1][0:META, (g % 2 * 2 + s_) * P:(g % 2 * 2 + s_ + 1) * P], L[:, v, 0:META], ident[:, :])
                ins.then_inc(pt_ps, 1)
                pe.wait_ge(pt_a, g + 1)
                pe.wait_ge(pt_d, pt_d_after(g))
                if g >= 2:
                    pe.wait_ge(ol_ev, g - 1)
                o_ = GP[1][:, SEQ + (g % 2) * 2 * P:SEQ + (g % 2 + 1) * 2 * P]
                mm(o_, kvm[:, :], PTm[:, g % 2, :], start=True, stop=False)
                for j in range(i + 1):
                    ins = mm(o_, kvn[:, j, :], PT[:, g % 2, j, :], start=False, stop=(j == i))
                ins.then_inc(pv_ps, 1)
            pe.wait_ge(ld_uv, 32)
            pe.wait_ge(ol_ev, GROUPS)
            for m in range(KT):
                if m >= 2:
                    pe.wait_ge(yl_b, m - 1)
                for s_ in range(2):
                    ins = mm(PA[m % 2][:, 0:SEQ], uvp[:, 2 * m + s_, :], qlat[:, 2 * m + s_, :], start=(s_ == 0), stop=(s_ == 1))
                ins.then_inc(uv_ps, 1)
            pe.wait_ge(yl_b, KT)
            for m in range(KT):
                gemm(f"yb{m}")
            gemm("ga")
            pe.wait_ge(gfree[tl["ga"].slot], tl["ga"].freed)
            pe.wait_ge(ld_a, 32)

            def level(h, l):
                k = 8 * h + l
                if l < len(LEVELS):
                    pe.wait_ge(lv_qk, 7 * h + l + 1)
                if k >= 4:
                    pe.wait_ge(lv_sel, k - 3)
                if h and l == 0:
                    pe.wait_ge(on_ok, 2 * h)
                for i in range(QT):
                    if l < len(LEVELS):
                        b = (7 * h + l) % 2
                        ins = mm(bank(k % 4)[:, i * 64:(i + 1) * 64], KL[:, b, i * P:(i + 1) * P], QL[:, b, i * 64:(i + 1) * 64],
                                 start=True, stop=True)
                    else:
                        ins = mm(bank(k % 4)[:, i * P:(i + 1) * P], kh[:, h % 2, META + i * P:META + (i + 1) * P],
                                 qh[:, h % 2, i * P:(i + 1) * P], start=True, stop=True)
                ins.then_inc(lv_ps, 1)

            def weighted(k, h):
                for v in range(2):
                    c = slice(v * P, (v + 1) * P)
                    mm(bank(v), vm[:, h % 2, c], ATm[:, :], start=True, stop=False)
                    for j in range(QT):
                        ins = mm(bank(v)[:, j * P:SEQ], vh[:, h % 2, j, c], AT[:, j, 0:SEQ - j * P], start=False, stop=(j == QT - 1))
                return ins

            def squares(k):
                pe.wait_ge(av_sq, k + 1)
                for v in range(2):
                    ins = mm(bank(2), ones[:, :], sqo[:, v, :], start=(v == 0), stop=(v == 1))
                ins.then_inc(av_ss, 1)

            def evacuated(*names):
                for nm in names:
                    pe.wait_ge(gfree[tl[nm].slot], tl[nm].freed)

            for nm in ("gq0", "gk0", "gg0", "gv0A", "gv0M"):
                gemm(nm)
            for h in range(HEADS):
                evacuated(f"gq{h}", f"gk{h}", f"gv{h}A", f"gv{h}M")
                nxt = [f"gq{h + 1}", f"gk{h + 1}", f"gg{h + 1}", f"gv{h + 1}A", f"gv{h + 1}M"] if h + 1 < HEADS else []
                for l in range(8):
                    level(h, l)
                    if l in (0, 1, 2) and nxt:
                        gemm(nxt[l])
                if nxt:
                    gemm(nxt[3])
                    gemm(nxt[4])
                pe.wait_ge(lv_sel, 8 * h + 8)
                for q, j in enumerate([2, 1, 0]):
                    pe.wait_ge(od_q, 4 * h + q + 1)
                    mm(bank(q)[:, 0:SEQ - (j + 1) * P], KHt[:, META + j * P:META + (j + 1) * P], QQ[:, (j + 1) * P:SEQ],
                       start=True, stop=True).then_inc(od_ps, 1)
                pe.wait_ge(od_q, 4 * h + 4)
                mm(bank(3)[0:META, :], KHt[:, 0:META], QQ[:, :], start=True, stop=True).then_inc(od_ps, 1)
                pe.wait_ge(od_ev, 4 * h + 4)
                weighted(h, h).then_inc(av_ps, 1)
                squares(h)
                gemm(f"gr{2 * h}")
                gemm(f"gr{2 * h + 1}")
            pe.wait_ge(yl_b, 2 * KT)
            for m in range(KT):
                gemm(f"ta{m}")
                gemm(f"ya{m}")
            gemm("mi")
            gemm("mf")
            pe.wait_ge(u_ok, 1)
            for t in range(QT):
                nc.tensor.transpose(bank(0)[:, t * HEADS:(t + 1) * HEADS], u[:, META + t * P:META + (t + 1) * P], ident[0:HEADS, 0:HEADS])
            nc.tensor.transpose(bank(0)[0:META, QT * HEADS:(QT + 1) * HEADS], u[:, 0:META], ident[0:HEADS, 0:HEADS]).then_inc(uT_ps, 1)
            for nm in ("mq0", "mk0", "mv0A", "mv0M"):
                gemm(nm)
            pe.wait_ge(M_ok, 1)
            pe.wait_ge(uT_ok, 2)
            for h in range(HEADS):
                if h + 1 < HEADS:
                    for nm in (f"mq{h + 1}", f"mk{h + 1}", f"mv{h + 1}A", f"mv{h + 1}M"):
                        gemm(nm)
                evacuated(f"mv{h}A", f"mv{h}M")
                pe.wait_ge(qk_ok, 2 * h + 2)
                if h:
                    pe.wait_ge(num_ok, 2 * h)
                    pe.wait_ge(av_rs, HEADS + h)
                mm(bank(0), ident[0:HEADS, h:h + 1].broadcast_to([HEADS, P]), M[:, META:ALL], start=True, stop=True).then_inc(mb_ps, 1)
                mm(bank(1), ident[0:HEADS, h:h + 1].broadcast_to([HEADS, P]), bcum[:, META:ALL], start=True, stop=True).then_inc(mb_ps, 1)
                for q in range(5):
                    if q == 2:
                        pe.wait_ge(mb_ok, h + 1)
                    if q == 3:
                        pe.wait_ge(em_ok, h + 1)
                    if q == 4:
                        pe.wait_ge(at_ok, 5 * h + 1)
                    b = bank((2 + q) % 4)
                    if q == 0:
                        ins = mm(b[0:META, :], kh[:, h % 2, 0:META], qh[:, h % 2, :], start=True, stop=True)
                    else:
                        j = q - 1
                        ins = mm(b[:, 0:SEQ - j * P], kh[:, h % 2, META + j * P:META + (j + 1) * P], qh[:, h % 2, j * P:SEQ],
                                 start=True, stop=True)
                    ins.then_inc(s_ps, 1)
                pe.wait_ge(at_ok, 5 * h + 5)
                weighted(HEADS + h, h)
                mm(bank(3), ones[0:META, :], ATm[:, :], start=True, stop=False)
                for j in range(QT):
                    ins = mm(bank(3)[:, j * P:SEQ], ones[:, :], AT[:, j, 0:SEQ - j * P], start=False, stop=(j == QT - 1))
                ins.then_inc(av_ps, 1)
                squares(HEADS + h)
                gemm(f"mo{2 * h}")
                gemm(f"mo{2 * h + 1}")
            pe.wait_ge(yl_b, 3 * KT)
            for m in range(KT):
                gemm(f"tc{m}")
                gemm(f"yc{m}")
            evacuated("yc6", "yc7", "tc6", "tc7")
            pe.wait_ge(yl_b, 4 * KT)
            for hf in range(2):
                for n_ in range(4):
                    token_gemm("out", n_, hf, n_ == 3, lambda k: (yh[:, 2 * n_ + k, :], yl[:, 2 * n_ + k, :]))
            for f in range(KT):
                pe.wait_ge(n_ok, QT)
                if f >= 4:
                    pe.wait_ge(nl_ok, f - 3)
                for t in range(QT):
                    ins = nc.tensor.transpose(bank(f % 4)[:, t * P:(t + 1) * P], xn[:, t, f * P:(f + 1) * P], ident[:, :])
                ins.then_inc(nt_ps, 1)
            pe.wait_ge(nl_ok, KT)
            for m in range(FT):
                gemm(f"up{m}")
            for hf in range(2):
                if hf:
                    evacuated(f"up{FT - 1}", f"up{FT - 2}")
                for n_ in range(FT // 2):
                    pe.wait_ge(ul_ok, hf * FT + 2 * n_ + 2)
                    token_gemm("down", n_, hf, n_ == FT // 2 - 1,
                               lambda k: (uh[:, (2 * n_ + k) % 4, :], ul[:, (2 * n_ + k) % 4, :]))


_INS = ["x", "meta_tokens", "t5_bias", "g_pre_mix", "w_in", "b_in", "w_gla_a2", "b_gla_a", "g_gla_head", "w_br_gla",
        "g_dsa_q", "w_dsa_uq", "w_idx_q", "g_dsa_kv", "w_dsa_uv", "idx_ln_g", "idx_ln_b", "w_br_dsa", "ml_conv",
        "ml_f_bias", "g_ml_head", "w_br_ml", "w_out", "g_post_mix", "g_pre_mlp", "w_up", "w_down", "g_post_mlp"]


def bucket_onehot():
    import numpy as np
    import math
    n = np.maximum(LINE - 1 - (P - 1) - np.arange(LINE), 0)
    nf = np.maximum(n, 1).astype(np.float32)
    half = BUCKETS // 2
    large = half + (np.log(nf / np.float32(half)) / np.float32(math.log(128 / half)) * np.float32(half)).astype(np.int32)
    b = np.where(n < half, n, np.minimum(large, BUCKETS - 1))
    return (np.arange(BUCKETS)[:, None] == b[None, :]).astype(np.float32)


def kernel(**inputs):
    import numpy as _np
    import concourse.bacc as _bacc
    from concourse.bass_utils import run_bass_kernel_spmd as _run

    nc = _bacc.Bacc("TRN2", target_bir_lowering=False, num_devices=1)
    arrays, aps = {}, {}
    for name in _INS:
        v = _np.ascontiguousarray(inputs[name])
        arrays[f"in_{name}"] = v
        aps[name] = nc.dram_tensor(f"in_{name}", v.shape, FP32, kind="ExternalInput").ap()
    v = bucket_onehot()
    arrays["in_onehot"] = v
    aps["onehot"] = nc.dram_tensor("in_onehot", v.shape, FP32, kind="ExternalInput").ap()
    scratch = nc.dram_tensor("line_rows", (P, DSA_H, LPITCH), FP32).ap()
    out = nc.dram_tensor("out_h", (1, SEQ, D), FP32, kind="ExternalOutput").ap()
    build(nc, aps, scratch, out)
    r = _run(nc, [arrays], core_ids=[0])
    return r.results[0]["out_h"]
```

```python
import concourse.bass as bass
from concourse import mybir
from contextlib import ExitStack

FP32 = mybir.dt.float32
F32R = mybir.dt.float32r
BF16 = mybir.dt.bfloat16
U32 = mybir.dt.uint32
ACT = mybir.ActivationFunctionType
ALU = mybir.AluOpType

D = 1024
SEQ = 512
META = 16
ALL = META + SEQ
HALF = ALL // 2
P = 128
KT = D // P
QT = SEQ // P
HEADS = 4
DK = D // 2 // HEADS
DV = D // HEADS
DSA_H = 16
IDX_H = 8
TOPK = 128
FF = 4 * D
FT = FF // P
BUCKETS = 32
LINE = 655
LPITCH = 656
EPS = 1e-6
BIG = 1e30
MARK = -3e38
LEVELS = [64, 32, 16, 8, 4, 2, 1]
NRAW = 3
NHL = 4
CH = 1024

C_GQ, C_GK, C_GV, C_GR, C_GA = 0, 512, 1024, 2048, 3072
C_CQ, C_CKV, C_IK, C_IW = 3088, 3344, 3472, 3536
C_MQ, C_MK, C_MV, C_MO, C_MI, C_MF = 3544, 4056, 4568, 5592, 6616, 6620
C_GATE = 6624

ROWS = {}
ROW_LIST = []


def _rows():
    at = 0
    for name, n, src in [
        ("gq", 4, "b_in"), ("gk", 4, "b_in"), ("gr", 8, "b_in"), ("cq", 2, "b_in"), ("ckv", 1, "b_in"),
        ("ik", 1, "b_in"), ("mq", 4, "b_in"), ("mk", 4, "b_in"), ("mo", 8, "b_in"), ("gate", 24, "b_in"),
        ("small", 1, "b_in"), ("a2", 4, "b_gla_a"), ("hg", 2, "g_gla_head"),
        ("hm", 2, "g_ml_head"), ("dq", 2, "g_dsa_q"), ("dkv", 1, "g_dsa_kv"), ("ig", 1, "idx_ln_g"),
        ("ib", 1, "idx_ln_b"), ("fb", 1, "ml_f_bias"), ("cv", 32, "ml_conv"),
    ]:
        ROWS[name] = at
        ROW_LIST.append((name, n, src))
        at += n
    return at


NROW = _rows()
COLUMNS = {"gq": C_GQ, "gk": C_GK, "gr": C_GR, "cq": C_CQ, "ckv": C_CKV, "ik": C_IK, "mq": C_MQ, "mk": C_MK,
           "mo": C_MO, "gate": C_GATE}
WIDTHS = {"ik": 64, "ig": 64, "ib": 64}


def row_sources(a, name, count, src):
    if name == "small":
        return [((0, 32 * n), a[src][0:1, c0:c0 + 32]) for n, c0 in enumerate(SMALL)]
    if name == "fb":
        return [((0, 64), a[src][0:1, 0:HEADS])]
    w = WIDTHS.get(name, P)
    if src == "ml_conv":
        return [((8 * k, 0), a[src][0, k:k + 1, :].rearrange("k (t p) -> (k t) p", p=P)) for k in range(4)]
    c0 = COLUMNS.get(name, 0)
    part = a[src][0, c0:c0 + count * w].rearrange("(t p) -> t p", p=w)
    if w == 64:
        return [((0, 0), part), ((0, 64), part)]
    return [((0, 0), part)]


NROWDMA = 29


SMALL = [C_IW, C_GA, C_MI, C_MF]


class Tile:

    def __init__(self, kind, m=P, kt=KT, both=False, rhs="x", off=0, width=P):
        self.kind, self.m, self.kt, self.both, self.rhs, self.off, self.width = kind, m, kt, both, rhs, off, width


def plan():
    chunks, tiles = [], {}
    state = {"done": 0, "slot": 0, "freed": [0, 0]}

    def tile(name, use, new=0, kind="F", **k):
        t = Tile(kind, **k)
        t.chunks = list(use)
        t.slot = state["slot"]
        state["slot"] ^= 1
        t.need = state["freed"][t.slot]
        state["freed"][t.slot] += 1
        t.freed = state["freed"][t.slot]
        state["done"] += 1
        t.val = state["done"]
        tiles[name] = t
        for c in t.chunks[:new]:
            chunks[c]["end"] = t.val
        return t

    def chunk(src, c0, ncol, kt=KT, k0=0, twice=False):
        chunks.append(dict(src=src, c0=c0, n=ncol, kt=kt, k0=k0, twice=twice, end=None))
        return len(chunks) - 1

    def feature(name, src, c0, m=P, kt=KT, both=False, twice=False, rhs="x"):
        c = chunk(src, c0, m, kt, twice=twice)
        tile(name, [c], 1, kind="F", m=m * (2 if twice else 1), kt=kt, both=both, rhs=rhs, off=0,
             width=m * (2 if twice else 1))

    def values(name, c0):
        c = [chunk("w_in", c0, P), chunk("w_in", c0 + P, P)]
        assert c[0] % 2 == 0
        tile(name + "A", c, 0, kind="V", off=0)
        tile(name + "B", c, 0, kind="V", off=2)
        tile(name + "M", c, 2, kind="VM")

    def pad():
        if len(chunks) % 2:
            chunks.append(None)

    feature("ik", "w_in", C_IK, 64, both=True, twice=True)
    chunks.append(dict(src="w_in", c0=None, n=P, kt=KT, k0=0, twice=False, end=None))
    tile("small", [len(chunks) - 1], 1, both=True)
    feature("cq0", "w_in", C_CQ)
    feature("cq1", "w_in", C_CQ + P)
    feature("ckv", "w_in", C_CKV, both=True)
    for m in range(2):
        feature(f"gb{m}", "w_in", C_GATE + D + m * P)
    c = chunk("w_idx_q", 0, 512, 2)
    for m in range(4):
        tile(f"iq{m}", [c], int(m == 3), kind="F", m=P, kt=2, both=False, rhs="cq", off=m * P, width=512)
    for m in range(2, 6):
        feature(f"gb{m}", "w_in", C_GATE + D + m * P)
    for n in range(4):
        c = chunk("w_dsa_uq", n * 512, 512, 2)
        for m in range(4):
            tile(f"uq{4 * n + m}", [c], int(m == 3), kind="F", m=P, kt=2, both=False, rhs="cq", off=m * P,
                 width=512)
    for m in range(6, 8):
        feature(f"gb{m}", "w_in", C_GATE + D + m * P)
    for m in range(8):
        feature(f"yb{m}", "w_br_dsa", m * P, rhs="y")
    def gla(h):
        feature(f"gq{h}", "w_in", C_GQ + h * DK)
        feature(f"gk{h}", "w_in", C_GK + h * DK, both=True)
        tile(f"gg{h}", [], 0, kind="G")

    def pairs(name, c0, h):
        for v in range(2):
            feature(f"{name}{2 * h + v}", "w_in", c0 + (2 * h + v) * P)

    def all_values(name, c0):
        pad()
        values(name, c0)

    gla(0)
    all_values("gv0", C_GV)
    for h in range(HEADS):
        if h + 1 < HEADS:
            gla(h + 1)
        pairs("gr", C_GR, h)
        if h + 1 < HEADS:
            all_values(f"gv{h + 1}", C_GV + (h + 1) * DV)
    for m in range(8):
        feature(f"ta{m}", "w_in", C_GATE + m * P)
        feature(f"ya{m}", "w_br_gla", m * P, rhs="y")
    feature("mq0", "w_in", C_MQ, both=True)
    feature("mk0", "w_in", C_MK, both=True)
    all_values("mv0", C_MV)
    for h in range(HEADS):
        if h + 1 < HEADS:
            feature(f"mq{h + 1}", "w_in", C_MQ + (h + 1) * DK, both=True)
            feature(f"mk{h + 1}", "w_in", C_MK + (h + 1) * DK, both=True)
        pairs("mo", C_MO, h)
        if h + 1 < HEADS:
            all_values(f"mv{h + 1}", C_MV + (h + 1) * DV)
    for m in range(8):
        feature(f"tc{m}", "w_in", C_GATE + 2 * D + m * P)
        feature(f"yc{m}", "w_br_ml", m * P, rhs="y")
    for hf in range(2):
        for n in range(4):
            c = chunk("w_out", hf * 512, 512, 2, 2 * n)
            tile(f"out{hf}_{n}", [c], 1, kind="O")
            state["slot"] ^= 1
            state["freed"][tiles[f"out{hf}_{n}"].slot] -= 1
    for m in range(FT):
        feature(f"up{m}", "w_up", m * P, rhs="n")
    for hf in range(2):
        for n in range(FT // 2):
            c = chunk("w_down", hf * 512, 512, 2, 2 * n)
            tile(f"down{hf}_{n}", [c], 1, kind="O")
            state["slot"] ^= 1
            state["freed"][tiles[f"down{hf}_{n}"].slot] -= 1
    real, held = [], [None] * NHL
    for n, c in enumerate(chunks):
        if c is None:
            continue
        c["r"] = len(real)
        c["raw"] = c["r"] % NRAW
        c["hl"] = n % NHL
        c["after"] = held[c["hl"]]
        held[c["hl"]] = c["end"]
        real.append(c)
    total = [0] * NRAW
    for c in real:
        total[c["raw"]] += 16 * (len(SMALL) if c["c0"] is None else 2 if c["twice"] else 1)
        c["load"] = total[c["raw"]]
    return chunks, real, tiles



def build(nc, a, line, scratch, out):
    chunks, real, tl = plan()
    ctx = ExitStack()
    with ctx:
        def sb(name, shape, dt=FP32):
            return ctx.enter_context(nc.sbuf_tensor(name, shape, dt))

        def sem(name):
            return ctx.enter_context(nc.semaphore(name))

        def region(offset, specs):
            with ExitStack() as r:
                if offset:
                    r.enter_context(nc.sbuf_tensor(f"below_{specs[0][0]}", [P, offset // 4], FP32))
                return [r.enter_context(nc.sbuf_tensor(n, sh, dt)) for n, sh, dt in specs]

        wraw = sb("wraw", [P, NRAW, CH])
        whi = sb("whi", [P, NHL, CH], F32R)
        wlo = sb("wlo", [P, NHL, CH], F32R)
        ident = sb("ident", [P, P])
        identb = sb("identb", [P, P], BF16)
        ones = sb("ones", [P, P])
        later_neg = sb("later_neg", [P, P])
        later_big = sb("later_big", [P, P], BF16)
        later_bigT = sb("later_bigT", [P, P])
        col = sb("col", [P, NROW])
        eps = sb("eps", [P, 1])
        lm = sb("lm", [P, len(LEVELS), 64])
        small = sb("small", [P, ALL])

        XO = 0
        MIXO = XO + 2 * KT * ALL * 4
        YO = MIXO + KT * SEQ * 4
        LO = YO + DSA_H * ALL * 4
        PTO = LO + 4 * ALL * 4
        KVO = PTO + 2 * (QT + 1) * 2 * P * 4
        xh, xl, mix = region(XO, [("xh", [P, KT, ALL], F32R), ("xl", [P, KT, ALL], F32R), ("mix", [P, KT, SEQ], FP32)])
        rline, oh, t5 = region(MIXO, [("rline", [DSA_H, LPITCH], FP32), ("oh", [BUCKETS, LINE], FP32),
                                      ("t5", [BUCKETS, DSA_H], FP32)])
        (table, L, PT, PTm, kvT, kvn, kvm, keep, low, psm, prec, qlat, S, top8, rl, kn, wi) = region(YO, [
            ("table", [P, DSA_H, ALL], FP32), ("L", [P, 4, ALL], FP32), ("PT", [P, 2, QT, 2 * P], FP32),
            ("PTm", [META, 2, 2 * P], FP32), ("kvT", [P, ALL], FP32), ("kvn", [P, QT, P], FP32),
            ("kvm", [META, P], FP32), ("keep", [P, QT, ALL], BF16), ("low", [P, 64], FP32), ("psm", [P, 64], FP32),
            ("prec", [P, 64], FP32), ("qlat", [P, DSA_H, SEQ], FP32), ("S", [P, QT, ALL], FP32),
            ("top8", [P, 8], FP32), ("rl", [P, 2, ALL], FP32), ("kn", [P, ALL], FP32), ("wi", [P, QT, IDX_H], FP32)])
        QO = KVO + (ALL + QT * P + P) * 4 + QT * ALL * 2 + 3 * 64 * 4
        SO = QO + DSA_H * SEQ * 4
        (uvp,) = region(SO, [("uvp", [P, DSA_H, P], FP32)])
        cq, sq = region(LO, [("cq", [P, 2, SEQ], FP32), ("sq", [P, 2, SEQ], FP32)])
        cqh, cql = region(PTO, [("cqh", [P, 2, SEQ], F32R), ("cql", [P, 2, SEQ], F32R)])
        (qi,) = region(QO, [("qi", [P, 4, SEQ], FP32)])
        rk, ckv, ki, sqk = region(SO, [("rk", [P, ALL], FP32), ("ckv", [P, ALL], FP32), ("ki", [P, ALL], FP32),
                                       ("sqk", [P, ALL], FP32)])
        rq, xc = region(SO + QT * ALL * 4 + 64, [("rq", [P, SEQ], FP32), ("xc", [P, ALL], FP32)])
        X, Xm, gbc, junk, brow, ss = region(QO, [
            ("X", [P, QT, D], FP32), ("Xm", [META, D], FP32), ("gbc", [P, D], FP32), ("junk", [P, D], FP32),
            ("brow", [NROW, P], FP32), ("ss", [P, QT + 1], FP32)])
        yh, yl = region(YO, [("yh", [P, KT, SEQ], F32R), ("yl", [P, KT, SEQ], F32R)])
        AO = YO + 2 * KT * SEQ * 4
        (sgate, gtmp, vb, qh, kh, vh, vm, AT, ATm, sqo, rso, on, sgr) = region(AO, [
            ("sgate", [P, 2, SEQ], FP32), ("gtmp", [P, 2, SEQ], FP32), ("vb", [P, D], FP32),
            ("qh", [P, 2, SEQ], FP32), ("kh", [P, 2, ALL], FP32), ("vh", [P, 2, QT, DV], FP32),
            ("vm", [META, 2, DV], FP32), ("AT", [P, QT, SEQ], FP32), ("ATm", [META, SEQ], FP32),
            ("sqo", [P, 2, SEQ], FP32), ("rso", [P, SEQ], FP32), ("on", [P, 2, SEQ], FP32), ("sgr", [P, SEQ], FP32)])
        BO = AO + (2 * SEQ * 2 + D + 2 * SEQ + 2 * ALL + 2 * QT * DV + 2 * DV + QT * SEQ + SEQ + 2 * SEQ + SEQ + 2 * SEQ + SEQ) * 4
        (a2, G, E, QL, KL, QQ, KHt, gt, gf, gch) = region(BO, [
            ("a2", [32 + META, HEADS * DK], FP32),
            ("G", [P, 2, ALL], FP32), ("E", [P, SEQ], FP32), ("QL", [P, 2, SEQ // 2], FP32), ("KL", [P, 2, SEQ], FP32),
            ("QQ", [P, SEQ], FP32), ("KHt", [P, ALL - P], FP32), ("gt", [P, QT + 1], FP32), ("gf", [P, QT + 1], FP32),
            ("gch", [P, ALL], FP32)])
        (zc, cv, sgc, lf_, bcum_, M_, uT, uTm, fbias_, Mb, Md, Wd, Wm, emn) = region(BO, [
            ("zc", [P, ALL + 3], FP32), ("cv", [P, ALL], FP32), ("sgc", [P, ALL], FP32), ("lf", [64 + HEADS, ALL], FP32),
            ("bcum", [64 + HEADS, ALL], FP32), ("M", [64 + HEADS, ALL], FP32),
            ("uT", [P, QT, HEADS], FP32), ("uTm", [META, HEADS], FP32),
            ("fbias", [64 + HEADS, 1], FP32), ("Mb", [P, SEQ], FP32), ("Md", [P, SEQ], FP32), ("Wd", [P, SEQ], FP32),
            ("Wm", [META, SEQ], FP32), ("emn", [P, SEQ], FP32)])
        GR = slice(64, 64 + HEADS)
        u, lf, bcum, M, fbias = small[GR, :], lf_[GR, :], bcum_[GR, :], M_[GR, :], fbias_[GR, :]
        (hres,) = region(0, [("hres", [P, QT, D], FP32)])
        nh, nl = region(QT * D * 4, [("nh", [P, KT, SEQ], F32R), ("nl", [P, KT, SEQ], F32R)])
        UO = QT * D * 4 + 2 * KT * SEQ * 4
        (U,) = region(UO, [("U", [P, FT, SEQ], FP32)])
        (xn,) = region(UO, [("xn", [P, QT, D], FP32)])
        (gains, uh, ul, jk, ssf) = region(UO + FT * SEQ * 4, [
            ("gains", [P, 3, D], FP32), ("uh", [P, 4, SEQ], F32R), ("ul", [P, 4, SEQ], F32R),
            ("jk", [P, SEQ], FP32), ("ssf", [P, 3, QT, 2], FP32)])

        def Ls(v):
            return L[:, v % 6, :] if v % 6 < 4 else rl[:, v % 6 - 4, :]

        GP = [ctx.enter_context(nc.psum_tensor(f"GP{i}", [P, 1024], FP32)) for i in range(2)]
        PA = [ctx.enter_context(nc.psum_tensor(f"PA{i}", [P, 1024], FP32)) for i in range(2)]

        def bank(i):
            return PA[i // 2][:, (i % 2) * SEQ:(i % 2 + 1) * SEQ]

        def halves(ps, n=P):
            return ps[0:n, :].rearrange("p (a b) -> p a b", a=2)[:, :, 0:HALF]

        def two(t, n=P):
            return t[0:n, 0:ALL].rearrange("p (a b) -> p a b", a=2)

        def accumulators(name, hf, t):
            pair = GP if (name == "out") == (hf == 0) else PA
            return pair[t // 2][:, (t % 2) * SEQ:(t % 2 + 1) * SEQ]

        def cc(name, k=0, n=P):
            return col[0:n, ROWS[name] + k:ROWS[name] + k + 1]

        raw_in = [sem(f"raw_in{i}") for i in range(NRAW)]
        hi_done, split_done, gemm_done = sem("hi_done"), sem("split_done"), sem("gemm_done")
        gfree = [sem(f"gfree{i}") for i in range(2)]
        act_c, dve_c, pool_c = sem("act_chain"), sem("dve_chain"), sem("pool_chain")
        row_zero, ld_rows, ld_x, ld_line = sem("row_zero"), sem("ld_rows"), sem("ld_x"), sem("ld_line")
        masks = sem("masks")
        col_ps, col_ok, ss_zero, rs_ok, xn_ok = sem("col_ps"), sem("col_ok"), sem("ss_zero"), sem("rs_ok"), sem("xn_ok")
        xt_ps, xh_ok, xl_ok = sem("xt_ps"), sem("xh_ok"), sem("xl_ok")
        line_ps, line_ok, table_in = sem("line_ps"), sem("line_ok"), sem("table_in")
        line_out, line_rep = sem("line_out"), sem("line_rep")
        cqsq, kvsq, kisq, xcsq, ssq_ps = sem("cqsq"), sem("kvsq"), sem("kisq"), sem("xcsq"), sem("ssq_ps")
        rq_ok, rk_ok, xc_ok = sem("rq_ok"), sem("rk_ok"), sem("xc_ok")
        cqs_ok, kvT_ok, kn_ok, kvn_ps, kvn_ok = sem("cqs_ok"), sem("kvT_ok"), sem("kn_ok"), sem("kvn_ps"), sem("kvn_ok")
        sc_ps, sc_rl, sc_acc, keep_ok = sem("sc_ps"), sem("sc_rl"), sem("sc_acc"), sem("keep_ok")
        lg_ps, lg_mn, p_exp, p_nrm = sem("lg_ps"), sem("lg_mn"), sem("p_exp"), sem("p_nrm")
        pt_ps, pt_a, pt_d, pv_ps, ol_ev = sem("pt_ps"), sem("pt_a"), sem("pt_d"), sem("pv_ps"), sem("ol_ev")
        uv_zero, ld_uv, uv_ps, yh_b, yl_b = sem("uv_zero"), sem("ld_uv"), sem("uv_ps"), sem("yh_b"), sem("yl_b")
        ld_a, gla_c, aT_ok, gg_a, gg_l, G_ok = sem("ld_a"), sem("gla_consts"), sem("aT_ok"), sem("gg_a"), sem("gg_l"), sem("G_ok")
        lv_w, lv_e, lv_qk, lv_ps, lv_sel = sem("lv_w"), sem("lv_e"), sem("lv_qk"), sem("lv_ps"), sem("lv_sel")
        od_e, od_q, od_ps, od_ev = sem("od_e"), sem("od_q"), sem("od_ps"), sem("od_ev")
        av_ps, av_sq, av_ss, av_rs, on_ok = sem("av_ps"), sem("av_sq"), sem("av_ss"), sem("av_rs"), sem("on_ok")
        sg_ok, y_ok, gate_ok, mix_ok = sem("sg_ok"), sem("y_ok"), sem("gate_ok"), sem("mix_ok")
        ld_v, zpad, z_ok, cv_ok, cs_ok, qk_ok = sem("ld_v"), sem("zpad"), sem("z_ok"), sem("cv_ok"), sem("cs_ok"), sem("qk_ok")
        fa_ok, fl_ok, u_ok, M_ok, uT_ps, uT_ok = sem("fa_ok"), sem("fl_ok"), sem("u_ok"), sem("M_ok"), sem("uT_ps"), sem("uT_ok")
        mb_ps, mb_ok, md_ok, em_ok = sem("mb_ps"), sem("mb_ok"), sem("md_ok"), sem("em_ok")
        s_ps, w_ok, at_ok, num_ok = sem("s_ps"), sem("w_ok"), sem("at_ok"), sem("num_ok")
        ms_ok, ms_d, M_one = sem("ms_ok"), sem("ms_d"), sem("M_one")
        ld_h, ld_g, out_s, o_ss, h_ok, h_rs, n_ok = sem("ld_h"), sem("ld_g"), sem("out_s"), sem("o_ss"), sem("h_ok"), sem("h_rs"), sem("n_ok")
        nt_ps, nh_ok, nl_ok = sem("nt_ps"), sem("nh_ok"), sem("nl_ok")
        u_r, U_ok, uh_ok, ul_ok, fin_ss, fin, out_done = sem("u_r"), sem("U_ok"), sem("uh_ok"), sem("ul_ok"), sem("fin_ss"), sem("fin"), sem("out_done")

        block = ctx.enter_context(nc.Block())
        NHEADS2 = DSA_H // 2
        WIO = 960
        GROUPS = QT * NHEADS2

        def pt_d_after(g):
            return g + 1 + max(g + 1 - 2 * NHEADS2, 0)

        @block.sync
        def _(sp):
            sp.wait_ge(row_zero, 1)
            n = 0
            for name, count, src in ROW_LIST:
                r = ROWS[name]
                for dst, part in row_sources(a, name, count, src):
                    sp.dma_start(brow[r + dst[0]:r + dst[0] + part.shape[0], dst[1]:dst[1] + part.shape[1]],
                                 part).then_inc(ld_rows, 16)
                    n += 1
            assert n == NROWDMA, n
            for c in real:
                if c["r"] >= NRAW:
                    sp.wait_ge(split_done, c["r"] - NRAW + 1)
                if c["r"] == 4:
                    sp.wait_ge(line_ok, 1)
                    sp.dma_start(line, rline[:, 0:LINE]).then_inc(line_out, 16)
                if c["r"] == 6:
                    sp.wait_ge(line_out, 16)
                    sp.dma_start(scratch[:, :, 0:LINE], line.unsqueeze(0).broadcast_to([P, DSA_H, LINE])).then_inc(line_rep, 16)
                if c["r"] == 14:
                    sp.wait_ge(line_rep, 16)
                    sp.dma_start(table[:, :, :], bass.AP(tensor=scratch.tensor, offset=P - 1,
                                                         ap=[[DSA_H * LPITCH - 1, P], [LPITCH, DSA_H], [1, ALL]])).then_inc(table_in, 16)
                if c["c0"] is None:
                    for n_, c0 in enumerate(SMALL):
                        sp.dma_start(wraw[:, c["raw"], :].rearrange("p (k n) -> p k n", n=P)[:, :, 32 * n_:32 * n_ + 32],
                                     a["w_in"][0, :, c0:c0 + 32].rearrange("(k p) n -> p k n", p=P)).then_inc(raw_in[c["raw"]], 16)
                    continue
                src = a[c["src"]][0, c["k0"] * P:(c["k0"] + c["kt"]) * P, c["c0"]:c["c0"] + c["n"]]
                src = src.rearrange("(k p) n -> p k n", p=P)
                w = c["n"] * (2 if c["twice"] else 1)
                dst = wraw[:, c["raw"], 0:c["kt"] * w].rearrange("p (k n) -> p k n", n=w)
                for rep in range(w // c["n"]):
                    sp.dma_start(dst[:, :, rep * c["n"]:(rep + 1) * c["n"]], src).then_inc(raw_in[c["raw"]], 16)

        @block.gpsimd
        def _(pool):
            nc.gpsimd.memset(ident[:, :], 0.0).then_inc(pool_c, 1)
            nc.gpsimd.memset(later_neg[:, :], 0.0).then_inc(pool_c, 1)
            nc.gpsimd.memset(later_bigT[:, :], 0.0).then_inc(pool_c, 1)
            pool.wait_ge(pool_c, 3)
            nc.gpsimd.affine_select(out=ident[:, :], in_=ident[:, :], compare_op=ALU.not_equal, fill=1.0, base=0,
                                    pattern=[[-1, P]], channel_multiplier=1).then_inc(pool_c, 1)
            nc.gpsimd.affine_select(out=later_neg[:, :], in_=later_neg[:, :], compare_op=ALU.is_ge, fill=-BIG, base=0,
                                    pattern=[[-1, P]], channel_multiplier=1).then_inc(pool_c, 1)
            nc.gpsimd.affine_select(out=later_bigT[:, :], in_=later_bigT[:, :], compare_op=ALU.is_ge, fill=BIG, base=0,
                                    pattern=[[1, P]], channel_multiplier=-1).then_inc(pool_c, 1)
            pool.wait_ge(pool_c, 6)
            nc.gpsimd.tensor_copy(identb[:, :], ident[:, :]).then_inc(masks, 1)
            nc.gpsimd.tensor_scalar(later_big[:, :], later_neg[:, :], -1.0, 1.0, ALU.mult, ALU.mult).then_inc(masks, 1)
            nc.gpsimd.memset(lm[:, :, :], 1.0).then_inc(pool_c, 1)
            pool.wait_ge(pool_c, 7)
            for l, B in enumerate(LEVELS):
                v = lm[:, l, :].rearrange("p (n b) -> p n b", b=B)
                nc.gpsimd.affine_select(out=v, in_=v, compare_op=ALU.is_ge, fill=0.0, base=0,
                                        pattern=[[-2 * B, 64 // B], [0, B]], channel_multiplier=1).then_inc(pool_c, 1)
                pool.wait_ge(pool_c, 8 + l)
            for l, B in enumerate(LEVELS):
                v = lm[:, l, :].rearrange("p (n b) -> p n b", b=B)
                nc.gpsimd.affine_select(out=v, in_=v, compare_op=ALU.is_ge, fill=0.0, base=B - 1,
                                        pattern=[[2 * B, 64 // B], [0, B]], channel_multiplier=-1).then_inc(masks, 1)
            pool.wait_ge(masks, 2 + len(LEVELS))
            for c in real:
                n = c["kt"] * c["n"] * (2 if c["twice"] else 1)
                src, hi, lo = wraw[:, c["raw"], 0:n], whi[:, c["hl"], 0:n], wlo[:, c["hl"], 0:n]
                pool.wait_ge(raw_in[c["raw"]], c["load"])
                if c["after"]:
                    pool.wait_ge(gemm_done, c["after"])
                nc.gpsimd.tensor_scalar(hi, src, 1.0, 1.0, ALU.mult, ALU.mult).then_inc(hi_done, 1)
                pool.wait_ge(hi_done, c["r"] + 1)
                nc.gpsimd.tensor_tensor(lo, src, hi.bitcast(FP32), ALU.subtract).then_inc(split_done, 1)

        @block.scalar
        def _(act):
            n = [0]

            def seq(ins):
                n[0] += 1
                ins.then_inc(act_c, 1)
                act.wait_ge(act_c, n[0])

            def lnexp():
                nc.scalar.preload_act_table_set("natural_log_exp_and_others")

            def inv_root(t, src, width):
                seq(nc.scalar.activation(t, src, ACT.Ln, bias=eps[0:t.shape[0], :], scale=1.0 / width))
                return nc.scalar.activation(t, t, ACT.Exp, scale=-0.5)

            def ready(name):
                t = tl[name]
                act.wait_ge(gemm_done, t.val)
                return GP[t.slot]

            def whole(name):
                act.wait_ge(gfree[tl[name].slot], tl[name].freed)

            act.dma_start(X[:, :, :], a["x"][0].rearrange("(t p) d -> p t d", p=P)).then_inc(ld_x, 16)
            act.dma_start(Xm[:, :], a["meta_tokens"]).then_inc(ld_x, 16)
            act.dma_start(gbc[:, :], a["g_pre_mix"].broadcast_to([P, D])).then_inc(ld_x, 16)
            act.dma_start(oh[:, :], a["onehot"]).then_inc(ld_line, 16)
            act.dma_start(t5[:, :], a["t5_bias"]).then_inc(ld_line, 16)
            lnexp()
            act.wait_ge(ld_x, 48)
            act.wait_ge(ss_zero, 1)
            seq(nc.scalar.activation(junk[0:META, :], Xm[:, :], ACT.Square, accum_out=ss[0:META, QT:QT + 1]))
            for t in range(QT):
                seq(nc.scalar.activation(junk[:, :], X[:, t, :], ACT.Square, accum_out=ss[:, t:t + 1]))
            inv_root(ss[:, :], ss[:, :], D).then_inc(rs_ok, 1)
            for f in range(KT):
                act.wait_ge(xt_ps, f + 1)
                nc.scalar.activation(xh[:, f, META:ALL], bank(f % 4), ACT.Copy).then_inc(xh_ok, 1)
            act.wait_ge(xt_ps, KT + 1)
            nc.scalar.activation(xh[:, :, 0:META], GP[1][:, 0:KT * META].rearrange("p (k m) -> p k m", m=META),
                                 ACT.Copy).then_inc(xh_ok, 1)
            act.wait_ge(line_ps, 1)
            nc.scalar.activation(rline[:, 0:LINE], GP[0][0:DSA_H, 0:LINE], ACT.Copy, scale=-1.0).then_inc(line_ok, 1)
            act.wait_ge(col_ok, 1)
            act.wait_ge(xl_ok, KT + 1)

            def gate_b(m):
                nc.scalar.activation(mix[:, m, :], ready(f"gb{m}")[:, 0:SEQ], ACT.Sigmoid, bias=cc("gate", 8 + m)).then_inc(gfree[tl[f"gb{m}"].slot], 1)

            nc.scalar.activation(two(ki), halves(ready("ik")), ACT.Identity, bias=cc("ik")).then_inc(gfree[tl["ik"].slot], 1)
            nc.scalar.activation(two(small), halves(ready("small")), ACT.Identity, bias=cc("small")).then_inc(gfree[tl["small"].slot], 1)
            act.wait_ge(xc_ok, 1)
            nc.scalar.activation(sqk[:, :], xc[:, :], ACT.Square).then_inc(xcsq, 1)
            act.wait_ge(ssq_ps, 2)
            inv_root(two(rk), halves(PA[1]), P).then_inc(rk_ok, 1)
            for k in range(2):
                nc.scalar.activation(cq[:, k, :], ready(f"cq{k}")[:, 0:SEQ], ACT.Identity, bias=cc("cq", k)).then_inc(gfree[tl[f"cq{k}"].slot], 1)
            whole("cq0")
            whole("cq1")
            nc.scalar.activation(sq[:, :, :], cq[:, :, :], ACT.Square).then_inc(cqsq, 1)
            nc.scalar.activation(two(ckv), halves(ready("ckv")), ACT.Identity, bias=cc("ckv")).then_inc(gfree[tl["ckv"].slot], 1)
            whole("ckv")
            nc.scalar.activation(sqk[:, :], ckv[:, :], ACT.Square).then_inc(kvsq, 1)
            act.wait_ge(ssq_ps, 3)
            inv_root(rq[:, :], PA[0][:, 0:SEQ], 2 * P).then_inc(rq_ok, 1)
            act.wait_ge(ssq_ps, 4)
            act.wait_ge(kn_ok, 1)
            inv_root(two(rk), halves(PA[1]), P).then_inc(rk_ok, 1)
            act.wait_ge(line_out, 16)
            gate_b(0)
            gate_b(1)
            act.wait_ge(kvn_ps, 1)
            nc.scalar.activation(kvn[:, :, :], PA[0][:, 0:QT * P].rearrange("p (t c) -> p t c", t=QT), ACT.Copy).then_inc(kvn_ok, 1)
            nc.scalar.activation(kvm[:, :], PA[0][0:META, QT * P:(QT + 1) * P], ACT.Copy).then_inc(kvn_ok, 1)
            nc.scalar.activation(wi[:, :, :], PA[0][:, WIO:WIO + QT * IDX_H].rearrange("p (t h) -> p t h", h=IDX_H),
                                 ACT.Copy, scale=IDX_H ** -0.5).then_inc(kvn_ok, 1)
            for m in range(4):
                nc.scalar.activation(qi[:, m, :], ready(f"iq{m}")[:, 0:SEQ], ACT.Copy, scale=0.125).then_inc(gfree[tl[f"iq{m}"].slot], 1)
            for v in range(QT * IDX_H):
                w = META + P * (v // IDX_H + 1)
                act.wait_ge(sc_ps, v + 1)
                if v >= 2:
                    act.wait_ge(sc_acc, v - 1)
                nc.scalar.activation(rl[:, v % 2, 0:w], PA[v % 2][:, 0:w], ACT.Relu).then_inc(sc_rl, 1)
                if v % IDX_H == IDX_H - 1:
                    gate_b(2 + v // IDX_H)
            for h in range(DSA_H):
                nc.scalar.activation(qlat[:, h, :], ready(f"uq{h}")[:, 0:SEQ], ACT.Copy, scale=-float(P) ** -0.5).then_inc(gfree[tl[f"uq{h}"].slot], 1)
            gate_b(6)
            gate_b(7)
            lnexp()

            def exps(v):
                i = v // DSA_H
                w = META + P * (i + 1)
                act.wait_ge(lg_mn, v + 1)
                nc.scalar.activation(Ls(v)[:, 0:w], Ls(v)[:, 0:w], ACT.Exp, bias=low[:, v:v + 1], scale=-1.0,
                                     accum_out=psm[:, v:v + 1]).then_inc(p_exp, 1)

            for v in range(4):
                exps(v)
            for g in range(GROUPS):
                i, h = g // NHEADS2, 2 * (g % NHEADS2)
                act.wait_ge(pt_ps, g + 1)
                if g >= 2:
                    act.wait_ge(pv_ps, g - 1)
                w = min(i + 1, 2)
                nc.scalar.activation(PT[:, g % 2, 0:w, :], GP[0][:, 0:w * 2 * P].rearrange("p (j n) -> p j n", j=w),
                                     ACT.Copy).then_inc(pt_a, 1)
                if g + 2 < GROUPS:
                    exps(2 * g + 4)
                    exps(2 * g + 5)
                act.wait_ge(pv_ps, g + 1)
                nc.scalar.activation(qlat[:, h:h + 2, i * P:(i + 1) * P],
                                     GP[1][:, SEQ + (g % 2) * 2 * P:SEQ + (g % 2 + 1) * 2 * P].rearrange("p (h n) -> p h n", h=2),
                                     ACT.Copy).then_inc(ol_ev, 1)
                if g == 3 * NHEADS2:
                    act.wait_ge(uv_zero, 1)
                    act.dma_start(uvp[:, 0::2, 0:64], a["w_dsa_uv"][0, 0::2].rearrange("h c d -> c h d")).then_inc(ld_uv, 16)
                    act.dma_start(uvp[:, 1::2, 64:P], a["w_dsa_uv"][0, 1::2].rearrange("h c d -> c h d")).then_inc(ld_uv, 16)
            for m in range(KT):
                act.wait_ge(uv_ps, m + 1)
                nc.scalar.activation(yh[:, m, :], PA[m % 2][:, 0:SEQ], ACT.Copy).then_inc(yh_b, 1)
            act.wait_ge(yl_b, KT)
            act.dma_start(a2[32:32 + META, :], a["w_gla_a2"][0]).then_inc(ld_a, 16)
            act.dma_start(vb[:, :], a["b_in"][0:1, C_GV:C_GV + D].broadcast_to([P, D])).then_inc(ld_a, 16)
            def gate_of(h):
                ps = ready(f"gg{h}")
                if h:
                    act.wait_ge(gg_l, h)
                    act.wait_ge(G_ok, h)
                nc.scalar.activation(two(gch), halves(ps), ACT.Abs, bias=cc("a2", h)).then_inc(gg_a, 1)
                act.wait_ge(gg_a, h + 1)
                seq(nc.scalar.activation(gch[:, :], gch[:, :], ACT.Exp, scale=-1.0))
                nc.scalar.activation(gch[:, :], gch[:, :], ACT.Ln, bias=1.0).then_inc(gg_l, 1)

            def level(h, l):
                k = len(LEVELS) * h + l
                act.wait_ge(lv_w, k + 1)
                nc.scalar.activation(E[:, :], E[:, :], ACT.Exp, scale=1.0 / 16.0).then_inc(lv_e, 1)

            def off(h):
                g0 = G[:, h % 2, :]
                if h:
                    act.wait_ge(od_q, 4 * h)
                    act.wait_ge(od_ps, 4 * h)
                nc.scalar.activation(QQ[:, :], g0[:, META:ALL], ACT.Exp, scale=1.0 / 16.0).then_inc(od_e, 1)
                nc.scalar.activation(gf[:, :], g0[:, META - 1::P], ACT.Exp, scale=1.0 / 16.0).then_inc(od_e, 1)
                seq(nc.scalar.activation(gt[:, :], g0[:, META - 1::P], ACT.Copy, scale=1.0 / 16.0))
                nc.scalar.activation(KHt[:, 0:META], g0[:, 0:META], ACT.Exp, bias=gt[:, 0:1], scale=-1.0 / 16.0).then_inc(od_e, 1)
                for j in range(3):
                    nc.scalar.activation(KHt[:, META + j * P:META + (j + 1) * P], g0[:, META + j * P:META + (j + 1) * P],
                                         ACT.Exp, bias=gt[:, j + 1:j + 2], scale=-1.0 / 16.0).then_inc(od_e, 1)
                if h:
                    act.wait_ge(av_ps, h)
                for q, j in enumerate([2, 1, 0]):
                    act.wait_ge(od_ps, 4 * h + q + 1)
                    w = SEQ - P * (j + 1)
                    nc.scalar.activation(AT[:, j, P:P + w], bank(q)[:, 0:w], ACT.Copy).then_inc(od_ev, 1)
                act.wait_ge(od_ps, 4 * h + 4)
                nc.scalar.activation(ATm[:, :], bank(3)[0:META, :], ACT.Copy).then_inc(od_ev, 1)

            def head_norm(k, src):
                nc.scalar.activation(sqo[:, :, :], src, ACT.Square).then_inc(av_sq, 1)
                act.wait_ge(av_ss, k + 1)
                inv_root(rso[:, :], bank(2), DV).then_inc(av_rs, 1)

            def silus(h):
                for v in range(2):
                    m = 2 * h + v
                    ps = ready(f"gr{m}")
                    if m >= 2:
                        act.wait_ge(y_ok, m - 1)
                    nc.scalar.activation(sgate[:, v, :], ps[:, 0:SEQ], ACT.Sigmoid, bias=cc("gr", m)).then_inc(sg_ok, 1)
                lnexp()

            def high_parts(base, h):
                for v in range(2):
                    m = 2 * h + v
                    act.wait_ge(y_ok, base + m + 1)
                    nc.scalar.activation(yh[:, m, :], on[:, v, :], ACT.Copy).then_inc(ms_ok, 1)

            def finish(h):
                act.wait_ge(av_ps, h + 1)
                head_norm(h, PA[0][:, :].rearrange("p (a b) -> p a b", a=2))

            gate_of(0)
            for h in range(HEADS):
                level(h, 0)
                if h:
                    finish(h - 1)
                level(h, 1)
                if h + 1 < HEADS:
                    gate_of(h + 1)
                level(h, 2)
                silus(h)
                if h:
                    high_parts(0, h - 1)
                for l in range(3, 7):
                    level(h, l)
                off(h)
            finish(HEADS - 1)
            high_parts(0, HEADS - 1)

            def gates(branch, name, at):
                for m in range(KT):
                    k = 8 * branch + m
                    ps = ready(f"{name}{m}")
                    if k >= 2:
                        act.wait_ge(mix_ok, k - 1)
                    nc.scalar.activation(sgate[:, m % 2, :], ps[:, 0:SEQ], ACT.Sigmoid, bias=cc("gate", at + m)).then_inc(gfree[tl[f"{name}{m}"].slot], 1)

            gates(0, "ta", 0)
            lnexp()
            act.wait_ge(mix_ok, KT)
            act.dma_start(vb[:, :], a["b_in"][0:1, C_MV:C_MV + D].broadcast_to([P, D])).then_inc(ld_v, 16)
            act.wait_ge(ms_d, 2)
            nc.scalar.activation(lf, bcum, ACT.Abs).then_inc(fa_ok, 1)
            act.wait_ge(fa_ok, 1)
            seq(nc.scalar.activation(lf, lf, ACT.Exp, scale=-1.0))
            nc.scalar.activation(lf, lf, ACT.Ln, bias=1.0).then_inc(fl_ok, 1)

            def conv_in(h, q):
                k = 2 * h + q
                ps = ready(f"m{'qk'[q]}{h}")
                act.wait_ge(zpad, 1)
                if k:
                    act.wait_ge(cv_ok, k)
                nc.scalar.activation(zc[:, 3:3 + ALL].rearrange("p (a b) -> p a b", a=2), halves(ps), ACT.Identity,
                                     bias=cc(f"m{'qk'[q]}", h)).then_inc(gfree[tl[f"m{'qk'[q]}{h}"].slot], 1)
                act.wait_ge(cv_ok, k + 1)
                if k:
                    act.wait_ge(qk_ok, k)
                nc.scalar.activation(sgc[:, :], cv[:, :], ACT.Sigmoid).then_inc(cs_ok, 1)

            def maxima(h):
                if h:
                    act.wait_ge(md_ok, h)
                    act.wait_ge(at_ok, 5 * h)
                act.wait_ge(mb_ps, 2 * h + 1)
                nc.scalar.activation(Mb[:, :], bank(0), ACT.Copy).then_inc(mb_ok, 1)
                act.wait_ge(mb_ps, 2 * h + 2)
                if h:
                    act.wait_ge(num_ok, 2 * h)
                nc.scalar.activation(emn[:, :], bank(1), ACT.Exp).then_inc(em_ok, 1)
                act.wait_ge(mb_ok, h + 1)
                act.wait_ge(uT_ok, 2)
                act.wait_ge(md_ok, h + 1)
                nc.scalar.activation(Wm[:, :], Mb[0:META, :], ACT.Exp, bias=uTm[:, h:h + 1], scale=-1.0).then_inc(w_ok, 1)

            def decay(h, j):
                if j:
                    act.wait_ge(at_ok, 5 * h + j + 1)
                nc.scalar.activation(Wd[:, 0:P], Md[:, j * P:(j + 1) * P], ACT.Exp, bias=uT[:, j, h:h + 1], scale=-1.0).then_inc(w_ok, 1)
                if j < QT - 1:
                    nc.scalar.activation(Wd[:, P:SEQ - j * P], Mb[:, (j + 1) * P:SEQ], ACT.Exp, bias=uT[:, j, h:h + 1],
                                         scale=-1.0).then_inc(w_ok, 1)

            def out_gates(h):
                for v in range(2):
                    m = 2 * h + v
                    ps = ready(f"mo{m}")
                    if h:
                        act.wait_ge(y_ok, 8 + m - 1)
                    nc.scalar.activation(sgate[:, v, :], ps[:, 0:SEQ], ACT.Sigmoid, bias=cc("mo", m)).then_inc(gfree[tl[f"mo{m}"].slot], 1)

            conv_in(0, 0)
            conv_in(0, 1)
            lnexp()
            for h in range(HEADS):
                if h:
                    act.wait_ge(num_ok, 2 * h)
                    head_norm(HEADS + h - 1, on[:, :, :])
                maxima(h)
                decay(h, 0)
                decay(h, 1)
                if h:
                    high_parts(8, h - 1)
                if h + 1 < HEADS:
                    conv_in(h + 1, 0)
                    lnexp()
                decay(h, 2)
                if h + 1 < HEADS:
                    conv_in(h + 1, 1)
                out_gates(h)
                lnexp()
                decay(h, 3)
            act.wait_ge(num_ok, 2 * HEADS)
            head_norm(2 * HEADS - 1, on[:, :, :])
            high_parts(8, HEADS - 1)
            gates(1, "tc", 16)
            lnexp()
            act.wait_ge(gemm_done, tl["tc7"].val)
            act.dma_start(hres[:, :, :], a["x"][0].rearrange("(t p) d -> p t d", p=P)).then_inc(ld_h, 16)
            act.wait_ge(gemm_done, tl["yc7"].val)
            for m in range(KT):
                act.wait_ge(mix_ok, KT + m + 1)
                nc.scalar.activation(yh[:, m, :], mix[:, m, :], ACT.Copy).then_inc(ms_ok, 1)
            act.wait_ge(ms_ok, 3 * KT)
            for n_, g_ in enumerate(["g_post_mix", "g_pre_mlp", "g_post_mlp"]):
                act.dma_start(gains[:, n_, :], a[g_].broadcast_to([P, D])).then_inc(ld_g, 16)

            def out_sums(k, base, name, stop):
                for hf in range(2):
                    act.wait_ge(gemm_done, tl[f"{name}{hf}_{stop}"].val)
                    for t in range(QT):
                        seq(nc.scalar.activation(jk[:, :], acc(name, hf, t), ACT.Square, accum_out=ssf[:, k, t, hf:hf + 1]))

            acc = accumulators
            out_sums(0, 0, "out", 3)
            nc.scalar.activation(jk[:, 0:1], eps[:, :], ACT.Copy).then_inc(out_s, 1)
            act.wait_ge(h_rs, 1)
            inv_root(ssf[:, 0, :, 0], ssf[:, 0, :, 0], D).then_inc(o_ss, 1)
            for t in range(QT):
                act.wait_ge(h_ok, t + 1)
                for hf in range(2):
                    seq(nc.scalar.activation(jk[:, :], hres[:, t, hf * SEQ:(hf + 1) * SEQ], ACT.Square, accum_out=ssf[:, 1, t, hf:hf + 1]))
            nc.scalar.activation(jk[:, 0:1], eps[:, :], ACT.Copy).then_inc(o_ss, 1)
            act.wait_ge(h_rs, 2)
            inv_root(ssf[:, 1, :, 0], ssf[:, 1, :, 0], D).then_inc(o_ss, 1)
            for f in range(KT):
                act.wait_ge(nt_ps, f + 1)
                nc.scalar.activation(nh[:, f, :], bank(f % 4), ACT.Copy).then_inc(nh_ok, 1)
            for m in range(FT):
                ps = ready(f"up{m}")
                nc.scalar.activation(U[:, m, :], ps[:, 0:SEQ], ACT.Relu).then_inc(gfree[tl[f"up{m}"].slot], 1)
            for k in range(2 * FT):
                act.wait_ge(U_ok, k % FT + 1)
                if k >= 4:
                    act.wait_ge(gemm_done, tl[f"down{(k - 4) // FT}_{(k - 4) % FT // 2}"].val)
                nc.scalar.activation(uh[:, k % 4, :], U[:, k % FT, :], ACT.Copy).then_inc(uh_ok, 1)
                if k == 2 * FT - 1:
                    break
                if k == FT + 3:
                    for t in range(QT):
                        seq(nc.scalar.activation(jk[:, :], acc("down", 0, t), ACT.Square, accum_out=ssf[:, 2, t, 0:1]))
            act.wait_ge(gemm_done, tl[f"down1_{FT // 2 - 1}"].val)
            for t in range(QT):
                seq(nc.scalar.activation(jk[:, :], acc("down", 1, t), ACT.Square, accum_out=ssf[:, 2, t, 1:2]))
            nc.scalar.activation(jk[:, 0:1], eps[:, :], ACT.Copy).then_inc(o_ss, 1)
            act.wait_ge(h_rs, 3)
            inv_root(ssf[:, 2, :, 0], ssf[:, 2, :, 0], D).then_inc(o_ss, 1)
            for t in range(QT):
                act.wait_ge(fin, t + 1)
                act.dma_start(out[0, t * P:(t + 1) * P, :], hres[:, t, :]).then_inc(out_done, 16)
            act.wait_ge(out_done, 16 * QT)

        @block.vector
        def _(dve):
            n = [0]

            def seq(ins):
                n[0] += 1
                ins.then_inc(dve_c, 1)
                dve.wait_ge(dve_c, n[0])

            def ready(name):
                t = tl[name]
                dve.wait_ge(gemm_done, t.val)
                return GP[t.slot]

            def whole(name):
                dve.wait_ge(gfree[tl[name].slot], tl[name].freed)

            tt, ts, stt = nc.vector.tensor_tensor, nc.vector.tensor_scalar, nc.vector.scalar_tensor_tensor
            nc.vector.memset(brow[:, :], 0.0).then_inc(row_zero, 1)
            nc.vector.memset(ones[:, :], 1.0)
            nc.vector.memset(eps[:, :], EPS)
            nc.vector.memset(ss[:, :], 1.0).then_inc(ss_zero, 1)
            dve.wait_ge(rs_ok, 1)
            dve.wait_ge(ld_x, 48)
            stt(Xm[:, :], Xm[:, :], ss[0:META, QT:QT + 1], gbc[0:META, :], ALU.mult, ALU.mult).then_inc(xn_ok, 1)
            for t in range(QT):
                stt(X[:, t, :], X[:, t, :], ss[:, t:t + 1], gbc[:, :], ALU.mult, ALU.mult).then_inc(xn_ok, 1)
            dve.wait_ge(col_ps, 1)
            nc.vector.tensor_copy(col[:, :], GP[0][:, 0:NROW]).then_inc(col_ok, 1)
            for f in range(KT):
                dve.wait_ge(xh_ok, f + 1)
                tt(xl[:, f, META:ALL], bank(f % 4), xh[:, f, META:ALL].bitcast(FP32), ALU.subtract).then_inc(xl_ok, 1)
            dve.wait_ge(xh_ok, KT + 1)
            tt(xl[:, :, 0:META], GP[1][:, 0:KT * META].rearrange("p (k m) -> p k m", m=META),
               xh[:, :, 0:META].bitcast(FP32), ALU.subtract).then_inc(xl_ok, 1)
            dve.wait_ge(col_ok, 1)
            dve.wait_ge(ssq_ps, 1)
            whole("ik")
            stt(two(xc), halves(PA[0]), -1.0 / P, two(ki), ALU.mult, ALU.add).then_inc(xc_ok, 1)
            dve.wait_ge(rk_ok, 1)
            dve.wait_ge(xc_ok, 1)
            seq(stt(kn[:, :], xc[:, :], cc("ig"), rk[:, :], ALU.mult, ALU.mult))
            ts(kn[:, :], kn[:, :], cc("ib"), None, ALU.add).then_inc(kn_ok, 1)
            dve.wait_ge(rq_ok, 1)
            for k in range(2):
                seq(stt(cq[:, k, :], cq[:, k, :], cc("dq", k), rq[:, :], ALU.mult, ALU.mult))
            seq(nc.vector.tensor_copy(cqh[:, :, :], cq[:, :, :]))
            tt(cql[:, :, :], cq[:, :, :], cqh[:, :, :].bitcast(FP32), ALU.subtract).then_inc(cqs_ok, 1)
            dve.wait_ge(rk_ok, 2)
            stt(kvT[:, :], ckv[:, :], cc("dkv"), rk[:, :], ALU.mult, ALU.mult).then_inc(kvT_ok, 1)
            dve.wait_ge(kvn_ok, 3)
            dve.wait_ge(masks, 2)
            for v in range(QT * IDX_H):
                i, h = v // IDX_H, v % IDX_H
                w = META + P * (i + 1)
                dve.wait_ge(sc_rl, v + 1)
                if h == 0:
                    ts(S[:, i, 0:w], rl[:, v % 2, 0:w], wi[:, i, h:h + 1], None, ALU.mult).then_inc(sc_acc, 1)
                else:
                    dve.wait_ge(sc_acc, v)
                    stt(S[:, i, 0:w], rl[:, v % 2, 0:w], wi[:, i, h:h + 1], S[:, i, 0:w], ALU.mult, ALU.add).then_inc(sc_acc, 1)
            dve.wait_ge(sc_acc, QT * IDX_H)

            def topk(i, rounds):
                w = META + P * (i + 1)
                for r in rounds:
                    if r == 0:
                        seq(tt(S[:, i, w - P:w], S[:, i, w - P:w], later_neg[:, :], ALU.add))
                    if r < TOPK // 8:
                        seq(nc.vector.max(top8[:, :], S[:, i, 0:w]))
                        seq(nc.vector.match_replace(S[:, i, 0:w], top8[:, :], S[:, i, 0:w], MARK))
                    if r == TOPK // 8:
                        seq(ts(keep[:, i, 0:w], S[:, i, 0:w], MARK / 2, BIG, ALU.is_gt, ALU.mult))
                        tt(keep[:, i, w - P:w], keep[:, i, w - P:w], later_big[:, :], ALU.max).then_inc(keep_ok, 1)

            topk(0, range(TOPK // 8 + 1))
            dve.wait_ge(table_in, 16)

            def logits(v):
                i, h = v // DSA_H, v % DSA_H
                w = META + P * (i + 1)
                dve.wait_ge(lg_ps, v + 1)
                if v >= 6:
                    dve.wait_ge(pt_ps, v // 2 - 2)
                nc.vector.tensor_tensor_reduce(out=Ls(v)[:, 0:w], in0=PA[v % 2][:, 0:w],
                                               in1=table[:, h, (QT - 1 - i) * P:(QT - 1 - i) * P + w], scale=1.0,
                                               scalar=3e38, op0=ALU.add, op1=ALU.min, accum_out=low[:, v:v + 1]).then_inc(lg_mn, 1)

            for v in range(4):
                logits(v)
            for g in range(GROUPS):
                i, gg = g // NHEADS2, g % NHEADS2
                w = META + P * (i + 1)
                for v in (2 * g, 2 * g + 1):
                    dve.wait_ge(p_exp, v + 1)
                    seq(nc.vector.reciprocal(prec[:, v:v + 1], psm[:, v:v + 1]))
                    ts(Ls(v)[:, 0:w], Ls(v)[:, 0:w], prec[:, v:v + 1], None, ALU.mult).then_inc(p_nrm, 1)
                if i + 1 < QT and gg < 6:
                    topk(i + 1, range(3 * gg, 3 * gg + 3))
                if g == 3 * NHEADS2 - 1:
                    dve.wait_ge(keep_ok, QT)
                    nc.vector.memset(uvp[:, :, :], 0.0).then_inc(uv_zero, 1)
                dve.wait_ge(pt_ps, g + 1)
                if g >= 2:
                    dve.wait_ge(pv_ps, g - 1)
                nc.vector.tensor_copy(PTm[:, g % 2, :], GP[1][0:META, (g % 2) * 2 * P:(g % 2 + 1) * 2 * P]).then_inc(pt_d, 1)
                if i >= 2:
                    nc.vector.tensor_copy(PT[:, g % 2, 2:i + 1, :],
                                          GP[0][:, SEQ:SEQ + (i - 1) * 2 * P].rearrange("p (j n) -> p j n", j=i - 1)).then_inc(pt_d, 1)
                if g + 2 < GROUPS:
                    logits(2 * g + 4)
                    logits(2 * g + 5)
            for m in range(KT):
                dve.wait_ge(yh_b, m + 1)
                tt(yl[:, m, :], PA[m % 2][:, 0:SEQ], yh[:, m, :].bitcast(FP32), ALU.subtract).then_inc(yl_b, 1)
            for m in range(KT):
                whole(f"gb{m}")
                tt(mix[:, m, :], mix[:, m, :], ready(f"yb{m}")[:, 0:SEQ], ALU.mult).then_inc(gfree[tl[f"yb{m}"].slot], 1)
            nc.vector.memset(AT[:, :, :], 0.0)
            nc.vector.memset(KL[:, :, :], 0.0)
            nc.vector.memset(KHt[:, :], 0.0).then_inc(gla_c, 1)
            dve.wait_ge(gla_c, 1)
            dve.wait_ge(ld_a, 32)

            def values(name, h, part):
                if part < 2:
                    t = tl[f"{name}{h}{'AB'[part]}"]
                    ps = ready(f"{name}{h}{'AB'[part]}")
                    tt(vh[:, h % 2, 2 * part:2 * part + 2, :], ps[:, 0:2 * DV].rearrange("p (t n) -> p t n", t=2),
                       vb[:, h * DV:(h + 1) * DV].unsqueeze(1).broadcast_to([P, 2, DV]), ALU.add).then_inc(gfree[t.slot], 1)
                    return
                ps = ready(f"{name}{h}M")
                tt(vm[:, h % 2, :], ps[0:META, 0:DV], vb[0:META, h * DV:(h + 1) * DV], ALU.add).then_inc(gfree[tl[f"{name}{h}M"].slot], 1)

            def q_in(h):
                ts(qh[:, h % 2, :], ready(f"gq{h}")[:, 0:SEQ], cc("gq", h), DK ** -0.5, ALU.add, ALU.mult).then_inc(gfree[tl[f"gq{h}"].slot], 1)

            def k_in(h):
                ts(two(kh[:, h % 2, :]), halves(ready(f"gk{h}")), cc("gk", h), None, ALU.add).then_inc(gfree[tl[f"gk{h}"].slot], 1)

            def forget(h):
                ps = ready(f"gg{h}")
                g0 = G[:, h % 2, :]
                dve.wait_ge(gg_l, h + 1)
                ts(two(g0), halves(ps), cc("a2", h), 0.0, ALU.add, ALU.min).then_inc(gfree[tl[f"gg{h}"].slot], 1)
                whole(f"gg{h}")
                seq(tt(gch[:, :], g0, gch[:, :], ALU.subtract))
                nc.vector.tensor_tensor_scan(g0[:, 0:META], ones[:, 0:META], gch[:, 0:META], 0.0, ALU.mult, ALU.add)
                for i in range(QT):
                    s0 = slice(META + i * P, META + (i + 1) * P)
                    ins = nc.vector.tensor_tensor_scan(g0[:, s0], ones[:, :], gch[:, s0], 0.0, ALU.mult, ALU.add)
                ins.then_inc(G_ok, 1)

            def parts(t, B):
                v = t.rearrange("p (n two b) -> p n two b", two=2, b=B)
                return v[:, :, 0, :], v[:, :, 1, :]

            def lv_write(h, l):
                B = LEVELS[l]
                lo_, up = parts(G[:, h % 2, META:ALL], B)
                N = SEQ // (2 * B)
                mid = lo_[:, :, B - 1:B].broadcast_to([P, N, B])
                k = len(LEVELS) * h + l
                if k:
                    dve.wait_ge(lv_qk, k)
                dve.wait_ge(G_ok, h + 1)
                tt(E[:, 0:SEQ // 2].rearrange("p (n b) -> p n b", b=B), up, mid, ALU.subtract)
                tt(E[:, SEQ // 2:SEQ].rearrange("p (n b) -> p n b", b=B), mid, lo_, ALU.subtract).then_inc(lv_w, 1)

            def lv_mul(h, l):
                B = LEVELS[l]
                k = len(LEVELS) * h + l
                dve.wait_ge(lv_e, k + 1)
                if k >= 2:
                    dve.wait_ge(lv_ps, 8 * ((k - 2) // 7) + (k - 2) % 7 + 1)
                _, uq = parts(qh[:, h % 2, :], B)
                lk, _ = parts(kh[:, h % 2, META:ALL], B)
                lo_, _ = parts(KL[:, k % 2, :], B)
                tt(QL[:, k % 2, :].rearrange("p (n b) -> p n b", b=B), uq, E[:, 0:SEQ // 2].rearrange("p (n b) -> p n b", b=B), ALU.mult)
                if k:
                    dve.wait_ge(lv_qk, k)
                tt(lo_, lk, E[:, SEQ // 2:SEQ].rearrange("p (n b) -> p n b", b=B), ALU.mult).then_inc(lv_qk, 1)

            def lv_select(h, l):
                k = 8 * h + l
                dve.wait_ge(lv_ps, k + 1)
                if k == 8 * h and h:
                    dve.wait_ge(av_ps, h)
                if k:
                    dve.wait_ge(lv_sel, k)
                if l < len(LEVELS):
                    B = LEVELS[l]
                    o_ = AT[:, :, 0:P].rearrange("p t (n two b) -> p t n two b", two=2, b=B)[:, :, :, 1, :]
                    m_ = lm[:, l, :].rearrange("p (n b) -> p n b", b=B).unsqueeze(1).broadcast_to([P, QT, 64 // B, B])
                    d_ = bank(k % 4)[:, 0:QT * 64].rearrange("p (t n b) -> p t n b", t=QT, b=B)
                    nc.vector.copy_predicated(o_, m_.bitcast(U32), d_).then_inc(lv_sel, 1)
                else:
                    m_ = ident[:, :].unsqueeze(1).broadcast_to([P, QT, P])
                    nc.vector.copy_predicated(AT[:, :, 0:P], m_.bitcast(U32),
                                              bank(k % 4).rearrange("p (t n) -> p t n", t=QT)).then_inc(lv_sel, 1)

            def off(h):
                dve.wait_ge(od_e, 6 * h + 6)
                seq(tt(KHt[:, :], KHt[:, :], kh[:, h % 2, 0:ALL - P], ALU.mult))
                tt(QQ[:, :], QQ[:, :], qh[:, h % 2, :], ALU.mult).then_inc(od_q, 1)
                for q, j in enumerate([2, 1, 0]):
                    dve.wait_ge(od_ps, 4 * h + q + 1)
                    dve.wait_ge(od_q, 4 * h + q + 1)
                    ts(QQ[:, (j + 1) * P:SEQ], QQ[:, (j + 1) * P:SEQ], gf[:, j + 1:j + 2], None, ALU.mult).then_inc(od_q, 1)

            def scaled(k, gname, src):
                dve.wait_ge(av_rs, k + 1)
                for v in range(2):
                    stt(on[:, v, :], src(v), cc(gname, v), rso[:, :], ALU.mult, ALU.mult).then_inc(on_ok, 1)

            def silus(h):
                for v in range(2):
                    m = 2 * h + v
                    dve.wait_ge(sg_ok, m + 1)
                    stt(sgate[:, v, :], ready(f"gr{m}")[:, 0:SEQ], cc("gr", m), sgate[:, v, :], ALU.add, ALU.mult).then_inc(gfree[tl[f"gr{m}"].slot], 1)

            def branch_out(base, h):
                dve.wait_ge(on_ok, base + 2 * h + 2)
                for v in range(2):
                    whole(f"{'gm'[base // 8]}{'ro'[base // 8]}{2 * h + v}")
                    tt(on[:, v, :], on[:, v, :], sgate[:, v, :], ALU.mult).then_inc(y_ok, 1)

            def low_parts(base, h):
                for v in range(2):
                    m = 2 * h + v
                    dve.wait_ge(ms_ok, base + m + 1)
                    tt(yl[:, m, :], on[:, v, :], yh[:, m, :].bitcast(FP32), ALU.subtract).then_inc(yl_b, 1)

            def finish(h):
                if h:
                    dve.wait_ge(ms_ok, 2 * h)
                    dve.wait_ge(yl_b, KT + 2 * h)
                scaled(h, "hg", lambda v: bank(v))
                branch_out(0, h)

            q_in(0)
            k_in(0)
            forget(0)
            for part in range(3):
                values("gv", 0, part)
            for h in range(HEADS):
                more = h + 1 < HEADS
                lv_write(h, 0)
                if more:
                    q_in(h + 1)
                lv_mul(h, 0)
                if h:
                    finish(h - 1)
                lv_write(h, 1)
                if more:
                    k_in(h + 1)
                lv_mul(h, 1)
                lv_write(h, 2)
                lv_select(h, 0)
                lv_select(h, 1)
                if more:
                    forget(h + 1)
                lv_mul(h, 2)
                lv_write(h, 3)
                if h:
                    low_parts(0, h - 1)
                silus(h)
                lv_mul(h, 3)
                lv_write(h, 4)
                lv_select(h, 2)
                lv_mul(h, 4)
                lv_write(h, 5)
                lv_select(h, 3)
                lv_mul(h, 5)
                lv_write(h, 6)
                lv_select(h, 4)
                if more:
                    values("gv", h + 1, 0)
                lv_mul(h, 6)
                lv_select(h, 5)
                lv_select(h, 6)
                lv_select(h, 7)
                off(h)
                if more:
                    values("gv", h + 1, 1)
                    values("gv", h + 1, 2)
            finish(HEADS - 1)
            low_parts(0, HEADS - 1)

            def mixing(branch, gate, name):
                for m in range(KT):
                    k = 8 * branch + m
                    dve.wait_ge(gfree[tl[f"{gate}{m}"].slot], tl[f"{gate}{m}"].freed)
                    if k >= 2:
                        dve.wait_ge(mix_ok, k - 1)
                    tt(gtmp[:, m % 2, :], ready(f"{name}{m}")[:, 0:SEQ], sgate[:, m % 2, :], ALU.mult).then_inc(gfree[tl[f"{name}{m}"].slot], 1)
                    whole(f"{name}{m}")
                    tt(mix[:, m, :], mix[:, m, :], gtmp[:, m % 2, :], ALU.add).then_inc(mix_ok, 1)

            mixing(0, "ta", "ya")
            nc.vector.memset(zc[:, 0:3], 0.0).then_inc(zpad, 1)
            dve.wait_ge(mix_ok, KT)
            nc.vector.memset(M_[GR, :], 1.0).then_inc(M_one, 1)
            nc.vector.tensor_copy(bcum, small[96:96 + HEADS, :]).then_inc(ms_d, 1)
            dve.wait_ge(ms_d, 1)
            seq(ts(bcum, bcum, col[GR, ROWS["fb"]:ROWS["fb"] + 1], None, ALU.add))
            nc.vector.memset(fbias, 0.0).then_inc(ms_d, 1)
            dve.wait_ge(fl_ok, 1)
            seq(ts(bcum, bcum, 0.0, None, ALU.min))
            seq(tt(lf, bcum, lf, ALU.subtract))
            dve.wait_ge(M_one, 1)
            seq(nc.vector.tensor_tensor_scan(bcum, M, lf, 0.0, ALU.mult, ALU.add))
            tt(u, u, bcum, ALU.subtract).then_inc(u_ok, 1)
            dve.wait_ge(u_ok, 1)
            seq(nc.vector.tensor_tensor_scan(M, u, u, 0.0, ALU.max, ALU.max))
            stt(bcum, bcum, -1.0, M, ALU.mult, ALU.subtract).then_inc(M_ok, 1)
            dve.wait_ge(uT_ps, 1)
            nc.vector.tensor_copy(uT[:, :, :], bank(0)[:, 0:QT * HEADS].rearrange("p (t h) -> p t h", h=HEADS)).then_inc(uT_ok, 1)
            nc.vector.tensor_copy(uTm[:, :], bank(0)[0:META, QT * HEADS:(QT + 1) * HEADS]).then_inc(uT_ok, 1)
            dve.wait_ge(ld_v, 16)

            def conv(h, q):
                k = 2 * h + q
                dve.wait_ge(zpad, 1)
                whole(f"m{'qk'[q]}{h}")
                if k:
                    dve.wait_ge(qk_ok, k)
                w = lambda tap: cc("cv", tap * 8 + q * 4 + h)
                seq(ts(cv[:, :], zc[:, 0:ALL], w(0), None, ALU.mult))
                for tap in range(1, 4):
                    ins = stt(cv[:, :], zc[:, tap:tap + ALL], w(tap), cv[:, :], ALU.mult, ALU.add)
                    if tap < 3:
                        seq(ins)
                ins.then_inc(cv_ok, 1)
                dve.wait_ge(cs_ok, k + 1)
                dve.wait_ge(cv_ok, k + 1)
                if q == 0:
                    stt(qh[:, h % 2, :], cv[:, META:ALL], DK ** -0.5, sgc[:, META:ALL], ALU.mult, ALU.mult).then_inc(qk_ok, 1)
                else:
                    tt(kh[:, h % 2, :], cv[:, :], sgc[:, :], ALU.mult).then_inc(qk_ok, 1)

            def masked(h):
                dve.wait_ge(mb_ok, h + 1)
                tt(Md[:, :].rearrange("p (t n) -> p t n", t=QT), Mb[:, :].rearrange("p (t n) -> p t n", t=QT),
                   later_bigT[:, :].unsqueeze(1).broadcast_to([P, QT, P]), ALU.add).then_inc(md_ok, 1)

            def weights_of(h, q):
                dve.wait_ge(s_ps, 5 * h + q + 1)
                if h and q == 0:
                    dve.wait_ge(av_ps, HEADS + h)
                b = bank((2 + q) % 4)
                if q == 0:
                    dve.wait_ge(w_ok, 8 * h + 1)
                    tt(ATm[:, :], b[0:META, :], Wm[:, :], ALU.mult).then_inc(at_ok, 1)
                else:
                    j = q - 1
                    dve.wait_ge(w_ok, 8 * h + min(2 * q + 1, 8))
                    tt(AT[:, j, 0:SEQ - j * P], b[:, 0:SEQ - j * P], Wd[:, 0:SEQ - j * P], ALU.mult).then_inc(at_ok, 1)

            def divide(h):
                dve.wait_ge(av_ps, HEADS + h + 1)
                dve.wait_ge(em_ok, h + 1)
                if h:
                    dve.wait_ge(ms_ok, 8 + 2 * h)
                    dve.wait_ge(yl_b, 2 * KT + 2 * h)
                seq(tt(gtmp[:, 0, :], bank(3), emn[:, :], ALU.max))
                seq(stt(gtmp[:, 0, :], bank(3), -1.0, gtmp[:, 0, :], ALU.mult, ALU.max))
                seq(nc.vector.reciprocal(gtmp[:, 1, :], gtmp[:, 0, :]))
                for v in range(2):
                    tt(on[:, v, :], bank(v), gtmp[:, 1, :], ALU.mult).then_inc(num_ok, 1)

            def finish(h):
                dve.wait_ge(num_ok, 2 * h + 2)
                scaled(HEADS + h, "hm", lambda v: on[:, v, :])
                branch_out(8, h)

            conv(0, 0)
            conv(0, 1)
            for part in range(3):
                values("mv", 0, part)
            for h in range(HEADS):
                more = h + 1 < HEADS
                if h:
                    finish(h - 1)
                masked(h)
                for q in range(3):
                    weights_of(h, q)
                if h:
                    low_parts(8, h - 1)
                if more:
                    conv(h + 1, 0)
                weights_of(h, 3)
                if more:
                    conv(h + 1, 1)
                weights_of(h, 4)
                if more:
                    values("mv", h + 1, 0)
                divide(h)
                if more:
                    values("mv", h + 1, 1)
                    values("mv", h + 1, 2)
            finish(HEADS - 1)
            low_parts(8, HEADS - 1)
            mixing(1, "tc", "yc")
            for m in range(KT):
                dve.wait_ge(ms_ok, 16 + m + 1)
                tt(yl[:, m, :], mix[:, m, :], yh[:, m, :].bitcast(FP32), ALU.subtract).then_inc(yl_b, 1)
            dve.wait_ge(out_s, 1)
            tt(ssf[:, 0, :, 0], ssf[:, 0, :, 0], ssf[:, 0, :, 1], ALU.add).then_inc(h_rs, 1)
            dve.wait_ge(o_ss, 1)
            dve.wait_ge(ld_h, 16)
            dve.wait_ge(ld_g, 48)
            for t in range(QT):
                for hf in range(2):
                    seq(stt(xn[:, t, hf * SEQ:(hf + 1) * SEQ], accumulators("out", hf, t), ssf[:, 0, t, 0:1],
                            gains[:, 0, hf * SEQ:(hf + 1) * SEQ], ALU.mult, ALU.mult))
                tt(hres[:, t, :], hres[:, t, :], xn[:, t, :], ALU.add).then_inc(h_ok, 1)
            dve.wait_ge(o_ss, 2)
            tt(ssf[:, 1, :, 0], ssf[:, 1, :, 0], ssf[:, 1, :, 1], ALU.add).then_inc(h_rs, 1)
            dve.wait_ge(o_ss, 3)
            dve.wait_ge(h_ok, QT)
            for t in range(QT):
                stt(xn[:, t, :], hres[:, t, :], ssf[:, 1, t, 0:1], gains[:, 1, :], ALU.mult, ALU.mult).then_inc(n_ok, 1)
            for f in range(KT):
                dve.wait_ge(nh_ok, f + 1)
                tt(nl[:, f, :], bank(f % 4), nh[:, f, :].bitcast(FP32), ALU.subtract).then_inc(nl_ok, 1)
            for m in range(FT):
                whole(f"up{m}")
                tt(U[:, m, :], U[:, m, :], U[:, m, :], ALU.mult).then_inc(U_ok, 1)
            for k in range(2 * FT):
                dve.wait_ge(U_ok, k % FT + 1)
                dve.wait_ge(uh_ok, k + 1)
                tt(ul[:, k % 4, :], U[:, k % FT, :], uh[:, k % 4, :].bitcast(FP32), ALU.subtract).then_inc(ul_ok, 1)
            dve.wait_ge(o_ss, 4)
            tt(ssf[:, 2, :, 0], ssf[:, 2, :, 0], ssf[:, 2, :, 1], ALU.add).then_inc(h_rs, 1)
            dve.wait_ge(o_ss, 5)
            for t in range(QT):
                for hf in range(2):
                    seq(stt(xn[:, t, hf * SEQ:(hf + 1) * SEQ], accumulators("down", hf, t), ssf[:, 2, t, 0:1],
                            gains[:, 2, hf * SEQ:(hf + 1) * SEQ], ALU.mult, ALU.mult))
                tt(hres[:, t, :], hres[:, t, :], xn[:, t, :], ALU.add).then_inc(fin, 1)

        @block.tensor
        def _(pe):
            mm = nc.tensor.matmul

            def rhs(kind, k):
                if kind == "x":
                    return xh[:, k, META:ALL], xl[:, k, META:ALL]
                h_, l_ = {"cq": (cqh, cql), "y": (yh, yl), "n": (nh, nl)}[kind]
                return h_[:, k, :], l_[:, k, :]

            def gemm(name):
                t = tl[name]
                if t.need:
                    pe.wait_ge(gfree[t.slot], t.need)
                for c in t.chunks:
                    pe.wait_ge(split_done, chunks[c]["r"] + 1)
                ps = GP[t.slot]
                if t.kind == "F":
                    s0 = chunks[t.chunks[0]]["hl"]
                    for k in range(t.kt):
                        w = slice(k * t.width + t.off, k * t.width + t.off + t.m)
                        ah, al = rhs(t.rhs, k)
                        for p_, (wt, av, hx) in enumerate([(whi, ah, xh), (whi, al, xl), (wlo, ah, xh)]):
                            st, sp_ = (k == 0 and p_ == 0), (k == t.kt - 1 and p_ == 2)
                            if t.both:
                                for b in range(2):
                                    ins = mm(ps[0:t.m, b * SEQ:b * SEQ + HALF], wt[:, s0, w],
                                             hx[:, k, b * HALF:(b + 1) * HALF], start=st, stop=sp_)
                            else:
                                ins = mm(ps[0:t.m, 0:SEQ], wt[:, s0, w], av, start=st, stop=sp_)
                elif t.kind in ("V", "VM"):
                    s0 = chunks[t.chunks[0]]["hl"]
                    for i in range(2 if t.kind == "V" else 1):
                        tok = slice(META + (t.off + i) * P, META + (t.off + i + 1) * P) if t.kind == "V" else slice(0, META)
                        o_ = ps[:, i * DV:(i + 1) * DV] if t.kind == "V" else ps[0:META, 0:DV]
                        for k in range(KT):
                            for p_, (at_, wt) in enumerate([(xh, whi), (xh, wlo), (xl, whi)]):
                                ins = mm(o_, at_[:, k, tok], wt[:, s0:s0 + 2, k * P:(k + 1) * P],
                                         start=(k == 0 and p_ == 0), stop=(k == KT - 1 and p_ == 2))
                else:
                    h = int(name[2:])
                    for b in range(2):
                        ins = mm(ps[:, b * SEQ:b * SEQ + HALF], a2[32:32 + META, h * DK:(h + 1) * DK],
                                 small[32:32 + META, b * HALF:(b + 1) * HALF],
                                 start=True, stop=True)
                ins.then_inc(gemm_done, 1)

            def token_gemm(name, n, hf, last, parts):
                t = tl[f"{name}{hf}_{n}"]
                c = chunks[t.chunks[0]]
                pe.wait_ge(split_done, c["r"] + 1)
                for k in range(2):
                    ah, al = parts(k)
                    for i in range(QT):
                        for p_, (av, wt) in enumerate([(ah, whi), (ah, wlo), (al, whi)]):
                            ins = mm(accumulators(name, hf, i), av[:, i * P:(i + 1) * P], wt[:, c["hl"], k * SEQ:(k + 1) * SEQ],
                                     start=(n == 0 and k == 0 and p_ == 0), stop=(last and k == 1 and p_ == 2))
                ins.then_inc(gemm_done, 1)

            pe.wait_ge(masks, 1)
            pe.wait_ge(pool_c, 7 + len(LEVELS))
            pe.wait_ge(ld_rows, 16 * NROWDMA)
            nc.tensor.transpose(GP[0][:, 0:NROW], brow[:, :], ident[0:NROW, 0:NROW]).then_inc(col_ps, 1)
            pe.wait_ge(xn_ok, QT + 1)
            for f in range(KT):
                if f >= 4:
                    pe.wait_ge(xl_ok, f - 3)
                for t in range(QT):
                    ins = nc.tensor.transpose(bank(f % 4)[:, t * P:(t + 1) * P], X[:, t, f * P:(f + 1) * P], ident[:, :])
                ins.then_inc(xt_ps, 1)
            for f in range(KT):
                ins = nc.tensor.transpose(GP[1][:, f * META:(f + 1) * META], Xm[:, f * P:(f + 1) * P], ident[0:META, 0:META])
            ins.then_inc(xt_ps, 1)
            pe.wait_ge(ld_line, 32)
            pe.wait_ge(col_ok, 1)
            for c0, c1 in ((0, SEQ), (SEQ, LINE)):
                ins = mm(GP[0][0:DSA_H, c0:c1], t5[:, :], oh[:, c0:c1], start=True, stop=True)
            ins.then_inc(line_ps, 1)
            pe.wait_ge(xl_ok, KT + 1)
            pe.wait_ge(line_ok, 1)

            def summed(ps, src):
                for b in range(2):
                    ins = mm(ps[:, b * SEQ:b * SEQ + HALF], ones[:, :], src[:, b * HALF:(b + 1) * HALF], start=True, stop=True)
                ins.then_inc(ssq_ps, 1)

            def evacuated(*names):
                for nm in names:
                    pe.wait_ge(gfree[tl[nm].slot], tl[nm].freed)

            gemm("ik")
            gemm("small")
            evacuated("ik")
            summed(PA[0], ki)
            gemm("cq0")
            pe.wait_ge(xcsq, 1)
            summed(PA[1], sqk)
            gemm("cq1")
            gemm("ckv")
            pe.wait_ge(cqsq, 1)
            pe.wait_ge(xc_ok, 1)
            for k in range(2):
                ins = mm(PA[0][:, 0:SEQ], ones[:, :], sq[:, k, :], start=(k == 0), stop=(k == 1))
            ins.then_inc(ssq_ps, 1)
            gemm("gb0")
            pe.wait_ge(kvsq, 1)
            pe.wait_ge(rk_ok, 1)
            summed(PA[1], sqk)
            gemm("gb1")
            pe.wait_ge(kvT_ok, 1)
            pe.wait_ge(rq_ok, 1)
            evacuated("small")
            for t in range(QT):
                nc.tensor.transpose(PA[0][:, t * P:(t + 1) * P], kvT[:, META + t * P:META + (t + 1) * P], ident[:, :])
                nc.tensor.transpose(PA[0][:, WIO + t * IDX_H:WIO + (t + 1) * IDX_H],
                                    small[0:IDX_H, META + t * P:META + (t + 1) * P], ident[0:IDX_H, 0:IDX_H])
            nc.tensor.transpose(PA[0][0:META, QT * P:(QT + 1) * P], kvT[:, 0:META], ident[:, :]).then_inc(kvn_ps, 1)
            pe.wait_ge(cqs_ok, 1)
            for m in range(4):
                gemm(f"iq{m}")
            pe.wait_ge(kn_ok, 1)
            pe.wait_ge(kvn_ok, 3)
            pe.wait_ge(rk_ok, 2)
            for m in range(4):
                evacuated(f"iq{m}")
            for v in range(QT * IDX_H):
                i, h = v // IDX_H, v % IDX_H
                w = META + P * (i + 1)
                if v >= 2:
                    pe.wait_ge(sc_rl, v - 1)
                r = slice(64 * (h % 2), 64 * (h % 2) + 64)
                for c0 in range(0, w, SEQ):
                    ins = mm(PA[v % 2][:, c0:min(c0 + SEQ, w)], qi[r, h // 2, i * P:(i + 1) * P], kn[r, c0:min(c0 + SEQ, w)],
                             start=True, stop=True)
                ins.then_inc(sc_ps, 1)
                if h == IDX_H - 1:
                    gemm(f"gb{2 + i}")
            for h in range(DSA_H):
                gemm(f"uq{h}")
            gemm("gb6")
            gemm("gb7")
            evacuated("uq14", "uq15", "gb6", "gb7")
            pe.wait_ge(sc_rl, QT * IDX_H)

            def logits(v):
                i, h = v // DSA_H, v % DSA_H
                w = META + P * (i + 1)
                pe.wait_ge(keep_ok, i + 1)
                if v >= 2:
                    pe.wait_ge(lg_mn, v - 1)
                for c0 in range(0, w, SEQ):
                    c = slice(c0, min(c0 + SEQ, w))
                    mm(PA[v % 2][:, c], qlat[:, h, i * P:(i + 1) * P], kvT[:, c], start=True, stop=False)
                    ins = mm(PA[v % 2][:, c], identb[:, :], keep[:, i, c], start=False, stop=True)
                ins.then_inc(lg_ps, 1)

            for v in range(4):
                logits(v)
            for g in range(GROUPS):
                i = g // NHEADS2
                pe.wait_ge(p_nrm, 2 * g + 2)
                if g:
                    pe.wait_ge(pt_a, g)
                    pe.wait_ge(pt_d, pt_d_after(g - 1))
                for s_ in range(2):
                    v = 2 * g + s_
                    for j in range(i + 1):
                        nc.tensor.transpose(GP[0][:, (2 * j + s_) * P:(2 * j + s_ + 1) * P],
                                            Ls(v)[:, META + j * P:META + (j + 1) * P], ident[:, :])
                    ins = nc.tensor.transpose(GP[1][0:META, (g % 2 * 2 + s_) * P:(g % 2 * 2 + s_ + 1) * P], Ls(v)[:, 0:META], ident[:, :])
                ins.then_inc(pt_ps, 1)
                if g + 2 < GROUPS:
                    logits(2 * g + 4)
                    logits(2 * g + 5)
                pe.wait_ge(pt_a, g + 1)
                pe.wait_ge(pt_d, pt_d_after(g))
                if g >= 2:
                    pe.wait_ge(ol_ev, g - 1)
                o_ = GP[1][:, SEQ + (g % 2) * 2 * P:SEQ + (g % 2 + 1) * 2 * P]
                mm(o_, kvm[:, :], PTm[:, g % 2, :], start=True, stop=False)
                for j in range(i + 1):
                    ins = mm(o_, kvn[:, j, :], PT[:, g % 2, j, :], start=False, stop=(j == i))
                ins.then_inc(pv_ps, 1)
            pe.wait_ge(ld_uv, 32)
            pe.wait_ge(ol_ev, GROUPS)
            for m in range(KT):
                if m >= 2:
                    pe.wait_ge(yl_b, m - 1)
                for s_ in range(2):
                    ins = mm(PA[m % 2][:, 0:SEQ], uvp[:, 2 * m + s_, :], qlat[:, 2 * m + s_, :], start=(s_ == 0), stop=(s_ == 1))
                ins.then_inc(uv_ps, 1)
            pe.wait_ge(yl_b, KT)
            for m in range(KT):
                gemm(f"yb{m}")
            pe.wait_ge(ld_a, 32)

            def level(h, l):
                k = 8 * h + l
                if l < len(LEVELS):
                    pe.wait_ge(lv_qk, 7 * h + l + 1)
                if k >= 4:
                    pe.wait_ge(lv_sel, k - 3)
                if h and l == 0:
                    pe.wait_ge(on_ok, 2 * h)
                    pe.wait_ge(av_rs, h)
                for i in range(QT):
                    if l < len(LEVELS):
                        b = (7 * h + l) % 2
                        ins = mm(bank(k % 4)[:, i * 64:(i + 1) * 64], KL[:, b, i * P:(i + 1) * P], QL[:, b, i * 64:(i + 1) * 64],
                                 start=True, stop=True)
                    else:
                        ins = mm(bank(k % 4)[:, i * P:(i + 1) * P], kh[:, h % 2, META + i * P:META + (i + 1) * P],
                                 qh[:, h % 2, i * P:(i + 1) * P], start=True, stop=True)
                ins.then_inc(lv_ps, 1)

            def weighted(k, h):
                for v in range(2):
                    c = slice(v * P, (v + 1) * P)
                    mm(bank(v), vm[:, h % 2, c], ATm[:, :], start=True, stop=False)
                    for j in range(QT):
                        ins = mm(bank(v)[:, j * P:SEQ], vh[:, h % 2, j, c], AT[:, j, 0:SEQ - j * P], start=False, stop=(j == QT - 1))
                return ins

            def squares(k):
                pe.wait_ge(av_sq, k + 1)
                for v in range(2):
                    ins = mm(bank(2), ones[:, :], sqo[:, v, :], start=(v == 0), stop=(v == 1))
                ins.then_inc(av_ss, 1)

            for nm in ("gq0", "gk0", "gg0", "gv0A", "gv0B", "gv0M"):
                gemm(nm)
            for h in range(HEADS):
                def nxt(*kinds):
                    if h + 1 < HEADS:
                        for kind in kinds:
                            gemm(f"{kind[0:2]}{h + 1}{kind[2:]}")

                evacuated(f"gq{h}", f"gk{h}", f"gv{h}A", f"gv{h}B", f"gv{h}M")
                nxt("gq")
                if h:
                    squares(h - 1)
                nxt("gk")
                level(h, 0)
                level(h, 1)
                nxt("gg")
                gemm(f"gr{2 * h}")
                level(h, 2)
                gemm(f"gr{2 * h + 1}")
                level(h, 3)
                level(h, 4)
                nxt("gvA")
                for l in range(5, 8):
                    level(h, l)
                nxt("gvB")
                pe.wait_ge(lv_sel, 8 * h + 8)
                for q, j in enumerate([2, 1, 0]):
                    pe.wait_ge(od_q, 4 * h + q + 1)
                    mm(bank(q)[:, 0:SEQ - (j + 1) * P], KHt[:, META + j * P:META + (j + 1) * P], QQ[:, (j + 1) * P:SEQ],
                       start=True, stop=True).then_inc(od_ps, 1)
                pe.wait_ge(od_q, 4 * h + 4)
                mm(bank(3)[0:META, :], KHt[:, 0:META], QQ[:, :], start=True, stop=True).then_inc(od_ps, 1)
                nxt("gvM")
                pe.wait_ge(od_ev, 4 * h + 4)
                weighted(h, h).then_inc(av_ps, 1)
            squares(HEADS - 1)
            pe.wait_ge(yl_b, 2 * KT)
            for m in range(KT):
                gemm(f"ta{m}")
                gemm(f"ya{m}")
            gemm("mq0")
            gemm("mk0")
            pe.wait_ge(u_ok, 1)
            idg = ident[GR, GR]
            for t in range(QT):
                nc.tensor.transpose(bank(0)[:, t * HEADS:(t + 1) * HEADS], u[:, META + t * P:META + (t + 1) * P], idg)
            nc.tensor.transpose(bank(0)[0:META, QT * HEADS:(QT + 1) * HEADS], u[:, 0:META], idg).then_inc(uT_ps, 1)
            for nm in ("mv0A", "mv0B", "mv0M"):
                gemm(nm)
            pe.wait_ge(M_ok, 1)
            pe.wait_ge(uT_ok, 2)

            def scores(h, q):
                if q == 2:
                    pe.wait_ge(mb_ok, h + 1)
                if q == 3:
                    pe.wait_ge(em_ok, h + 1)
                if q == 4:
                    pe.wait_ge(at_ok, 5 * h + 1)
                b = bank((2 + q) % 4)
                if q == 0:
                    ins = mm(b[0:META, :], kh[:, h % 2, 0:META], qh[:, h % 2, :], start=True, stop=True)
                else:
                    j = q - 1
                    ins = mm(b[:, 0:SEQ - j * P], kh[:, h % 2, META + j * P:META + (j + 1) * P], qh[:, h % 2, j * P:SEQ],
                             start=True, stop=True)
                ins.then_inc(s_ps, 1)

            for h in range(HEADS):
                def nxt(*kinds):
                    if h + 1 < HEADS:
                        for kind in kinds:
                            gemm(f"{kind[0:2]}{h + 1}{kind[2:]}")

                evacuated(f"mv{h}A", f"mv{h}B", f"mv{h}M")
                pe.wait_ge(qk_ok, 2 * h + 2)
                if h:
                    pe.wait_ge(num_ok, 2 * h)
                for src in (M, bcum):
                    mm(bank(0 if src is M else 1), ident[GR, 64 + h:65 + h].broadcast_to([HEADS, P]), src[:, META:ALL],
                       start=True, stop=True).then_inc(mb_ps, 1)
                if h:
                    squares(HEADS + h - 1)
                    pe.wait_ge(av_rs, HEADS + h)
                nxt("mq")
                scores(h, 0)
                scores(h, 1)
                scores(h, 2)
                nxt("mk")
                scores(h, 3)
                gemm(f"mo{2 * h}")
                scores(h, 4)
                gemm(f"mo{2 * h + 1}")
                pe.wait_ge(at_ok, 5 * h + 5)
                weighted(HEADS + h, h)
                mm(bank(3), ones[0:META, :], ATm[:, :], start=True, stop=False)
                for j in range(QT):
                    ins = mm(bank(3)[:, j * P:SEQ], ones[:, :], AT[:, j, 0:SEQ - j * P], start=False, stop=(j == QT - 1))
                ins.then_inc(av_ps, 1)
                nxt("mvA", "mvB", "mvM")
            squares(2 * HEADS - 1)
            pe.wait_ge(yl_b, 3 * KT)
            for m in range(KT):
                gemm(f"tc{m}")
                gemm(f"yc{m}")
            evacuated("yc6", "yc7", "tc6", "tc7")
            pe.wait_ge(yl_b, 4 * KT)
            for hf in range(2):
                for n_ in range(4):
                    token_gemm("out", n_, hf, n_ == 3, lambda k: (yh[:, 2 * n_ + k, :], yl[:, 2 * n_ + k, :]))
            for f in range(KT):
                pe.wait_ge(n_ok, QT)
                if f >= 4:
                    pe.wait_ge(nl_ok, f - 3)
                for t in range(QT):
                    ins = nc.tensor.transpose(bank(f % 4)[:, t * P:(t + 1) * P], xn[:, t, f * P:(f + 1) * P], ident[:, :])
                ins.then_inc(nt_ps, 1)
            pe.wait_ge(nl_ok, KT)
            for m in range(FT):
                gemm(f"up{m}")
            for hf in range(2):
                if hf:
                    evacuated(f"up{FT - 1}", f"up{FT - 2}")
                for n_ in range(FT // 2):
                    pe.wait_ge(ul_ok, hf * FT + 2 * n_ + 2)
                    token_gemm("down", n_, hf, n_ == FT // 2 - 1,
                               lambda k: (uh[:, (2 * n_ + k) % 4, :], ul[:, (2 * n_ + k) % 4, :]))


_INS = ["x", "meta_tokens", "t5_bias", "g_pre_mix", "w_in", "b_in", "w_gla_a2", "b_gla_a", "g_gla_head", "w_br_gla",
        "g_dsa_q", "w_dsa_uq", "w_idx_q", "g_dsa_kv", "w_dsa_uv", "idx_ln_g", "idx_ln_b", "w_br_dsa", "ml_conv",
        "ml_f_bias", "g_ml_head", "w_br_ml", "w_out", "g_post_mix", "g_pre_mlp", "w_up", "w_down", "g_post_mlp"]


def bucket_onehot():
    import numpy as np
    import math
    n = np.maximum(LINE - 1 - (P - 1) - np.arange(LINE), 0)
    nf = np.maximum(n, 1).astype(np.float32)
    half = BUCKETS // 2
    large = half + (np.log(nf / np.float32(half)) / np.float32(math.log(128 / half)) * np.float32(half)).astype(np.int32)
    b = np.where(n < half, n, np.minimum(large, BUCKETS - 1))
    return (np.arange(BUCKETS)[:, None] == b[None, :]).astype(np.float32)


def kernel(**inputs):
    import numpy as _np
    import concourse.bacc as _bacc
    from concourse.bass_utils import run_bass_kernel_spmd as _run

    nc = _bacc.Bacc("TRN2", target_bir_lowering=False, num_devices=1)
    arrays, aps = {}, {}
    for name in _INS:
        v = _np.ascontiguousarray(inputs[name])
        arrays[f"in_{name}"] = v
        aps[name] = nc.dram_tensor(f"in_{name}", v.shape, FP32, kind="ExternalInput").ap()
    v = bucket_onehot()
    arrays["in_onehot"] = v
    aps["onehot"] = nc.dram_tensor("in_onehot", v.shape, FP32, kind="ExternalInput").ap()
    line = nc.dram_tensor("bias_line", (DSA_H, LINE), FP32).ap()
    scratch = nc.dram_tensor("line_rows", (P, DSA_H, LPITCH), FP32).ap()
    out = nc.dram_tensor("out_h", (1, SEQ, D), FP32, kind="ExternalOutput").ap()
    build(nc, aps, line, scratch, out)
    r = _run(nc, [arrays], core_ids=[0])
    return r.results[0]["out_h"]
```

```python
import concourse.bass as bass
from concourse import mybir
from contextlib import ExitStack

FP32 = mybir.dt.float32
F32R = mybir.dt.float32r
BF16 = mybir.dt.bfloat16
U32 = mybir.dt.uint32
ACT = mybir.ActivationFunctionType
ALU = mybir.AluOpType

D = 1024
SEQ = 512
META = 16
ALL = META + SEQ
HALF = ALL // 2
P = 128
KT = D // P
QT = SEQ // P
HEADS = 4
DK = D // 2 // HEADS
DV = D // HEADS
DSA_H = 16
IDX_H = 8
TOPK = 128
FF = 4 * D
FT = FF // P
BUCKETS = 32
LINE = 655
LPITCH = 656
EPS = 1e-6
BIG = 1e30
MARK = -3e38
LEVELS = [64, 32, 16, 8, 4, 2, 1]
NRAW = 3
NHL = 4
CH = 1024

C_GQ, C_GK, C_GV, C_GR, C_GA = 0, 512, 1024, 2048, 3072
C_CQ, C_CKV, C_IK, C_IW = 3088, 3344, 3472, 3536
C_MQ, C_MK, C_MV, C_MO, C_MI, C_MF = 3544, 4056, 4568, 5592, 6616, 6620
C_GATE = 6624

ROWS = {}
ROW_LIST = []


def _rows():
    at = 0
    for name, n, src in [
        ("gq", 4, "b_in"), ("gk", 4, "b_in"), ("gr", 8, "b_in"), ("cq", 2, "b_in"), ("ckv", 1, "b_in"),
        ("ik", 1, "b_in"), ("mq", 4, "b_in"), ("mk", 4, "b_in"), ("mo", 8, "b_in"), ("gate", 24, "b_in"),
        ("small", 1, "b_in"), ("a2", 4, "b_gla_a"), ("hg", 2, "g_gla_head"),
        ("hm", 2, "g_ml_head"), ("dq", 2, "g_dsa_q"), ("dkv", 1, "g_dsa_kv"), ("ig", 1, "idx_ln_g"),
        ("ib", 1, "idx_ln_b"), ("fb", 1, "ml_f_bias"), ("cv", 32, "ml_conv"),
    ]:
        ROWS[name] = at
        ROW_LIST.append((name, n, src))
        at += n
    return at


NROW = _rows()
COLUMNS = {"gq": C_GQ, "gk": C_GK, "gr": C_GR, "cq": C_CQ, "ckv": C_CKV, "ik": C_IK, "mq": C_MQ, "mk": C_MK,
           "mo": C_MO, "gate": C_GATE}
WIDTHS = {"ik": 64, "ig": 64, "ib": 64}


def row_sources(a, name, count, src):
    if name == "small":
        return [((0, 32 * n), a[src][0:1, c0:c0 + 32]) for n, c0 in enumerate(SMALL)]
    if name == "fb":
        return [((0, 64), a[src][0:1, 0:HEADS])]
    w = WIDTHS.get(name, P)
    if src == "ml_conv":
        return [((8 * k, 0), a[src][0, k:k + 1, :].rearrange("k (t p) -> (k t) p", p=P)) for k in range(4)]
    c0 = COLUMNS.get(name, 0)
    part = a[src][0, c0:c0 + count * w].rearrange("(t p) -> t p", p=w)
    if w == 64:
        return [((0, 0), part), ((0, 64), part)]
    return [((0, 0), part)]


NROWDMA = 29


SMALL = [C_IW, C_GA, C_MI, C_MF]


class Tile:

    def __init__(self, kind, m=P, kt=KT, both=False, rhs="x", off=0, width=P):
        self.kind, self.m, self.kt, self.both, self.rhs, self.off, self.width = kind, m, kt, both, rhs, off, width


def plan():
    chunks, tiles = [], {}
    state = {"done": 0, "slot": 0, "freed": [0, 0]}

    def tile(name, use, new=0, kind="F", **k):
        t = Tile(kind, **k)
        t.chunks = list(use)
        t.slot = state["slot"]
        state["slot"] ^= 1
        t.need = state["freed"][t.slot]
        state["freed"][t.slot] += 1
        t.freed = state["freed"][t.slot]
        state["done"] += 1
        t.val = state["done"]
        tiles[name] = t
        for c in t.chunks[:new]:
            chunks[c]["end"] = t.val
        return t

    def chunk(src, c0, ncol, kt=KT, k0=0, twice=False):
        chunks.append(dict(src=src, c0=c0, n=ncol, kt=kt, k0=k0, twice=twice, end=None))
        return len(chunks) - 1

    def feature(name, src, c0, m=P, kt=KT, both=False, twice=False, rhs="x"):
        c = chunk(src, c0, m, kt, twice=twice)
        tile(name, [c], 1, kind="F", m=m * (2 if twice else 1), kt=kt, both=both, rhs=rhs, off=0,
             width=m * (2 if twice else 1))

    def values(name, c0):
        c = [chunk("w_in", c0, P), chunk("w_in", c0 + P, P)]
        assert c[0] % 2 == 0
        tile(name + "A", c, 0, kind="V", off=0)
        tile(name + "B", c, 0, kind="V", off=2)
        tile(name + "M", c, 2, kind="VM")

    def pad():
        if len(chunks) % 2:
            chunks.append(None)

    feature("cq0", "w_in", C_CQ)
    feature("cq1", "w_in", C_CQ + P)
    feature("ik", "w_in", C_IK, 64, both=True, twice=True)
    chunks.append(dict(src="w_in", c0=None, n=P, kt=KT, k0=0, twice=False, end=None))
    tile("small", [len(chunks) - 1], 1, both=True)
    feature("ckv", "w_in", C_CKV, both=True)
    for m in range(2):
        feature(f"gb{m}", "w_in", C_GATE + D + m * P)
    c = chunk("w_idx_q", 0, 512, 2)
    for m in range(4):
        tile(f"iq{m}", [c], int(m == 3), kind="F", m=P, kt=2, both=False, rhs="cq", off=m * P, width=512)
    for i, n in enumerate([1, 2, 3, 0]):
        if n == 0:
            feature("gb5", "w_in", C_GATE + D + 5 * P)
        c = chunk("w_dsa_uq", n * 512, 512, 2)
        for m in range(4):
            tile(f"uq{4 * n + m}", [c], int(m == 3), kind="F", m=P, kt=2, both=False, rhs="cq", off=m * P,
                 width=512)
        if n:
            feature(f"gb{2 + i}", "w_in", C_GATE + D + (2 + i) * P)
    for m in range(6, 8):
        feature(f"gb{m}", "w_in", C_GATE + D + m * P)
    for m in range(8):
        feature(f"yb{m}", "w_br_dsa", m * P, rhs="y")
    def gla(h):
        feature(f"gq{h}", "w_in", C_GQ + h * DK)
        feature(f"gk{h}", "w_in", C_GK + h * DK, both=True)
        tile(f"gg{h}", [], 0, kind="G")

    def pairs(name, c0, h):
        for v in range(2):
            feature(f"{name}{2 * h + v}", "w_in", c0 + (2 * h + v) * P)

    def gates(name, c0, m0, m1):
        for m in range(m0, m1):
            feature(f"{name}{m}", "w_in", c0 + m * P)

    def all_values(name, c0):
        pad()
        values(name, c0)

    gla(0)
    all_values("gv0", C_GV)
    for h in range(HEADS):
        if h + 1 < HEADS:
            gla(h + 1)
        else:
            gates("ta", C_GATE, 0, 2)
        pairs("gr", C_GR, h)
        if h + 1 < HEADS:
            all_values(f"gv{h + 1}", C_GV + (h + 1) * DV)
    gates("ta", C_GATE, 2, 8)
    for m in range(8):
        feature(f"ya{m}", "w_br_gla", m * P, rhs="y")
    feature("mq0", "w_in", C_MQ, both=True)
    feature("mk0", "w_in", C_MK, both=True)
    all_values("mv0", C_MV)
    for h in range(HEADS):
        if h + 1 < HEADS:
            feature(f"mq{h + 1}", "w_in", C_MQ + (h + 1) * DK, both=True)
            feature(f"mk{h + 1}", "w_in", C_MK + (h + 1) * DK, both=True)
        else:
            gates("tc", C_GATE + 2 * D, 0, 2)
        pairs("mo", C_MO, h)
        if h + 1 < HEADS:
            all_values(f"mv{h + 1}", C_MV + (h + 1) * DV)
    gates("tc", C_GATE + 2 * D, 2, 8)
    for m in range(8):
        feature(f"yc{m}", "w_br_ml", m * P, rhs="y")
    for hf in range(2):
        for n in range(4):
            c = chunk("w_out", hf * 512, 512, 2, 2 * n)
            tile(f"out{hf}_{n}", [c], 1, kind="O")
            state["slot"] ^= 1
            state["freed"][tiles[f"out{hf}_{n}"].slot] -= 1
    for m in range(FT):
        feature(f"up{m}", "w_up", m * P, rhs="n")
    for hf in range(2):
        for n in range(FT // 2):
            c = chunk("w_down", hf * 512, 512, 2, 2 * n)
            tile(f"down{hf}_{n}", [c], 1, kind="O")
            state["slot"] ^= 1
            state["freed"][tiles[f"down{hf}_{n}"].slot] -= 1
    real, held = [], [None] * NHL
    for n, c in enumerate(chunks):
        if c is None:
            continue
        c["r"] = len(real)
        c["raw"] = c["r"] % NRAW
        c["hl"] = n % NHL
        c["after"] = held[c["hl"]]
        held[c["hl"]] = c["end"]
        real.append(c)
    total = [0] * NRAW
    for c in real:
        total[c["raw"]] += 16 * (len(SMALL) if c["c0"] is None else 2 if c["twice"] else 1)
        c["load"] = total[c["raw"]]
    return chunks, real, tiles



def build(nc, a, line, scratch, rows, out):
    chunks, real, tl = plan()
    ctx = ExitStack()
    with ctx:
        def sb(name, shape, dt=FP32):
            return ctx.enter_context(nc.sbuf_tensor(name, shape, dt))

        def sem(name):
            return ctx.enter_context(nc.semaphore(name))

        def region(offset, specs):
            with ExitStack() as r:
                if offset:
                    r.enter_context(nc.sbuf_tensor(f"below_{specs[0][0]}", [P, offset // 4], FP32))
                return [r.enter_context(nc.sbuf_tensor(n, sh, dt)) for n, sh, dt in specs]

        wraw = sb("wraw", [P, NRAW, CH])
        whi = sb("whi", [P, NHL, CH], F32R)
        wlo = sb("wlo", [P, NHL, CH], F32R)
        ident = sb("ident", [P, P])
        identb = sb("identb", [P, P], BF16)
        ones = sb("ones", [P, P])
        later_neg = sb("later_neg", [P, P])
        later_big = sb("later_big", [P, P], BF16)
        later_bigT = sb("later_bigT", [P, P])
        col = sb("col", [P, NROW])
        eps = sb("eps", [P, 1])
        lm = sb("lm", [P, len(LEVELS), 64])
        small = sb("small", [P, ALL])
        xm = sb("xm", [P, KT, 2 * META], F32R)
        first16 = sb("first16", [2 * META, 1])

        XO = 0
        MIXO = XO + 2 * KT * ALL * 4
        YO = MIXO + KT * SEQ * 4
        LO = YO + DSA_H * ALL * 4
        PTO = LO + 4 * ALL * 4
        KVO = PTO + 2 * (QT + 1) * 2 * P * 4
        xh, xl, mix = region(XO, [("xh", [P, KT, ALL], F32R), ("xl", [P, KT, ALL], F32R), ("mix", [P, KT, SEQ], FP32)])
        rline, oh, t5 = region(MIXO, [("rline", [DSA_H, LPITCH], FP32), ("oh", [BUCKETS, LINE], FP32),
                                      ("t5", [BUCKETS, DSA_H], FP32)])
        (table, L, PT, PTm, kvT, kvn, kvm, keep, low, psm, prec, qlat, S, top8, rl, wi) = region(YO, [
            ("table", [P, DSA_H, ALL], FP32), ("L", [P, 4, ALL], FP32), ("PT", [P, 2, QT, 2 * P], FP32),
            ("PTm", [META, 2, 2 * P], FP32), ("kvT", [P, ALL], FP32), ("kvn", [P, QT, P], FP32),
            ("kvm", [META, P], FP32), ("keep", [P, QT, ALL], BF16), ("low", [P, 64], FP32), ("psm", [P, 64], FP32),
            ("prec", [P, 64], FP32), ("qlat", [P, DSA_H, SEQ], FP32), ("S", [P, QT, ALL], FP32),
            ("top8", [P, 8], FP32), ("rl", [P, 2, ALL], FP32), ("wi", [P, QT, IDX_H], FP32)])
        QO = KVO + (ALL + QT * P + P) * 4 + QT * ALL * 2 + 3 * 64 * 4
        SO = QO + DSA_H * SEQ * 4
        (uvp,) = region(SO, [("uvp", [P, DSA_H, P], FP32)])
        (kn,) = region(LO, [("kn", [P, ALL], FP32)])
        cq, sq = region(QO + 4 * SEQ * 4, [("cq", [P, 2, SEQ], FP32), ("sq", [P, 2, SEQ], FP32)])
        cqh, cql = region(PTO, [("cqh", [P, 2, SEQ], F32R), ("cql", [P, 2, SEQ], F32R)])
        (qi,) = region(QO, [("qi", [P, 4, SEQ], FP32)])
        rk, ckv, ki, sqk = region(SO, [("rk", [P, ALL], FP32), ("ckv", [P, ALL], FP32), ("ki", [P, ALL], FP32),
                                       ("sqk", [P, ALL], FP32)])
        rq, xc = region(SO + QT * ALL * 4 + 64, [("rq", [P, SEQ], FP32), ("xc", [P, ALL], FP32)])
        X, Xm, gbc, junk, brow, ss = region(QO, [
            ("X", [P, QT, D], FP32), ("Xm", [META, D], FP32), ("gbc", [P, D], FP32), ("junk", [P, D], FP32),
            ("brow", [NROW, P], FP32), ("ss", [P, QT + 1], FP32)])
        mixh, mixl = region(XO, [("mixh", [P, KT, SEQ], F32R), ("mixl", [P, KT, SEQ], F32R)])
        yh, yl = region(YO, [("yh", [P, KT, SEQ], F32R), ("yl", [P, KT, SEQ], F32R)])
        AO = YO + 2 * KT * SEQ * 4
        (sgate, gtmp, vb, qh, kh, vh, vm, AT, ATm, sqo, rso, on, km) = region(AO, [
            ("sgate", [P, 2, SEQ], FP32), ("gtmp", [P, 2, SEQ], FP32), ("vb", [P, D], FP32),
            ("qh", [P, 2, SEQ], FP32), ("kh", [P, 2, ALL], FP32), ("vh", [P, 2, QT, DV], FP32),
            ("vm", [2 * META, 2, DV], FP32), ("AT", [P, QT, SEQ], FP32), ("ATm", [2 * META, SEQ], FP32),
            ("sqo", [P, 2, SEQ], FP32), ("rso", [P, SEQ], FP32), ("on", [P, 2, SEQ], FP32), ("km", [P, 2, 2 * META], FP32)])
        BO = AO + (2 * SEQ * 2 + D + 2 * SEQ + 2 * ALL + 2 * QT * DV + 2 * DV + QT * SEQ + SEQ + 2 * SEQ + SEQ + 2 * SEQ + 4 * META) * 4
        (a2, G, E, QL, KL, QQ, KHt, gt, gf, gch) = region(BO, [
            ("a2", [32 + META, HEADS * DK], FP32),
            ("G", [P, 2, ALL], FP32), ("E", [P, SEQ], FP32), ("QL", [P, 2, SEQ // 2], FP32), ("KL", [P, 2, SEQ], FP32),
            ("QQ", [P, SEQ], FP32), ("KHt", [P, ALL - P], FP32), ("gt", [P, QT + 1], FP32), ("gf", [P, QT + 1], FP32),
            ("gch", [P, ALL], FP32)])
        (zc, cv, sgc, lf_, bcum_, M_, uT, uTm, fbias_, um_, Mb, Md, Wd, Wm, emn) = region(BO, [
            ("zc", [P, ALL + 3], FP32), ("cv", [P, ALL], FP32), ("sgc", [P, ALL], FP32), ("lf", [64 + HEADS, ALL], FP32),
            ("bcum", [64 + HEADS, ALL], FP32), ("M", [64 + HEADS, ALL], FP32),
            ("uT", [P, QT, HEADS], FP32), ("uTm", [2 * META, HEADS], FP32),
            ("fbias", [64 + HEADS, 1], FP32), ("um", [64 + HEADS, 2 * META], FP32), ("Mb", [P, SEQ], FP32), ("Md", [P, SEQ], FP32), ("Wd", [P, SEQ], FP32),
            ("Wm", [2 * META, SEQ], FP32), ("emn", [P, SEQ], FP32)])
        GR = slice(64, 64 + HEADS)
        um = um_[GR, :]
        u, lf, bcum, M, fbias = small[GR, :], lf_[GR, :], bcum_[GR, :], M_[GR, :], fbias_[GR, :]
        NO = XO + 2 * KT * SEQ * 4
        nh, nl = region(NO, [("nh", [P, KT, SEQ], F32R), ("nl", [P, KT, SEQ], F32R)])
        UO = NO + 2 * KT * SEQ * 4
        (U,) = region(UO, [("U", [P, FT, SEQ], FP32)])
        (xn,) = region(UO, [("xn", [P, QT, D], FP32)])
        uh, ul = region(XO, [("uh", [P, 4, SEQ], F32R), ("ul", [P, 4, SEQ], F32R)])
        gains, jk, ssf, hres = region(UO + FT * SEQ * 4, [
            ("gains", [P, 2, D], FP32), ("jk", [P, SEQ], FP32), ("ssf", [P, 3, QT, 2], FP32),
            ("hres", [P, QT, D], FP32)])

        def gate_store(m):
            return [vh[:, 0, 0:2, :].rearrange("p a b -> p (a b)"), vh[:, 0, 2:4, :].rearrange("p a b -> p (a b)"),
                    kh[:, 0, 0:SEQ], qh[:, 0, :], vb[:, 0:SEQ], vb[:, SEQ:D], AT[:, 0, :], AT[:, 1, :]][m]

        def Ls(v):
            return L[:, v % 6, :] if v % 6 < 4 else rl[:, v % 6 - 4, :]

        GP = [ctx.enter_context(nc.psum_tensor(f"GP{i}", [P, 1024], FP32)) for i in range(2)]
        PA = [ctx.enter_context(nc.psum_tensor(f"PA{i}", [P, 1024], FP32)) for i in range(2)]

        def bank(i):
            return PA[i // 2][:, (i % 2) * SEQ:(i % 2 + 1) * SEQ]

        def halves(ps, n=P):
            return ps[0:n, :].rearrange("p (a b) -> p a b", a=2)[:, :, 0:HALF]

        def two(t, n=P):
            return t[0:n, 0:ALL].rearrange("p (a b) -> p a b", a=2)

        def accumulators(name, hf, t):
            pair = GP if hf else PA
            return pair[t // 2][:, (t % 2) * SEQ:(t % 2 + 1) * SEQ]

        def cc(name, k=0, n=P):
            return col[0:n, ROWS[name] + k:ROWS[name] + k + 1]

        raw_in = [sem(f"raw_in{i}") for i in range(NRAW)]
        hi_done, split_done, gemm_done = sem("hi_done"), sem("split_done"), sem("gemm_done")
        gfree = [sem(f"gfree{i}") for i in range(2)]
        act_c, dve_c, pool_c = sem("act_chain"), sem("dve_chain"), sem("pool_chain")
        row_zero, ld_rows, ld_line = sem("row_zero"), sem("ld_rows"), sem("ld_line")
        ld_x, ld_pre = [sem(f"ld_x{t}") for t in range(QT + 1)], sem("ld_pre")
        masks, f16_ok = sem("masks"), sem("first16_ok")
        col_ps, col_ok, ss_zero, rs_ok, xn_ok = sem("col_ps"), sem("col_ok"), sem("ss_zero"), sem("rs_ok"), sem("xn_ok")
        xt_ps, xh_ok, xl_ok = sem("xt_ps"), sem("xh_ok"), sem("xl_ok")
        line_ps, line_ok, table_in = sem("line_ps"), sem("line_ok"), sem("table_in")
        line_out, line_rep = sem("line_out"), sem("line_rep")
        cqsq, kvsq, xcsq, ssq_ps = sem("cqsq"), sem("kvsq"), sem("xcsq"), sem("ssq_ps")
        rq_ok, rk_ok, xc_ok = sem("rq_ok"), sem("rk_ok"), sem("xc_ok")
        cqs_ok, kvT_ok, kn_ok, kvn_ps, kvn_ok = sem("cqs_ok"), sem("kvT_ok"), sem("kn_ok"), sem("kvn_ps"), sem("kvn_ok")
        sc_ps, sc_rl, sc_acc, keep_ok = sem("sc_ps"), sem("sc_rl"), sem("sc_acc"), sem("keep_ok")
        lg_ps, lg_mn, p_exp, p_nrm = sem("lg_ps"), sem("lg_mn"), sem("p_exp"), sem("p_nrm")
        pt_ps, pt_a, pt_d, pv_ps, ol_ev = sem("pt_ps"), sem("pt_a"), sem("pt_d"), sem("pv_ps"), sem("ol_ev")
        uv_zero, ld_uv, uv_ps, yh_b, yl_b = sem("uv_zero"), sem("ld_uv"), sem("uv_ps"), sem("yh_b"), sem("yl_b")
        ld_a, gla_c, gg_a, gg_l, G_ok = sem("ld_a"), sem("gla_consts"), sem("gg_a"), sem("gg_l"), sem("G_ok")
        lv_w, lv_e, lv_qk, lv_ps, lv_sel = sem("lv_w"), sem("lv_e"), sem("lv_qk"), sem("lv_ps"), sem("lv_sel")
        od_e, od_q, od_ps, od_ev = sem("od_e"), sem("od_q"), sem("od_ps"), sem("od_ev")
        km_ok, sum_sq, av_ps, av_sq, av_ss, av_rs, on_ok = sem("km_ok"), sem("sum_sq"), sem("av_ps"), sem("av_sq"), sem("av_ss"), sem("av_rs"), sem("on_ok")
        sg_ok, silu_ok, y_ok, gate_ok, mix_ok = sem("sg_ok"), sem("silu_ok"), sem("y_ok"), sem("gate_ok"), sem("mix_ok")
        ld_v, zpad, cv_ok, cs_ok, qk_ok = sem("ld_v"), sem("zpad"), sem("cv_ok"), sem("cs_ok"), sem("qk_ok")
        fa_ok, fl_ok, u_ok, M_ok, uT_ps, uT_ok = sem("fa_ok"), sem("fl_ok"), sem("u_ok"), sem("M_ok"), sem("uT_ps"), sem("uT_ok")
        rows_out, mb_ok, md_ok, em_in, em_ok = sem("rows_out"), sem("mb_ok"), sem("md_ok"), sem("em_in"), sem("em_ok")
        s_ps, w_ok, at_ok, num_ok = sem("s_ps"), sem("w_ok"), sem("at_ok"), sem("num_ok")
        ms_ok, ms_d, M_one = sem("ms_ok"), sem("ms_d"), sem("M_one")
        ld_h, ld_g, tok_done, o_ss, h_ok, n_ok = sem("ld_h"), sem("ld_g"), sem("tok_done"), sem("o_ss"), sem("h_ok"), sem("n_ok")
        nt_ps, nh_ok, nl_ok = sem("nt_ps"), sem("nh_ok"), sem("nl_ok")
        U_ok, uh_ok, ul_ok, fin, out_done = sem("U_ok"), sem("uh_ok"), sem("ul_ok"), sem("fin"), sem("out_done")

        block = ctx.enter_context(nc.Block())
        NHEADS2 = DSA_H // 2
        ROUNDS = TOPK // 8 + 1
        EARLY = 9
        WIO = 960
        GROUPS = QT * NHEADS2

        def pt_d_after(g):
            return max(g + 1 - 2 * NHEADS2, 0)

        @block.sync
        def _(sp):
            for t in range(QT):
                sp.dma_start(X[:, t, :], a["x"][0, t * P:(t + 1) * P, :]).then_inc(ld_x[t], 16)
                if t == 0:
                    sp.dma_start(gbc[:, :], a["g_pre_mix"].broadcast_to([P, D])).then_inc(ld_pre, 16)
            sp.dma_start(Xm[:, :], a["meta_tokens"]).then_inc(ld_x[QT], 16)
            for c in real:
                if c["r"] == NRAW:
                    sp.wait_ge(row_zero, 1)
                    n = 0
                    for name, count, src in ROW_LIST:
                        r = ROWS[name]
                        for dst, part in row_sources(a, name, count, src):
                            sp.dma_start(brow[r + dst[0]:r + dst[0] + part.shape[0], dst[1]:dst[1] + part.shape[1]],
                                         part).then_inc(ld_rows, 16)
                            n += 1
                    assert n == NROWDMA, n
                if c["r"] >= NRAW:
                    sp.wait_ge(split_done, c["r"] - NRAW + 1)
                if c["r"] == 4:
                    sp.wait_ge(line_ok, 1)
                    sp.dma_start(line, rline[:, 0:LINE]).then_inc(line_out, 16)
                if c["r"] == 6:
                    sp.wait_ge(line_out, 16)
                    sp.dma_start(scratch[:, :, 0:LINE], line.unsqueeze(0).broadcast_to([P, DSA_H, LINE])).then_inc(line_rep, 16)
                if c["r"] == 14:
                    sp.wait_ge(line_rep, 16)
                    sp.dma_start(table[:, :, :], bass.AP(tensor=scratch.tensor, offset=P - 1,
                                                         ap=[[DSA_H * LPITCH - 1, P], [LPITCH, DSA_H], [1, ALL]])).then_inc(table_in, 16)
                if c["c0"] is None:
                    for n_, c0 in enumerate(SMALL):
                        sp.dma_start(wraw[:, c["raw"], :].rearrange("p (k n) -> p k n", n=P)[:, :, 32 * n_:32 * n_ + 32],
                                     a["w_in"][0, :, c0:c0 + 32].rearrange("(k p) n -> p k n", p=P)).then_inc(raw_in[c["raw"]], 16)
                    continue
                src = a[c["src"]][0, c["k0"] * P:(c["k0"] + c["kt"]) * P, c["c0"]:c["c0"] + c["n"]]
                src = src.rearrange("(k p) n -> p k n", p=P)
                w = c["n"] * (2 if c["twice"] else 1)
                dst = wraw[:, c["raw"], 0:c["kt"] * w].rearrange("p (k n) -> p k n", n=w)
                for rep in range(w // c["n"]):
                    sp.dma_start(dst[:, :, rep * c["n"]:(rep + 1) * c["n"]], src).then_inc(raw_in[c["raw"]], 16)
                if c["src"] == "w_down" and c["c0"] == 0 and c["k0"] == 0:
                    sp.wait_ge(h_ok, 2 * QT)
                    sp.dma_start(gains[:, 0, :], a["g_post_mlp"].broadcast_to([P, D])).then_inc(ld_g, 16)
            for t in range(QT):
                for hf in range(2):
                    sp.wait_ge(fin, 2 * t + hf + 1)
                    sp.dma_start(out[0, t * P:(t + 1) * P, hf * SEQ:(hf + 1) * SEQ],
                                 hres[:, t, hf * SEQ:(hf + 1) * SEQ]).then_inc(out_done, 16)
            sp.wait_ge(out_done, 16 * 2 * QT)

        @block.gpsimd
        def _(pool):
            nc.gpsimd.memset(ident[:, :], 0.0).then_inc(pool_c, 1)
            nc.gpsimd.memset(later_neg[:, :], 0.0).then_inc(pool_c, 1)
            nc.gpsimd.memset(later_bigT[:, :], 0.0).then_inc(pool_c, 1)
            pool.wait_ge(pool_c, 3)
            nc.gpsimd.affine_select(out=ident[:, :], in_=ident[:, :], compare_op=ALU.not_equal, fill=1.0, base=0,
                                    pattern=[[-1, P]], channel_multiplier=1).then_inc(pool_c, 1)
            nc.gpsimd.affine_select(out=later_neg[:, :], in_=later_neg[:, :], compare_op=ALU.is_ge, fill=-BIG, base=0,
                                    pattern=[[-1, P]], channel_multiplier=1).then_inc(pool_c, 1)
            nc.gpsimd.affine_select(out=later_bigT[:, :], in_=later_bigT[:, :], compare_op=ALU.is_ge, fill=BIG, base=0,
                                    pattern=[[1, P]], channel_multiplier=-1).then_inc(pool_c, 1)
            pool.wait_ge(pool_c, 6)
            nc.gpsimd.tensor_copy(identb[:, :], ident[:, :]).then_inc(masks, 1)
            nc.gpsimd.tensor_scalar(later_big[:, :], later_neg[:, :], -1.0, 1.0, ALU.mult, ALU.mult).then_inc(masks, 1)
            nc.gpsimd.memset(lm[:, :, :], 1.0).then_inc(pool_c, 1)
            pool.wait_ge(pool_c, 7)
            for l, B in enumerate(LEVELS):
                v = lm[:, l, :].rearrange("p (n b) -> p n b", b=B)
                nc.gpsimd.affine_select(out=v, in_=v, compare_op=ALU.is_ge, fill=0.0, base=0,
                                        pattern=[[-2 * B, 64 // B], [0, B]], channel_multiplier=1).then_inc(pool_c, 1)
                pool.wait_ge(pool_c, 8 + l)
            for l, B in enumerate(LEVELS):
                v = lm[:, l, :].rearrange("p (n b) -> p n b", b=B)
                nc.gpsimd.affine_select(out=v, in_=v, compare_op=ALU.is_ge, fill=0.0, base=B - 1,
                                        pattern=[[2 * B, 64 // B], [0, B]], channel_multiplier=-1).then_inc(masks, 1)
            pool.wait_ge(masks, 2 + len(LEVELS))
            for c in real:
                n = c["kt"] * c["n"] * (2 if c["twice"] else 1)
                src, hi, lo = wraw[:, c["raw"], 0:n], whi[:, c["hl"], 0:n], wlo[:, c["hl"], 0:n]
                if c is chunks[tl["yb4"].chunks[0]]:
                    pool.wait_ge(keep_ok, QT)
                    nc.gpsimd.memset(uvp[:, :, :], 0.0).then_inc(uv_zero, 1)
                pool.wait_ge(raw_in[c["raw"]], c["load"])
                if c["after"]:
                    pool.wait_ge(gemm_done, c["after"])
                nc.gpsimd.tensor_scalar(hi, src, 1.0, 1.0, ALU.mult, ALU.mult).then_inc(hi_done, 1)
                pool.wait_ge(hi_done, c["r"] + 1)
                nc.gpsimd.tensor_tensor(lo, src, hi.bitcast(FP32), ALU.subtract).then_inc(split_done, 1)

        @block.scalar
        def _(act):
            n = [0]

            def seq(ins):
                n[0] += 1
                ins.then_inc(act_c, 1)
                act.wait_ge(act_c, n[0])

            def lnexp():
                nc.scalar.preload_act_table_set("natural_log_exp_and_others")

            def inv_root(t, src, width, wait=False):
                seq(nc.scalar.activation(t, src, ACT.Ln, bias=eps[0:t.shape[0], :], scale=1.0 / width))
                return nc.scalar.activation(t, t, ACT.Exp, scale=-0.5)

            def ready(name):
                t = tl[name]
                act.wait_ge(gemm_done, t.val)
                return GP[t.slot]

            def whole(name):
                act.wait_ge(gfree[tl[name].slot], tl[name].freed)

            act.dma_start(oh[:, :], a["onehot"]).then_inc(ld_line, 16)
            act.dma_start(t5[:, :], a["t5_bias"]).then_inc(ld_line, 16)
            lnexp()
            act.wait_ge(ss_zero, 1)

            def input_norm(t):
                src = X[:, t, :] if t < QT else Xm[:, :]
                n_ = src.shape[0]
                act.wait_ge(ld_x[t], 16)
                seq(nc.scalar.activation(junk[0:n_, :], src, ACT.Square, accum_out=ss[0:n_, t:t + 1]))
                inv_root(ss[0:n_, t:t + 1], ss[0:n_, t:t + 1], D, wait=True).then_inc(rs_ok, 1)

            def input_high(t):
                if t == QT:
                    act.wait_ge(xt_ps, KT + 1)
                    nc.scalar.activation(xh[:, :, 0:META], GP[1][:, 0:KT * META].rearrange("p (k m) -> p k m", m=META),
                                         ACT.Copy).then_inc(xh_ok, 1)
                    act.wait_ge(xh_ok, KT + 1)
                    nc.scalar.activation(xm[:, :, 0:META], xh[:, :, 0:META].bitcast(FP32), ACT.Copy).then_inc(xh_ok, 1)
                    return
                for hf in range(2):
                    act.wait_ge(xt_ps, 2 * t + hf + 1)
                    nc.scalar.activation(xh[:, 4 * hf:4 * hf + 4, META + t * P:META + (t + 1) * P],
                                         bank(2 * (t % 2) + hf).rearrange("p (f n) -> p f n", n=P), ACT.Copy).then_inc(xh_ok, 1)

            input_norm(0)
            for t in range(1, QT):
                input_norm(t)
                input_high(t - 1)
                if t == 3:
                    act.wait_ge(line_ps, 1)
                    nc.scalar.activation(rline[:, 0:LINE], GP[0][0:DSA_H, 0:LINE], ACT.Copy, scale=-1.0).then_inc(line_ok, 1)
            input_high(QT - 1)
            input_norm(QT)
            input_high(QT)
            act.wait_ge(col_ok, 1)
            act.wait_ge(xl_ok, KT + 1)

            def gate_b(m):
                nc.scalar.activation(mix[:, m, :], ready(f"gb{m}")[:, 0:SEQ], ACT.Sigmoid, bias=cc("gate", 8 + m)).then_inc(gfree[tl[f"gb{m}"].slot], 1)

            for k in range(2):
                nc.scalar.activation(cq[:, k, :], ready(f"cq{k}")[:, 0:SEQ], ACT.Identity, bias=cc("cq", k)).then_inc(gfree[tl[f"cq{k}"].slot], 1)
            whole("cq0")
            whole("cq1")
            nc.scalar.activation(sq[:, :, :], cq[:, :, :], ACT.Square).then_inc(cqsq, 1)
            nc.scalar.activation(two(ki), halves(ready("ik")), ACT.Identity, bias=cc("ik")).then_inc(gfree[tl["ik"].slot], 1)
            act.wait_ge(ssq_ps, 1)
            inv_root(rq[:, :], PA[0][:, 0:SEQ], 2 * P).then_inc(rq_ok, 1)
            nc.scalar.activation(two(small), halves(ready("small")), ACT.Identity, bias=cc("small")).then_inc(gfree[tl["small"].slot], 1)
            act.wait_ge(xc_ok, 1)
            nc.scalar.activation(sqk[:, :], xc[:, :], ACT.Square).then_inc(xcsq, 1)
            nc.scalar.activation(two(ckv), halves(ready("ckv")), ACT.Identity, bias=cc("ckv")).then_inc(gfree[tl["ckv"].slot], 1)
            act.wait_ge(ssq_ps, 3)
            inv_root(two(rk), halves(PA[1]), P).then_inc(rk_ok, 1)
            whole("ckv")
            nc.scalar.activation(sqk[:, :], ckv[:, :], ACT.Square).then_inc(kvsq, 1)
            act.wait_ge(ssq_ps, 4)
            act.wait_ge(kn_ok, 1)
            inv_root(two(rk), halves(PA[1]), P).then_inc(rk_ok, 1)
            act.wait_ge(line_out, 16)
            gate_b(0)
            gate_b(1)
            act.wait_ge(kvn_ps, 1)
            nc.scalar.activation(kvn[:, :, :], PA[0][:, 0:QT * P].rearrange("p (t c) -> p t c", t=QT), ACT.Copy).then_inc(kvn_ok, 1)
            nc.scalar.activation(kvm[:, :], PA[0][0:META, QT * P:(QT + 1) * P], ACT.Copy).then_inc(kvn_ok, 1)
            nc.scalar.activation(wi[:, :, :], PA[0][:, WIO:WIO + QT * IDX_H].rearrange("p (t h) -> p t h", h=IDX_H),
                                 ACT.Copy, scale=IDX_H ** -0.5).then_inc(kvn_ok, 1)
            def query(h):
                nc.scalar.activation(qlat[:, h, :], ready(f"uq{h}")[:, 0:SEQ], ACT.Copy, scale=-float(P) ** -0.5).then_inc(gfree[tl[f"uq{h}"].slot], 1)

            for m in range(4):
                nc.scalar.activation(qi[:, m, :], ready(f"iq{m}")[:, 0:SEQ], ACT.Copy, scale=0.125).then_inc(gfree[tl[f"iq{m}"].slot], 1)
            for v in range(QT * IDX_H):
                w = META + P * (v // IDX_H + 1)
                act.wait_ge(sc_ps, v + 1)
                if v >= 2:
                    act.wait_ge(sc_acc, v - 1)
                nc.scalar.activation(rl[:, v % 2, 0:w], PA[v % 2][:, 0:w], ACT.Relu).then_inc(sc_rl, 1)
                if v % 2 and v // 2 < DSA_H - 4:
                    query(4 + v // 2)
                if v % IDX_H == IDX_H - 1:
                    gate_b(2 + v // IDX_H)
            act.wait_ge(sc_ps, QT * IDX_H)
            for h in range(4):
                query(h)
            gate_b(6)
            gate_b(7)
            lnexp()

            def exps(v):
                i = v // DSA_H
                w = META + P * (i + 1)
                act.wait_ge(lg_mn, v + 1)
                nc.scalar.activation(Ls(v)[:, 0:w], Ls(v)[:, 0:w], ACT.Exp, bias=low[:, v:v + 1], scale=-1.0,
                                     accum_out=psm[:, v:v + 1]).then_inc(p_exp, 1)

            for v in range(4):
                exps(v)
            for g in range(GROUPS):
                i, h = g // NHEADS2, 2 * (g % NHEADS2)
                act.wait_ge(pt_ps, g + 1)
                if g >= 2:
                    act.wait_ge(pv_ps, g - 1)
                w = min(i + 1, 2)
                nc.scalar.activation(PT[:, g % 2, 0:w, :], GP[0][:, 0:w * 2 * P].rearrange("p (j n) -> p j n", j=w),
                                     ACT.Copy).then_inc(pt_a, 1)
                nc.scalar.activation(PTm[:, g % 2, :], GP[1][0:META, (g % 2) * 2 * P:(g % 2 + 1) * 2 * P],
                                     ACT.Copy).then_inc(pt_a, 1)
                if g + 2 < GROUPS:
                    exps(2 * g + 4)
                    exps(2 * g + 5)
                act.wait_ge(pv_ps, g + 1)
                nc.scalar.activation(qlat[:, h:h + 2, i * P:(i + 1) * P],
                                     GP[1][:, SEQ + (g % 2) * 2 * P:SEQ + (g % 2 + 1) * 2 * P].rearrange("p (h n) -> p h n", h=2),
                                     ACT.Copy).then_inc(ol_ev, 1)
                if g == 3 * NHEADS2:
                    act.wait_ge(uv_zero, 1)
                    act.dma_start(uvp[:, 0::2, 0:64], a["w_dsa_uv"][0, 0::2].rearrange("h c d -> c h d")).then_inc(ld_uv, 16)
                    act.dma_start(uvp[:, 1::2, 64:P], a["w_dsa_uv"][0, 1::2].rearrange("h c d -> c h d")).then_inc(ld_uv, 16)
            for m in range(KT):
                act.wait_ge(uv_ps, m + 1)
                nc.scalar.activation(yh[:, m, :], PA[m % 2][:, 0:SEQ], ACT.Copy).then_inc(yh_b, 1)
            act.wait_ge(yl_b, KT)
            act.dma_start(a2[32:32 + META, :], a["w_gla_a2"][0]).then_inc(ld_a, 16)
            act.dma_start(vb[:, :], a["b_in"][0:1, C_GV:C_GV + D].broadcast_to([P, D])).then_inc(ld_a, 16)
            def gate_of(h):
                ps = ready(f"gg{h}")
                if h:
                    act.wait_ge(gg_l, h)
                    act.wait_ge(G_ok, h)
                nc.scalar.activation(two(gch), halves(ps), ACT.Abs, bias=cc("a2", h)).then_inc(gg_a, 1)
                act.wait_ge(gg_a, h + 1)
                seq(nc.scalar.activation(gch[:, :], gch[:, :], ACT.Exp, scale=-1.0))
                nc.scalar.activation(gch[:, :], gch[:, :], ACT.Ln, bias=1.0).then_inc(gg_l, 1)

            def level(h, l):
                k = len(LEVELS) * h + l
                act.wait_ge(lv_w, k + 1)
                nc.scalar.activation(E[:, :], E[:, :], ACT.Exp, scale=1.0 / 16.0).then_inc(lv_e, 1)

            def off(h):
                g0 = G[:, h % 2, :]
                if h:
                    act.wait_ge(od_q, 4 * h)
                    act.wait_ge(od_ps, 4 * h)
                nc.scalar.activation(QQ[:, :], g0[:, META:ALL], ACT.Exp, scale=1.0 / 16.0).then_inc(od_e, 1)
                nc.scalar.activation(gf[:, :], g0[:, META - 1::P], ACT.Exp, scale=1.0 / 16.0).then_inc(od_e, 1)
                seq(nc.scalar.activation(gt[:, :], g0[:, META - 1::P], ACT.Copy, scale=1.0 / 16.0))
                nc.scalar.activation(KHt[:, 0:META], g0[:, 0:META], ACT.Exp, bias=gt[:, 0:1], scale=-1.0 / 16.0).then_inc(od_e, 1)
                for j in range(3):
                    nc.scalar.activation(KHt[:, META + j * P:META + (j + 1) * P], g0[:, META + j * P:META + (j + 1) * P],
                                         ACT.Exp, bias=gt[:, j + 1:j + 2], scale=-1.0 / 16.0).then_inc(od_e, 1)

            def off_out(h):
                if h:
                    act.wait_ge(av_ps, h)
                for q, j in enumerate([2, 1, 0]):
                    act.wait_ge(od_ps, 4 * h + q + 1)
                    w = SEQ - P * (j + 1)
                    nc.scalar.activation(AT[:, j, P:P + w], bank(q)[:, 0:w], ACT.Copy).then_inc(od_ev, 1)
                act.wait_ge(od_ps, 4 * h + 4)
                nc.scalar.activation(ATm[:, :], bank(3)[0:2 * META, :], ACT.Copy).then_inc(od_ev, 1)

            def head_norm(k, src):
                nc.scalar.activation(sqo[:, :, :], src, ACT.Square).then_inc(av_sq, 1)
                act.wait_ge(av_ss, k + 1)
                inv_root(rso[:, :], bank(2), DV).then_inc(av_rs, 1)

            def raw(h, v):
                m = 2 * h + v
                ps = ready(f"gr{m}")
                if h:
                    act.wait_ge(silu_ok, 2 * h)
                nc.scalar.activation(gtmp[:, v, :], ps[:, 0:SEQ], ACT.Identity, bias=cc("gr", m)).then_inc(gfree[tl[f"gr{m}"].slot], 1)

            def sigmoids(h):
                for v in range(2):
                    whole(f"gr{2 * h + v}")
                    if h:
                        act.wait_ge(y_ok, 2 * h)
                    nc.scalar.activation(sgate[:, v, :], gtmp[:, v, :], ACT.Sigmoid).then_inc(sg_ok, 1)
                lnexp()

            def gate_in(name, at, m):
                ps = ready(f"{name}{m}")
                nc.scalar.activation(gate_store(m), ps[:, 0:SEQ], ACT.Identity, bias=cc("gate", at + m)).then_inc(gfree[tl[f"{name}{m}"].slot], 1)

            def gates(name):
                for m in range(KT):
                    whole(f"{name}{m}")
                    nc.scalar.activation(gate_store(m), gate_store(m), ACT.Sigmoid).then_inc(gate_ok, 1)
                lnexp()

            def high_parts(base, h):
                for v in range(2):
                    m = 2 * h + v
                    act.wait_ge(y_ok, base + m + 1)
                    nc.scalar.activation(yh[:, m, :], on[:, v, :], ACT.Copy).then_inc(ms_ok, 1)

            def finish(h):
                act.wait_ge(av_ps, h + 1)
                head_norm(h, PA[0][:, :].rearrange("p (a b) -> p a b", a=2))

            gate_of(0)
            for h in range(HEADS):
                last = h == HEADS - 1
                level(h, 0)
                if h:
                    finish(h - 1)
                if last:
                    gate_in("ta", 0, 0)
                level(h, 1)
                level(h, 2)
                if last:
                    gate_in("ta", 0, 1)
                else:
                    gate_of(h + 1)
                level(h, 3)
                raw(h, 0)
                if h:
                    high_parts(0, h - 1)
                level(h, 4)
                level(h, 5)
                raw(h, 1)
                level(h, 6)
                off(h)
                if last:
                    gate_in("ta", 0, 2)
                off_out(h)
                sigmoids(h)
                if last:
                    whole("gv3M")
                    gate_in("ta", 0, 3)
                    gate_in("ta", 0, 4)
            finish(HEADS - 1)
            gate_in("ta", 0, 5)
            gate_in("ta", 0, 6)
            high_parts(0, HEADS - 1)
            gate_in("ta", 0, 7)
            gates("ta")
            act.wait_ge(mix_ok, KT)
            act.wait_ge(gate_ok, KT)
            act.dma_start(vb[:, :], a["b_in"][0:1, C_MV:C_MV + D].broadcast_to([P, D])).then_inc(ld_v, 16)
            act.wait_ge(ms_d, 2)
            nc.scalar.activation(lf, bcum, ACT.Abs).then_inc(fa_ok, 1)
            act.wait_ge(fa_ok, 1)
            seq(nc.scalar.activation(lf, lf, ACT.Exp, scale=-1.0))
            nc.scalar.activation(lf, lf, ACT.Ln, bias=1.0).then_inc(fl_ok, 1)

            def conv_in(h, q):
                k = 2 * h + q
                ps = ready(f"m{'qk'[q]}{h}")
                act.wait_ge(zpad, 1)
                if k:
                    act.wait_ge(cv_ok, k)
                nc.scalar.activation(zc[:, 3:3 + ALL].rearrange("p (a b) -> p a b", a=2), halves(ps), ACT.Identity,
                                     bias=cc(f"m{'qk'[q]}", h)).then_inc(gfree[tl[f"m{'qk'[q]}{h}"].slot], 1)

            def conv_sig(h, q):
                k = 2 * h + q
                act.wait_ge(cv_ok, k + 1)
                if k:
                    act.wait_ge(qk_ok, k)
                nc.scalar.activation(sgc[:, :], cv[:, :], ACT.Sigmoid).then_inc(cs_ok, 1)

            def fetch_maxima(h):
                if h:
                    act.wait_ge(md_ok, h)
                    act.wait_ge(w_ok, 8 * h)
                act.wait_ge(rows_out, 32)
                act.dma_start(Mb[:, :], rows[0, h:h + 1, META:ALL].broadcast_to([P, SEQ])).then_inc(mb_ok, 16)

            def maxima(h):
                if h:
                    act.wait_ge(num_ok, 2 * h)
                act.dma_start(emn[:, :], rows[1, h:h + 1, META:ALL].broadcast_to([P, SEQ])).then_inc(em_in, 16)
                act.wait_ge(mb_ok, 16 * (h + 1))
                act.wait_ge(uT_ok, 2)
                if h:
                    act.wait_ge(at_ok, 5 * h)
                act.wait_ge(md_ok, h + 1)
                nc.scalar.activation(Wm[:, :], Mb[0:2 * META, :], ACT.Exp, bias=uTm[:, h:h + 1], scale=-1.0).then_inc(w_ok, 1)

            def floor_of(h):
                act.wait_ge(em_in, 16 * (h + 1))
                nc.scalar.activation(emn[:, :], emn[:, :], ACT.Exp).then_inc(em_ok, 1)

            def decay(h, j):
                if j:
                    act.wait_ge(at_ok, 5 * h + j + 1)
                nc.scalar.activation(Wd[:, 0:P], Md[:, j * P:(j + 1) * P], ACT.Exp, bias=uT[:, j, h:h + 1], scale=-1.0).then_inc(w_ok, 1)
                if j < QT - 1:
                    nc.scalar.activation(Wd[:, P:SEQ - j * P], Mb[:, (j + 1) * P:SEQ], ACT.Exp, bias=uT[:, j, h:h + 1],
                                         scale=-1.0).then_inc(w_ok, 1)

            def out_gate(h, v):
                m = 2 * h + v
                ps = ready(f"mo{m}")
                act.wait_ge(y_ok, 8 + 2 * h)
                nc.scalar.activation(sgate[:, v, :], ps[:, 0:SEQ], ACT.Sigmoid, bias=cc("mo", m)).then_inc(gfree[tl[f"mo{m}"].slot], 1)

            for q in range(2):
                conv_in(0, q)
                conv_sig(0, q)
            lnexp()
            act.wait_ge(M_ok, 1)
            act.dma_start(rows[0], M).then_inc(rows_out, 16)
            act.dma_start(rows[1], bcum).then_inc(rows_out, 16)
            fetch_maxima(0)
            for h in range(HEADS):
                more = h + 1 < HEADS
                if h:
                    act.wait_ge(num_ok, 2 * h)
                    head_norm(HEADS + h - 1, on[:, :, :])
                maxima(h)
                decay(h, 0)
                floor_of(h)
                decay(h, 1)
                if more:
                    conv_in(h + 1, 0)
                else:
                    gate_in("tc", 16, 0)
                if h:
                    high_parts(8, h - 1)
                decay(h, 2)
                decay(h, 3)
                if more:
                    fetch_maxima(h + 1)
                    conv_sig(h + 1, 0)
                    conv_in(h + 1, 1)
                else:
                    gate_in("tc", 16, 1)
                out_gate(h, 0)
                if more:
                    conv_sig(h + 1, 1)
                out_gate(h, 1)
                lnexp()
            for m in range(2, 4):
                gate_in("tc", 16, m)
            act.wait_ge(num_ok, 2 * HEADS)
            head_norm(2 * HEADS - 1, on[:, :, :])
            whole("mv3M")
            gate_in("tc", 16, 4)
            gate_in("tc", 16, 5)
            gate_in("tc", 16, 6)
            high_parts(8, HEADS - 1)
            gate_in("tc", 16, 7)
            gates("tc")
            act.wait_ge(yl_b, 3 * KT)
            act.dma_start(hres[:, :, :], a["x"][0].rearrange("(t p) d -> p t d", p=P)).then_inc(ld_h, 16)
            for n_, g_ in enumerate(["g_post_mix", "g_pre_mlp"]):
                act.dma_start(gains[:, n_, :], a[g_].broadcast_to([P, D])).then_inc(ld_g, 16)
            for m in range(KT):
                act.wait_ge(mix_ok, KT + m + 1)
                nc.scalar.activation(mixh[:, m, :], mix[:, m, :], ACT.Copy).then_inc(ms_ok, 1)

            def first_half(k, t, src):
                seq(nc.scalar.activation(jk[:, :], src, ACT.Square, accum_out=ssf[:, k, t, 0:1]))
                return nc.scalar.activation(ssf[:, k, t, 0:1], ssf[:, k, t, 0:1], ACT.Identity, bias=eps[:, :], scale=1.0 / D)

            def root(k, t, src):
                seq(nc.scalar.activation(jk[:, :], src, ACT.Square, accum_out=ssf[:, k, t, 1:2]))
                seq(nc.scalar.activation(ssf[:, k, t, 0:1], ssf[:, k, t, 1:2], ACT.Ln, bias=ssf[:, k, t, 0:1], scale=1.0 / D))
                nc.scalar.activation(ssf[:, k, t, 0:1], ssf[:, k, t, 0:1], ACT.Exp, scale=-0.5).then_inc(o_ss, 1)

            act.wait_ge(gemm_done, tl["out0_3"].val)
            for t in range(QT):
                seq(first_half(0, t, accumulators("out", 0, t)))

            def projected(t):
                act.wait_ge(tok_done, t + 1)
                root(0, t, accumulators("out", 1, t))

            def residual(t):
                act.wait_ge(h_ok, 2 * t + 1)
                seq(first_half(1, t, hres[:, t, 0:SEQ]))
                act.wait_ge(h_ok, 2 * t + 2)
                root(1, t, hres[:, t, SEQ:D])

            def high_norm(t):
                for hf in range(2):
                    act.wait_ge(nt_ps, 2 * t + hf + 1)
                    nc.scalar.activation(nh[:, 4 * hf:4 * hf + 4, t * P:(t + 1) * P],
                                         accumulators("out", hf, t).rearrange("p (f n) -> p f n", n=P), ACT.Copy).then_inc(nh_ok, 1)

            for t in range(QT):
                projected(t)
                if t >= 2:
                    high_norm(t - 2)
                residual(t)
            high_norm(QT - 2)
            high_norm(QT - 1)
            def hidden_high(k):
                act.wait_ge(U_ok, k % FT + 1)
                if k >= 4:
                    act.wait_ge(gemm_done, tl[f"down{(k - 4) // FT}_{(k - 4) % FT // 2}"].val)
                nc.scalar.activation(uh[:, k % 4, :], U[:, k % FT, :], ACT.Copy).then_inc(uh_ok, 1)

            for m in range(FT):
                ps = ready(f"up{m}")
                nc.scalar.activation(U[:, m, :], ps[:, 0:SEQ], ACT.Relu).then_inc(gfree[tl[f"up{m}"].slot], 1)
                if m >= FT - 4:
                    hidden_high(m - FT + 4)
            for k in range(4, 2 * FT):
                hidden_high(k)
                if k == FT + 3:
                    for t in range(QT):
                        seq(first_half(2, t, accumulators("down", 0, t)))
            for t in range(QT):
                act.wait_ge(tok_done, QT + t + 1)
                root(2, t, accumulators("down", 1, t))

        @block.vector
        def _(dve):
            n = [0]

            def seq(ins):
                n[0] += 1
                ins.then_inc(dve_c, 1)
                dve.wait_ge(dve_c, n[0])

            def ready(name):
                t = tl[name]
                dve.wait_ge(gemm_done, t.val)
                return GP[t.slot]

            def whole(name):
                dve.wait_ge(gfree[tl[name].slot], tl[name].freed)

            def twice(out_, meta, signal):
                nc.vector.tensor_copy(out_.rearrange("p (a b) -> p a b", a=2),
                                      meta.unsqueeze(1).broadcast_to([meta.shape[0], 2, META])).then_inc(signal, 1)

            tt, ts, stt = nc.vector.tensor_tensor, nc.vector.tensor_scalar, nc.vector.scalar_tensor_tensor
            nc.vector.memset(brow[:, :], 0.0).then_inc(row_zero, 1)
            nc.vector.memset(ones[:, :], 1.0)
            nc.vector.memset(first16[:, :], 0.0).then_inc(f16_ok, 1)
            dve.wait_ge(f16_ok, 1)
            nc.vector.memset(first16[0:META, :], 1.0).then_inc(f16_ok, 1)
            nc.vector.memset(eps[:, :], EPS)
            nc.vector.memset(ss[:, :], 1.0).then_inc(ss_zero, 1)
            dve.wait_ge(ld_pre, 16)

            def input_scaled(t):
                dve.wait_ge(rs_ok, t + 1)
                dve.wait_ge(ld_x[t], 16)
                if t == QT:
                    stt(Xm[:, :], Xm[:, :], ss[0:META, QT:QT + 1], gbc[0:META, :], ALU.mult, ALU.mult).then_inc(xn_ok, 1)
                else:
                    stt(X[:, t, :], X[:, t, :], ss[:, t:t + 1], gbc[:, :], ALU.mult, ALU.mult).then_inc(xn_ok, 1)

            def input_low(t):
                if t == QT:
                    dve.wait_ge(xh_ok, KT + 1)
                    tt(xl[:, :, 0:META], GP[1][:, 0:KT * META].rearrange("p (k m) -> p k m", m=META),
                       xh[:, :, 0:META].bitcast(FP32), ALU.subtract).then_inc(xl_ok, 1)
                    dve.wait_ge(xl_ok, KT + 1)
                    nc.vector.tensor_copy(xm[:, :, META:2 * META], xl[:, :, 0:META].bitcast(FP32)).then_inc(xl_ok, 1)
                    return
                for hf in range(2):
                    dve.wait_ge(xh_ok, 2 * t + hf + 1)
                    c = slice(META + t * P, META + (t + 1) * P)
                    tt(xl[:, 4 * hf:4 * hf + 4, c], bank(2 * (t % 2) + hf).rearrange("p (f n) -> p f n", n=P),
                       xh[:, 4 * hf:4 * hf + 4, c].bitcast(FP32), ALU.subtract).then_inc(xl_ok, 1)

            input_scaled(0)
            for t in range(1, QT):
                input_scaled(t)
                input_low(t - 1)
            input_low(QT - 1)
            input_scaled(QT)
            input_low(QT)
            dve.wait_ge(col_ps, 1)
            nc.vector.tensor_copy(col[:, :], PA[1][:, 0:NROW]).then_inc(col_ok, 1)
            dve.wait_ge(col_ok, 1)
            dve.wait_ge(rq_ok, 1)
            for k in range(2):
                seq(stt(cq[:, k, :], cq[:, k, :], cc("dq", k), rq[:, :], ALU.mult, ALU.mult))
            seq(nc.vector.tensor_copy(cqh[:, :, :], cq[:, :, :]))
            tt(cql[:, :, :], cq[:, :, :], cqh[:, :, :].bitcast(FP32), ALU.subtract).then_inc(cqs_ok, 1)
            dve.wait_ge(ssq_ps, 2)
            whole("ik")
            stt(two(xc), halves(PA[0]), -1.0 / P, two(ki), ALU.mult, ALU.add).then_inc(xc_ok, 1)
            dve.wait_ge(rk_ok, 1)
            dve.wait_ge(xc_ok, 1)
            seq(stt(kn[:, :], xc[:, :], cc("ig"), rk[:, :], ALU.mult, ALU.mult))
            ts(kn[:, :], kn[:, :], cc("ib"), None, ALU.add).then_inc(kn_ok, 1)
            dve.wait_ge(rk_ok, 2)
            stt(kvT[:, :], ckv[:, :], cc("dkv"), rk[:, :], ALU.mult, ALU.mult).then_inc(kvT_ok, 1)
            dve.wait_ge(kvn_ok, 3)
            def topk(i, rounds):
                w = META + P * (i + 1)
                for r in rounds:
                    if r == 0:
                        seq(tt(S[:, i, w - P:w], S[:, i, w - P:w], later_neg[:, :], ALU.add))
                    if r < TOPK // 8:
                        seq(nc.vector.max(top8[:, :], S[:, i, 0:w]))
                        seq(nc.vector.match_replace(S[:, i, 0:w], top8[:, :], S[:, i, 0:w], MARK))
                    if r == TOPK // 8:
                        seq(ts(keep[:, i, 0:w], S[:, i, 0:w], MARK / 2, BIG, ALU.is_gt, ALU.mult))
                        tt(keep[:, i, w - P:w], keep[:, i, w - P:w], later_big[:, :], ALU.max).then_inc(keep_ok, 1)

            dve.wait_ge(masks, 2)
            beside = [(0, r) for r in range(ROUNDS)] + [(1, r) for r in range((QT - 1) * IDX_H - ROUNDS)]
            for v in range(QT * IDX_H):
                i, h = v // IDX_H, v % IDX_H
                w = META + P * (i + 1)
                dve.wait_ge(sc_rl, v + 1)
                if h == 0:
                    ts(S[:, i, 0:w], rl[:, v % 2, 0:w], wi[:, i, h:h + 1], None, ALU.mult).then_inc(sc_acc, 1)
                else:
                    dve.wait_ge(sc_acc, v)
                    stt(S[:, i, 0:w], rl[:, v % 2, 0:w], wi[:, i, h:h + 1], S[:, i, 0:w], ALU.mult, ALU.add).then_inc(sc_acc, 1)
                if i:
                    tile_, r = beside[v - IDX_H]
                    dve.wait_ge(sc_acc, (tile_ + 1) * IDX_H)
                    topk(tile_, [r])
            dve.wait_ge(sc_acc, QT * IDX_H)

            topk(1, range((QT - 1) * IDX_H - ROUNDS, ROUNDS))
            topk(2, range(EARLY))
            dve.wait_ge(table_in, 16)
            rest = [(2, r) for r in range(EARLY, ROUNDS)] + [(3, r) for r in range(ROUNDS)]

            def logits(v):
                i, h = v // DSA_H, v % DSA_H
                w = META + P * (i + 1)
                dve.wait_ge(lg_ps, v + 1)
                if v >= 6:
                    dve.wait_ge(pt_ps, v // 2 - 2)
                nc.vector.tensor_tensor_reduce(out=Ls(v)[:, 0:w], in0=PA[v % 2][:, 0:w],
                                               in1=table[:, h, (QT - 1 - i) * P:(QT - 1 - i) * P + w], scale=1.0,
                                               scalar=3e38, op0=ALU.add, op1=ALU.min, accum_out=low[:, v:v + 1]).then_inc(lg_mn, 1)

            def normalised(g):
                w = META + P * (g // NHEADS2 + 1)
                for v in (2 * g, 2 * g + 1):
                    dve.wait_ge(p_exp, v + 1)
                    seq(nc.vector.reciprocal(prec[:, v:v + 1], psm[:, v:v + 1]))
                    ts(Ls(v)[:, 0:w], Ls(v)[:, 0:w], prec[:, v:v + 1], None, ALU.mult).then_inc(p_nrm, 1)

            for v in range(4):
                logits(v)
            normalised(0)
            for g in range(GROUPS):
                i = g // NHEADS2
                for tile_, r in rest[g + g // 8:g + 1 + (g + 1) // 8]:
                    topk(tile_, [r])
                if i >= 2:
                    dve.wait_ge(pt_ps, g + 1)
                    dve.wait_ge(pv_ps, g - 1)
                    nc.vector.tensor_copy(PT[:, g % 2, 2:i + 1, :],
                                          GP[0][:, SEQ:SEQ + (i - 1) * 2 * P].rearrange("p (j n) -> p j n", j=i - 1)).then_inc(pt_d, 1)
                if g + 1 < GROUPS:
                    normalised(g + 1)
                if g + 2 < GROUPS:
                    logits(2 * g + 4)
                    logits(2 * g + 5)
            for m in range(KT):
                dve.wait_ge(yh_b, m + 1)
                tt(yl[:, m, :], PA[m % 2][:, 0:SEQ], yh[:, m, :].bitcast(FP32), ALU.subtract).then_inc(yl_b, 1)
            for m in range(KT):
                whole(f"gb{m}")
                tt(mix[:, m, :], mix[:, m, :], ready(f"yb{m}")[:, 0:SEQ], ALU.mult).then_inc(gfree[tl[f"yb{m}"].slot], 1)
            nc.vector.memset(AT[:, :, :], 0.0)
            nc.vector.memset(KL[:, :, :], 0.0)
            nc.vector.memset(KHt[:, :], 0.0).then_inc(gla_c, 1)
            dve.wait_ge(gla_c, 1)
            dve.wait_ge(ld_a, 32)

            def values(name, h, part):
                if part < 2:
                    t = tl[f"{name}{h}{'AB'[part]}"]
                    ps = ready(f"{name}{h}{'AB'[part]}")
                    tt(vh[:, h % 2, 2 * part:2 * part + 2, :], ps[:, 0:2 * DV].rearrange("p (t n) -> p t n", t=2),
                       vb[:, h * DV:(h + 1) * DV].unsqueeze(1).broadcast_to([P, 2, DV]), ALU.add).then_inc(gfree[t.slot], 1)
                    return
                ps = ready(f"{name}{h}M")
                dve.wait_ge(f16_ok, 2)
                stt(vm[:, h % 2, :], vb[0:2 * META, h * DV:(h + 1) * DV], first16[:, :], ps[0:2 * META, 0:DV], ALU.mult, ALU.add).then_inc(gfree[tl[f"{name}{h}M"].slot], 1)

            def q_in(h):
                ts(qh[:, h % 2, :], ready(f"gq{h}")[:, 0:SEQ], cc("gq", h), DK ** -0.5, ALU.add, ALU.mult).then_inc(gfree[tl[f"gq{h}"].slot], 1)

            def k_in(h):
                ts(two(kh[:, h % 2, :]), halves(ready(f"gk{h}")), cc("gk", h), None, ALU.add).then_inc(gfree[tl[f"gk{h}"].slot], 1)

            def forget(h):
                ps = ready(f"gg{h}")
                g0 = G[:, h % 2, :]
                dve.wait_ge(gg_l, h + 1)
                ts(two(g0), halves(ps), cc("a2", h), 0.0, ALU.add, ALU.min).then_inc(gfree[tl[f"gg{h}"].slot], 1)
                whole(f"gg{h}")
                seq(tt(gch[:, :], g0, gch[:, :], ALU.subtract))
                nc.vector.tensor_tensor_scan(g0[:, 0:META], ones[:, 0:META], gch[:, 0:META], 0.0, ALU.mult, ALU.add)
                for i in range(QT):
                    s0 = slice(META + i * P, META + (i + 1) * P)
                    ins = nc.vector.tensor_tensor_scan(g0[:, s0], ones[:, :], gch[:, s0], 0.0, ALU.mult, ALU.add)
                ins.then_inc(G_ok, 1)

            def parts(t, B):
                v = t.rearrange("p (n two b) -> p n two b", two=2, b=B)
                return v[:, :, 0, :], v[:, :, 1, :]

            def lv_write(h, l):
                B = LEVELS[l]
                lo_, up = parts(G[:, h % 2, META:ALL], B)
                N = SEQ // (2 * B)
                mid = lo_[:, :, B - 1:B].broadcast_to([P, N, B])
                k = len(LEVELS) * h + l
                if k:
                    dve.wait_ge(lv_qk, k)
                dve.wait_ge(G_ok, h + 1)
                tt(E[:, 0:SEQ // 2].rearrange("p (n b) -> p n b", b=B), up, mid, ALU.subtract)
                tt(E[:, SEQ // 2:SEQ].rearrange("p (n b) -> p n b", b=B), mid, lo_, ALU.subtract).then_inc(lv_w, 1)

            def lv_mul(h, l):
                B = LEVELS[l]
                k = len(LEVELS) * h + l
                dve.wait_ge(lv_e, k + 1)
                if k >= 2:
                    dve.wait_ge(lv_ps, 8 * ((k - 2) // 7) + (k - 2) % 7 + 1)
                _, uq = parts(qh[:, h % 2, :], B)
                lk, _ = parts(kh[:, h % 2, META:ALL], B)
                lo_, _ = parts(KL[:, k % 2, :], B)
                tt(QL[:, k % 2, :].rearrange("p (n b) -> p n b", b=B), uq, E[:, 0:SEQ // 2].rearrange("p (n b) -> p n b", b=B), ALU.mult)
                if k:
                    dve.wait_ge(lv_qk, k)
                tt(lo_, lk, E[:, SEQ // 2:SEQ].rearrange("p (n b) -> p n b", b=B), ALU.mult).then_inc(lv_qk, 1)

            def lv_select(h, l):
                k = 8 * h + l
                dve.wait_ge(lv_ps, k + 1)
                if k == 8 * h and h:
                    dve.wait_ge(av_ps, h)
                if k:
                    dve.wait_ge(lv_sel, k)
                if l < len(LEVELS):
                    B = LEVELS[l]
                    o_ = AT[:, :, 0:P].rearrange("p t (n two b) -> p t n two b", two=2, b=B)[:, :, :, 1, :]
                    m_ = lm[:, l, :].rearrange("p (n b) -> p n b", b=B).unsqueeze(1).broadcast_to([P, QT, 64 // B, B])
                    d_ = bank(k % 4)[:, 0:QT * 64].rearrange("p (t n b) -> p t n b", t=QT, b=B)
                    nc.vector.copy_predicated(o_, m_.bitcast(U32), d_).then_inc(lv_sel, 1)
                else:
                    m_ = ident[:, :].unsqueeze(1).broadcast_to([P, QT, P])
                    nc.vector.copy_predicated(AT[:, :, 0:P], m_.bitcast(U32),
                                              bank(k % 4).rearrange("p (t n) -> p t n", t=QT)).then_inc(lv_sel, 1)

            def off(h):
                dve.wait_ge(od_e, 6 * h + 6)
                seq(tt(KHt[:, :], KHt[:, :], kh[:, h % 2, 0:ALL - P], ALU.mult))
                twice(km[:, h % 2, :], KHt[:, 0:META], km_ok)
                tt(QQ[:, :], QQ[:, :], qh[:, h % 2, :], ALU.mult).then_inc(od_q, 1)
                for q, j in enumerate([2, 1, 0]):
                    dve.wait_ge(od_ps, 4 * h + q + 1)
                    dve.wait_ge(od_q, 4 * h + q + 1)
                    ts(QQ[:, (j + 1) * P:SEQ], QQ[:, (j + 1) * P:SEQ], gf[:, j + 1:j + 2], None, ALU.mult).then_inc(od_q, 1)

            def sum_squares(k):
                dve.wait_ge(av_sq, k + 1)
                tt(sqo[:, 0, :], sqo[:, 0, :], sqo[:, 1, :], ALU.add).then_inc(sum_sq, 1)

            def scaled(k, gname, src):
                dve.wait_ge(av_rs, k + 1)
                for v in range(2):
                    stt(on[:, v, :], src(v), cc(gname, v), rso[:, :], ALU.mult, ALU.mult).then_inc(on_ok, 1)

            def silus(h):
                for v in range(2):
                    m = 2 * h + v
                    dve.wait_ge(sg_ok, m + 1)
                    tt(sgate[:, v, :], gtmp[:, v, :], sgate[:, v, :], ALU.mult).then_inc(silu_ok, 1)

            def branch_out(base, h):
                dve.wait_ge(on_ok, base + 2 * h + 2)
                for v in range(2):
                    if base:
                        whole(f"mo{2 * h + v}")
                    else:
                        dve.wait_ge(silu_ok, 2 * h + v + 1)
                    tt(on[:, v, :], on[:, v, :], sgate[:, v, :], ALU.mult).then_inc(y_ok, 1)

            def low_parts(base, h):
                for v in range(2):
                    m = 2 * h + v
                    dve.wait_ge(ms_ok, base + m + 1)
                    tt(yl[:, m, :], on[:, v, :], yh[:, m, :].bitcast(FP32), ALU.subtract).then_inc(yl_b, 1)

            def finish(h):
                if h:
                    dve.wait_ge(ms_ok, 2 * h)
                    dve.wait_ge(yl_b, KT + 2 * h)
                scaled(h, "hg", lambda v: bank(v))
                branch_out(0, h)

            q_in(0)
            k_in(0)
            forget(0)
            for part in range(3):
                values("gv", 0, part)
            for h in range(HEADS):
                more = h + 1 < HEADS
                lv_write(h, 0)
                lv_mul(h, 0)
                if h:
                    sum_squares(h - 1)
                if more:
                    q_in(h + 1)
                if h:
                    finish(h - 1)
                lv_write(h, 1)
                if more:
                    k_in(h + 1)
                lv_mul(h, 1)
                lv_write(h, 2)
                lv_select(h, 0)
                lv_select(h, 1)
                lv_mul(h, 2)
                lv_write(h, 3)
                if more:
                    forget(h + 1)
                lv_mul(h, 3)
                lv_write(h, 4)
                lv_select(h, 2)
                if h:
                    low_parts(0, h - 1)
                lv_mul(h, 4)
                lv_write(h, 5)
                lv_select(h, 3)
                lv_mul(h, 5)
                lv_write(h, 6)
                lv_select(h, 4)
                lv_mul(h, 6)
                for l in range(5, 8):
                    lv_select(h, l)
                off(h)
                if more:
                    for part in range(3):
                        values("gv", h + 1, part)
                silus(h)
            sum_squares(HEADS - 1)
            finish(HEADS - 1)
            low_parts(0, HEADS - 1)

            def mixing(branch, name):
                for m in range(KT):
                    k = 8 * branch + m
                    dve.wait_ge(gate_ok, k + 1)
                    if k >= 2:
                        dve.wait_ge(mix_ok, k - 1)
                    tt(gtmp[:, m % 2, :], ready(f"{name}{m}")[:, 0:SEQ], gate_store(m), ALU.mult).then_inc(gfree[tl[f"{name}{m}"].slot], 1)
                    whole(f"{name}{m}")
                    tt(mix[:, m, :], mix[:, m, :], gtmp[:, m % 2, :], ALU.add).then_inc(mix_ok, 1)
                    if branch:
                        dve.wait_ge(ms_ok, 16 + m + 1)
                        tt(mixl[:, m, :], mix[:, m, :], mixh[:, m, :].bitcast(FP32), ALU.subtract).then_inc(yl_b, 1)

            mixing(0, "ya")
            nc.vector.memset(zc[:, 0:3], 0.0).then_inc(zpad, 1)
            dve.wait_ge(mix_ok, KT)
            nc.vector.memset(M_[GR, :], 1.0).then_inc(M_one, 1)
            nc.vector.tensor_copy(bcum, small[96:96 + HEADS, :]).then_inc(ms_d, 1)
            dve.wait_ge(ms_d, 1)
            seq(ts(bcum, bcum, col[GR, ROWS["fb"]:ROWS["fb"] + 1], None, ALU.add))
            nc.vector.memset(fbias, 0.0).then_inc(ms_d, 1)
            dve.wait_ge(fl_ok, 1)
            seq(ts(bcum, bcum, 0.0, None, ALU.min))
            seq(tt(lf, bcum, lf, ALU.subtract))
            dve.wait_ge(M_one, 1)
            seq(nc.vector.tensor_tensor_scan(bcum, M, lf, 0.0, ALU.mult, ALU.add))
            seq(tt(u, u, bcum, ALU.subtract))
            twice(um, u[:, 0:META], u_ok)
            seq(nc.vector.tensor_tensor_scan(M, u, u, 0.0, ALU.max, ALU.max))
            stt(bcum, bcum, -1.0, M, ALU.mult, ALU.subtract).then_inc(M_ok, 1)
            dve.wait_ge(uT_ps, 1)
            nc.vector.tensor_copy(uT[:, :, :], bank(0)[:, 0:QT * HEADS].rearrange("p (t h) -> p t h", h=HEADS)).then_inc(uT_ok, 1)
            nc.vector.tensor_copy(uTm[:, :], bank(0)[0:2 * META, QT * HEADS:(QT + 1) * HEADS]).then_inc(uT_ok, 1)
            dve.wait_ge(ld_v, 16)

            def conv(h, q):
                k = 2 * h + q
                dve.wait_ge(zpad, 1)
                whole(f"m{'qk'[q]}{h}")
                if k:
                    dve.wait_ge(qk_ok, k)
                w = lambda tap: cc("cv", tap * 8 + q * 4 + h)
                seq(ts(cv[:, :], zc[:, 0:ALL], w(0), None, ALU.mult))
                for tap in range(1, 4):
                    ins = stt(cv[:, :], zc[:, tap:tap + ALL], w(tap), cv[:, :], ALU.mult, ALU.add)
                    if tap < 3:
                        seq(ins)
                ins.then_inc(cv_ok, 1)

            def conv_mul(h, q):
                k = 2 * h + q
                dve.wait_ge(cs_ok, k + 1)
                dve.wait_ge(cv_ok, k + 1)
                if q == 0:
                    stt(qh[:, h % 2, :], cv[:, META:ALL], DK ** -0.5, sgc[:, META:ALL], ALU.mult, ALU.mult).then_inc(qk_ok, 1)
                else:
                    tt(kh[:, h % 2, :], cv[:, :], sgc[:, :], ALU.mult).then_inc(qk_ok, 1)
                    dve.wait_ge(qk_ok, 2 * h + 2)
                    twice(km[:, h % 2, :], kh[:, h % 2, 0:META], km_ok)

            def masked(h):
                dve.wait_ge(mb_ok, 16 * (h + 1))
                tt(Md[:, :].rearrange("p (t n) -> p t n", t=QT), Mb[:, :].rearrange("p (t n) -> p t n", t=QT),
                   later_bigT[:, :].unsqueeze(1).broadcast_to([P, QT, P]), ALU.add).then_inc(md_ok, 1)

            def weights_of(h, q):
                dve.wait_ge(s_ps, 5 * h + q + 1)
                if h and q == 0:
                    dve.wait_ge(av_ps, HEADS + h)
                b = bank((2 + q) % 4)
                if q == 0:
                    dve.wait_ge(w_ok, 8 * h + 1)
                    tt(ATm[:, :], b[0:2 * META, :], Wm[:, :], ALU.mult).then_inc(at_ok, 1)
                else:
                    j = q - 1
                    dve.wait_ge(w_ok, 8 * h + min(2 * q + 1, 8))
                    tt(AT[:, j, 0:SEQ - j * P], b[:, 0:SEQ - j * P], Wd[:, 0:SEQ - j * P], ALU.mult).then_inc(at_ok, 1)

            def divide(h):
                dve.wait_ge(av_ps, HEADS + h + 1)
                dve.wait_ge(em_ok, h + 1)
                if h:
                    dve.wait_ge(ms_ok, 8 + 2 * h)
                    dve.wait_ge(yl_b, 2 * KT + 2 * h)
                seq(tt(gtmp[:, 0, :], bank(3), emn[:, :], ALU.max))
                seq(stt(gtmp[:, 0, :], bank(3), -1.0, gtmp[:, 0, :], ALU.mult, ALU.max))
                seq(nc.vector.reciprocal(gtmp[:, 1, :], gtmp[:, 0, :]))
                for v in range(2):
                    tt(on[:, v, :], bank(v), gtmp[:, 1, :], ALU.mult).then_inc(num_ok, 1)

            def finish(h):
                dve.wait_ge(num_ok, 2 * h + 2)
                scaled(HEADS + h, "hm", lambda v: on[:, v, :])
                branch_out(8, h)

            for q in range(2):
                conv(0, q)
                conv_mul(0, q)
            for part in range(3):
                values("mv", 0, part)
            for h in range(HEADS):
                more = h + 1 < HEADS
                if h:
                    finish(h - 1)
                masked(h)
                for q in range(3):
                    weights_of(h, q)
                if more:
                    conv(h + 1, 0)
                weights_of(h, 3)
                weights_of(h, 4)
                if more:
                    conv_mul(h + 1, 0)
                    conv(h + 1, 1)
                if h:
                    low_parts(8, h - 1)
                if more:
                    conv_mul(h + 1, 1)
                divide(h)
                if more:
                    for part in range(3):
                        values("mv", h + 1, part)
                sum_squares(HEADS + h)
            finish(HEADS - 1)
            low_parts(8, HEADS - 1)
            mixing(1, "yc")
            dve.wait_ge(ld_h, 16)
            dve.wait_ge(ld_g, 32)

            def add_to_residual(name, t, k, signal):
                for hf in range(2):
                    c = slice(hf * SEQ, (hf + 1) * SEQ)
                    seq(stt(xn[:, t, c], accumulators(name, hf, t), ssf[:, k, t, 0:1], gains[:, 0, c], ALU.mult, ALU.mult))
                    tt(hres[:, t, c], hres[:, t, c], xn[:, t, c], ALU.add).then_inc(signal, 1)

            def scaled_norm(t):
                dve.wait_ge(o_ss, 2 * t + 2)
                for hf in range(2):
                    c = slice(hf * SEQ, (hf + 1) * SEQ)
                    stt(xn[:, t, c], hres[:, t, c], ssf[:, 1, t, 0:1], gains[:, 1, c], ALU.mult, ALU.mult).then_inc(n_ok, 1)

            def low_norm(t):
                for hf in range(2):
                    dve.wait_ge(nh_ok, 2 * t + hf + 1)
                    c = slice(t * P, (t + 1) * P)
                    tt(nl[:, 4 * hf:4 * hf + 4, c], accumulators("out", hf, t).rearrange("p (f n) -> p f n", n=P),
                       nh[:, 4 * hf:4 * hf + 4, c].bitcast(FP32), ALU.subtract).then_inc(nl_ok, 1)

            for t in range(QT):
                dve.wait_ge(o_ss, 2 * t + 1)
                add_to_residual("out", t, 0, h_ok)
                if t >= 2:
                    low_norm(t - 2)
                dve.wait_ge(h_ok, 2 * t + 2)
                scaled_norm(t)
            low_norm(QT - 2)
            low_norm(QT - 1)
            def hidden_low(k):
                dve.wait_ge(U_ok, k % FT + 1)
                dve.wait_ge(uh_ok, k + 1)
                tt(ul[:, k % 4, :], U[:, k % FT, :], uh[:, k % 4, :].bitcast(FP32), ALU.subtract).then_inc(ul_ok, 1)

            for m in range(FT):
                whole(f"up{m}")
                tt(U[:, m, :], U[:, m, :], U[:, m, :], ALU.mult).then_inc(U_ok, 1)
                if m >= FT - 4:
                    hidden_low(m - FT + 4)
            for k in range(4, 2 * FT):
                hidden_low(k)
            dve.wait_ge(ld_g, 48)
            for t in range(QT):
                dve.wait_ge(o_ss, 2 * QT + t + 1)
                add_to_residual("down", t, 2, fin)

        @block.tensor
        def _(pe):
            mm = nc.tensor.matmul

            def rhs(kind, k):
                if kind == "x":
                    return xh[:, k, META:ALL], xl[:, k, META:ALL]
                h_, l_ = {"cq": (cqh, cql), "y": (yh, yl), "n": (nh, nl)}[kind]
                return h_[:, k, :], l_[:, k, :]

            def gemm(name, part=None):
                t = tl[name]
                if part != 1:
                    if t.need:
                        pe.wait_ge(gfree[t.slot], t.need)
                    for c in t.chunks:
                        pe.wait_ge(split_done, chunks[c]["r"] + 1)
                ps = GP[t.slot]
                if t.kind == "F":
                    s0 = chunks[t.chunks[0]]["hl"]
                    for k in (range(t.kt) if part is None else range(part * t.kt // 2, (part + 1) * t.kt // 2)):
                        w = slice(k * t.width + t.off, k * t.width + t.off + t.m)
                        ah, al = rhs(t.rhs, k)
                        for p_, (wt, av, hx) in enumerate([(whi, ah, xh), (whi, al, xl), (wlo, ah, xh)]):
                            st, sp_ = (k == 0 and p_ == 0), (k == t.kt - 1 and p_ == 2)
                            if t.both:
                                for b in range(2):
                                    ins = mm(ps[0:t.m, b * SEQ:b * SEQ + HALF], wt[:, s0, w],
                                             hx[:, k, b * HALF:(b + 1) * HALF], start=st, stop=sp_)
                            else:
                                ins = mm(ps[0:t.m, 0:SEQ], wt[:, s0, w], av, start=st, stop=sp_)
                elif t.kind in ("V", "VM"):
                    s0 = chunks[t.chunks[0]]["hl"]
                    if t.kind == "VM":
                        for k in range(KT):
                            w = slice(k * P, (k + 1) * P)
                            mm(ps[0:2 * META, 0:DV], xm[:, k, :], whi[:, s0:s0 + 2, w], start=(k == 0), stop=False)
                            ins = mm(ps[0:2 * META, 0:DV], xm[:, k, :], wlo[:, s0:s0 + 2, w], start=False, stop=(k == KT - 1))
                    tokens = [] if t.kind == "VM" else [0, 1] if part is None else [part]
                    for i in tokens:
                        tok = slice(META + (t.off + i) * P, META + (t.off + i + 1) * P)
                        o_ = ps[:, i * DV:(i + 1) * DV]
                        for k in range(KT):
                            for p_, (at_, wt) in enumerate([(xh, whi), (xh, wlo), (xl, whi)]):
                                ins = mm(o_, at_[:, k, tok], wt[:, s0:s0 + 2, k * P:(k + 1) * P],
                                         start=(k == 0 and p_ == 0), stop=(k == KT - 1 and p_ == 2))
                else:
                    h = int(name[2:])
                    for b in range(2):
                        ins = mm(ps[:, b * SEQ:b * SEQ + HALF], a2[32:32 + META, h * DK:(h + 1) * DK],
                                 small[32:32 + META, b * HALF:(b + 1) * HALF],
                                 start=True, stop=True)
                if part != 0:
                    ins.then_inc(gemm_done, 1)

            def token_gemm(name, n, hf, parts, tiles=range(QT), last=False):
                c = chunks[tl[f"{name}{hf}_{n}"].chunks[0]]
                pe.wait_ge(split_done, c["r"] + 1)
                stop = n == (4 if name == "out" else FT // 2) - 1
                for k in range(2):
                    ah, al = parts(k)
                    for i in tiles:
                        for p_, (av, wt) in enumerate([(ah, whi), (ah, wlo), (al, whi)]):
                            ins = mm(accumulators(name, hf, i), av[:, i * P:(i + 1) * P], wt[:, c["hl"], k * SEQ:(k + 1) * SEQ],
                                     start=(n == 0 and k == 0 and p_ == 0), stop=(stop and k == 1 and p_ == 2))
                if last:
                    ins.then_inc(gemm_done, 1)
                return ins

            pe.wait_ge(ld_line, 32)
            for c0, c1 in ((0, SEQ), (SEQ, LINE)):
                ins = mm(GP[0][0:DSA_H, c0:c1], t5[:, :], oh[:, c0:c1], start=True, stop=True)
            ins.then_inc(line_ps, 1)
            pe.wait_ge(masks, 1)
            for t in range(QT):
                pe.wait_ge(xn_ok, t + 1)
                if t >= 2:
                    pe.wait_ge(xl_ok, 2 * (t - 1))
                for hf in range(2):
                    for f in range(4):
                        ins = nc.tensor.transpose(bank(2 * (t % 2) + hf)[:, f * P:(f + 1) * P],
                                                  X[:, t, (4 * hf + f) * P:(4 * hf + f + 1) * P], ident[:, :])
                    ins.then_inc(xt_ps, 1)
            def summed(ps, src):
                for b in range(2):
                    ins = mm(ps[:, b * SEQ:b * SEQ + HALF], ones[:, :], src[:, b * HALF:(b + 1) * HALF], start=True, stop=True)
                ins.then_inc(ssq_ps, 1)

            def evacuated(*names):
                for nm in names:
                    pe.wait_ge(gfree[tl[nm].slot], tl[nm].freed)

            pe.wait_ge(xl_ok, KT)
            pe.wait_ge(line_ok, 1)
            gemm("cq0")
            pe.wait_ge(xn_ok, QT + 1)
            for f in range(KT):
                ins = nc.tensor.transpose(GP[1][:, f * META:(f + 1) * META], Xm[:, f * P:(f + 1) * P], ident[0:META, 0:META])
            ins.then_inc(xt_ps, 1)
            pe.wait_ge(ld_rows, 16 * NROWDMA)
            nc.tensor.transpose(PA[1][:, 0:NROW], brow[:, :], ident[0:NROW, 0:NROW]).then_inc(col_ps, 1)
            pe.wait_ge(xl_ok, KT + 2)
            pe.wait_ge(xh_ok, KT + 2)
            gemm("cq1")
            gemm("ik")
            pe.wait_ge(cqsq, 1)
            for k in range(2):
                ins = mm(PA[0][:, 0:SEQ], ones[:, :], sq[:, k, :], start=(k == 0), stop=(k == 1))
            ins.then_inc(ssq_ps, 1)
            gemm("small")
            evacuated("ik")
            pe.wait_ge(rq_ok, 1)
            summed(PA[0], ki)
            gemm("ckv")
            pe.wait_ge(xcsq, 1)
            pe.wait_ge(col_ok, 1)
            summed(PA[1], sqk)
            gemm("gb0")
            pe.wait_ge(kvsq, 1)
            pe.wait_ge(rk_ok, 1)
            summed(PA[1], sqk)
            gemm("gb1")
            pe.wait_ge(kvT_ok, 1)
            pe.wait_ge(xc_ok, 1)
            evacuated("small")
            for t in range(QT):
                nc.tensor.transpose(PA[0][:, t * P:(t + 1) * P], kvT[:, META + t * P:META + (t + 1) * P], ident[:, :])
                nc.tensor.transpose(PA[0][:, WIO + t * IDX_H:WIO + (t + 1) * IDX_H],
                                    small[0:IDX_H, META + t * P:META + (t + 1) * P], ident[0:IDX_H, 0:IDX_H])
            nc.tensor.transpose(PA[0][0:META, QT * P:(QT + 1) * P], kvT[:, 0:META], ident[:, :]).then_inc(kvn_ps, 1)
            pe.wait_ge(cqs_ok, 1)
            for m in range(4):
                gemm(f"iq{m}")
            pe.wait_ge(kn_ok, 1)
            pe.wait_ge(kvn_ok, 3)
            pe.wait_ge(rk_ok, 2)
            for m in range(4):
                evacuated(f"iq{m}")
            for v in range(QT * IDX_H):
                i, h = v // IDX_H, v % IDX_H
                w = META + P * (i + 1)
                if v >= 2:
                    pe.wait_ge(sc_rl, v - 1)
                r = slice(64 * (h % 2), 64 * (h % 2) + 64)
                for c0 in range(0, w, SEQ):
                    ins = mm(PA[v % 2][:, c0:min(c0 + SEQ, w)], qi[r, h // 2, i * P:(i + 1) * P], kn[r, c0:min(c0 + SEQ, w)],
                             start=True, stop=True)
                ins.then_inc(sc_ps, 1)
                if v % 2 and v // 2 < DSA_H - 4:
                    gemm(f"uq{4 + v // 2}")
                if h == IDX_H - 1:
                    gemm(f"gb{2 + i}")
            for h in range(4):
                gemm(f"uq{h}")
            gemm("gb6")
            gemm("gb7")
            evacuated(*[f"uq{h}" for h in range(DSA_H)])
            pe.wait_ge(sc_rl, QT * IDX_H)

            def logits(v):
                i, h = v // DSA_H, v % DSA_H
                w = META + P * (i + 1)
                pe.wait_ge(keep_ok, i + 1)
                if v >= 2:
                    pe.wait_ge(lg_mn, v - 1)
                for c0 in range(0, w, SEQ):
                    c = slice(c0, min(c0 + SEQ, w))
                    mm(PA[v % 2][:, c], qlat[:, h, i * P:(i + 1) * P], kvT[:, c], start=True, stop=False)
                    ins = mm(PA[v % 2][:, c], identb[:, :], keep[:, i, c], start=False, stop=True)
                ins.then_inc(lg_ps, 1)

            for v in range(4):
                logits(v)
            evacuated("gb6", "gb7")
            for g in range(GROUPS):
                i = g // NHEADS2
                pe.wait_ge(p_nrm, 2 * g + 2)
                if g:
                    pe.wait_ge(pt_a, 2 * g)
                    if pt_d_after(g - 1):
                        pe.wait_ge(pt_d, pt_d_after(g - 1))
                for s_ in range(2):
                    v = 2 * g + s_
                    for j in range(i + 1):
                        nc.tensor.transpose(GP[0][:, (2 * j + s_) * P:(2 * j + s_ + 1) * P],
                                            Ls(v)[:, META + j * P:META + (j + 1) * P], ident[:, :])
                    ins = nc.tensor.transpose(GP[1][0:META, (g % 2 * 2 + s_) * P:(g % 2 * 2 + s_ + 1) * P], Ls(v)[:, 0:META], ident[:, :])
                ins.then_inc(pt_ps, 1)
                if g + 2 < GROUPS:
                    logits(2 * g + 4)
                    logits(2 * g + 5)
                pe.wait_ge(pt_a, 2 * g + 2)
                if pt_d_after(g):
                    pe.wait_ge(pt_d, pt_d_after(g))
                if g >= 2:
                    pe.wait_ge(ol_ev, g - 1)
                o_ = GP[1][:, SEQ + (g % 2) * 2 * P:SEQ + (g % 2 + 1) * 2 * P]
                mm(o_, kvm[:, :], PTm[:, g % 2, :], start=True, stop=False)
                for j in range(i + 1):
                    ins = mm(o_, kvn[:, j, :], PT[:, g % 2, j, :], start=False, stop=(j == i))
                ins.then_inc(pv_ps, 1)
            pe.wait_ge(ld_uv, 32)
            pe.wait_ge(ol_ev, GROUPS)
            for m in range(KT):
                if m >= 2:
                    pe.wait_ge(yl_b, m - 1)
                for s_ in range(2):
                    ins = mm(PA[m % 2][:, 0:SEQ], uvp[:, 2 * m + s_, :], qlat[:, 2 * m + s_, :], start=(s_ == 0), stop=(s_ == 1))
                ins.then_inc(uv_ps, 1)
            pe.wait_ge(yl_b, KT - 2)
            gemm("yb0", 0)
            pe.wait_ge(yl_b, KT)
            gemm("yb0", 1)
            for m in range(1, KT):
                gemm(f"yb{m}")
            pe.wait_ge(ld_a, 32)

            def level(h, l):
                k = 8 * h + l
                if l < len(LEVELS):
                    pe.wait_ge(lv_qk, 7 * h + l + 1)
                if k >= 4:
                    pe.wait_ge(lv_sel, k - 3)
                if h and l == 0:
                    pe.wait_ge(on_ok, 2 * h)
                    pe.wait_ge(av_rs, h)
                for i in range(QT):
                    if l < len(LEVELS):
                        b = (7 * h + l) % 2
                        ins = mm(bank(k % 4)[:, i * 64:(i + 1) * 64], KL[:, b, i * P:(i + 1) * P], QL[:, b, i * 64:(i + 1) * 64],
                                 start=True, stop=True)
                    else:
                        ins = mm(bank(k % 4)[:, i * P:(i + 1) * P], kh[:, h % 2, META + i * P:META + (i + 1) * P],
                                 qh[:, h % 2, i * P:(i + 1) * P], start=True, stop=True)
                ins.then_inc(lv_ps, 1)

            def weighted(k, h):
                for v in range(2):
                    c = slice(v * P, (v + 1) * P)
                    mm(bank(v), vm[:, h % 2, c], ATm[:, :], start=True, stop=False)
                    for j in range(QT):
                        ins = mm(bank(v)[:, j * P:SEQ], vh[:, h % 2, j, c], AT[:, j, 0:SEQ - j * P], start=False, stop=(j == QT - 1))
                return ins

            def squares(k):
                pe.wait_ge(sum_sq, k + 1)
                mm(bank(2), ones[:, :], sqo[:, 0, :], start=True, stop=True).then_inc(av_ss, 1)

            for nm in ("gq0", "gk0", "gg0", "gv0A", "gv0B", "gv0M"):
                gemm(nm)
            for h in range(HEADS):
                def nxt(kind, part=None):
                    if h + 1 < HEADS:
                        gemm(f"{kind[0:2]}{h + 1}{kind[2:]}", part)
                    elif kind != "gg":
                        gemm({"gq": "ta0", "gk": "ta1", "gvA": "ta2", "gvB": "ta3", "gvM": "ta4"}[kind], part)

                evacuated(f"gq{h}", f"gk{h}")
                nxt("gq")
                if h:
                    squares(h - 1)
                nxt("gk")
                level(h, 0)
                nxt("gg")
                level(h, 1)
                gemm(f"gr{2 * h}", 0)
                level(h, 2)
                gemm(f"gr{2 * h}", 1)
                level(h, 3)
                gemm(f"gr{2 * h + 1}", 0)
                level(h, 4)
                gemm(f"gr{2 * h + 1}", 1)
                level(h, 5)
                nxt("gvA", 0)
                level(h, 6)
                level(h, 7)
                nxt("gvA", 1)
                pe.wait_ge(lv_sel, 8 * h + 8)
                for q, j in enumerate([2, 1, 0]):
                    pe.wait_ge(od_q, 4 * h + q + 1)
                    mm(bank(q)[:, 0:SEQ - (j + 1) * P], KHt[:, META + j * P:META + (j + 1) * P], QQ[:, (j + 1) * P:SEQ],
                       start=True, stop=True).then_inc(od_ps, 1)
                    if q < 2:
                        nxt("gvB", q)
                pe.wait_ge(od_q, 4 * h + 4)
                pe.wait_ge(km_ok, h + 1)
                mm(bank(3)[0:2 * META, :], km[:, h % 2, :], QQ[:, :], start=True, stop=True).then_inc(od_ps, 1)
                nxt("gvM")
                pe.wait_ge(od_ev, 4 * h + 4)
                evacuated(f"gv{h}A", f"gv{h}B", f"gv{h}M")
                weighted(h, h).then_inc(av_ps, 1)
            gemm("ta5")
            squares(HEADS - 1)
            gemm("ta6")
            gemm("ta7")
            pe.wait_ge(yl_b, 2 * KT)
            for m in range(KT):
                gemm(f"ya{m}")
            gemm("mq0")
            gemm("mk0")
            pe.wait_ge(u_ok, 1)
            idg = ident[GR, GR]
            for t in range(QT):
                nc.tensor.transpose(bank(0)[:, t * HEADS:(t + 1) * HEADS], u[:, META + t * P:META + (t + 1) * P], idg)
            nc.tensor.transpose(bank(0)[0:2 * META, QT * HEADS:(QT + 1) * HEADS], um, idg).then_inc(uT_ps, 1)
            for nm in ("mv0A", "mv0B", "mv0M"):
                gemm(nm)
            pe.wait_ge(M_ok, 1)
            pe.wait_ge(uT_ok, 2)

            def scores(h, q):
                if h and q == 1:
                    pe.wait_ge(num_ok, 2 * h)
                if q == 4:
                    pe.wait_ge(at_ok, 5 * h + 1)
                b = bank((2 + q) % 4)
                if q == 0:
                    ins = mm(b[0:2 * META, :], km[:, h % 2, :], qh[:, h % 2, :], start=True, stop=True)
                else:
                    j = q - 1
                    ins = mm(b[:, 0:SEQ - j * P], kh[:, h % 2, META + j * P:META + (j + 1) * P], qh[:, h % 2, j * P:SEQ],
                             start=True, stop=True)
                ins.then_inc(s_ps, 1)

            for h in range(HEADS):
                def nxt(kind, part=None):
                    if h + 1 < HEADS:
                        gemm(f"{kind[0:2]}{h + 1}{kind[2:]}", part)
                    else:
                        gemm({"mq": "tc0", "mk": "tc1", "mvA": "tc2", "mvB": "tc3", "mvM": "tc4"}[kind], part)

                pe.wait_ge(qk_ok, 2 * h + 2)
                pe.wait_ge(km_ok, HEADS + h + 1)
                nxt("mq", 0)
                if h:
                    squares(HEADS + h - 1)
                nxt("mq", 1)
                if h:
                    pe.wait_ge(av_rs, HEADS + h)
                scores(h, 0)
                scores(h, 1)
                scores(h, 2)
                nxt("mk")
                scores(h, 3)
                scores(h, 4)
                gemm(f"mo{2 * h}")
                gemm(f"mo{2 * h + 1}")
                pe.wait_ge(at_ok, 5 * h + 5)
                evacuated(f"mv{h}A", f"mv{h}B", f"mv{h}M")
                weighted(HEADS + h, h)
                mm(bank(3), ones[0:META, :], ATm[0:META, :], start=True, stop=False)
                for j in range(QT):
                    ins = mm(bank(3)[:, j * P:SEQ], ones[:, :], AT[:, j, 0:SEQ - j * P], start=False, stop=(j == QT - 1))
                ins.then_inc(av_ps, 1)
                nxt("mvA")
                nxt("mvB")
                nxt("mvM")
            squares(2 * HEADS - 1)
            for m in range(5, KT):
                gemm(f"tc{m}")
            pe.wait_ge(yl_b, 3 * KT)
            for m in range(KT):
                gemm(f"yc{m}")
            def mixed(n_):
                return lambda k: (mixh[:, 2 * n_ + k, :], mixl[:, 2 * n_ + k, :])

            pe.wait_ge(on_ok, 4 * HEADS)
            for n_ in range(4):
                pe.wait_ge(yl_b, 3 * KT + 2 * n_ + 2)
                token_gemm("out", n_, 0, mixed(n_), last=True)
            evacuated("yc6", "yc7")

            def transposed(t):
                for hf in range(2):
                    pe.wait_ge(n_ok, 2 * t + hf + 1)
                    for f in range(4):
                        ins = nc.tensor.transpose(accumulators("out", hf, t)[:, f * P:(f + 1) * P],
                                                  xn[:, t, (4 * hf + f) * P:(4 * hf + f + 1) * P], ident[:, :])
                        if t == QT - 2 and hf == 0 and f == 0:
                            ins.then_inc(gemm_done, 1)
                    ins.then_inc(nt_ps, 1)

            for t in range(QT):
                for n_ in range(4):
                    ins = token_gemm("out", n_, 1, mixed(n_), tiles=[t])
                    if t == QT - 1 and n_ < 3:
                        ins.then_inc(gemm_done, 1)
                ins.then_inc(tok_done, 1)
                if t >= 2:
                    transposed(t - 2)
            pe.wait_ge(tok_done, QT)
            for t in range(QT - 2, QT):
                transposed(t)
            pe.wait_ge(nl_ok, 2 * QT - 1)
            gemm("up0", 0)
            pe.wait_ge(nl_ok, 2 * QT)
            gemm("up0", 1)
            for m in range(1, FT):
                gemm(f"up{m}")

            def hidden(n_):
                return lambda k: (uh[:, (2 * n_ + k) % 4, :], ul[:, (2 * n_ + k) % 4, :])

            for n_ in range(FT // 2):
                pe.wait_ge(ul_ok, 2 * n_ + 2)
                token_gemm("down", n_, 0, hidden(n_), last=True)
            evacuated(f"up{FT - 1}", f"up{FT - 2}")
            for n_ in range(FT // 2 - 2):
                pe.wait_ge(ul_ok, FT + 2 * n_ + 2)
                token_gemm("down", n_, 1, hidden(n_), last=True)
            for t, n_ in [(0, 0), (1, 0), (0, 1), (1, 1), (2, 0), (2, 1), (3, 0), (3, 1)]:
                pe.wait_ge(ul_ok, 2 * FT - 2 + 2 * n_)
                ins = token_gemm("down", FT // 2 - 2 + n_, 1, hidden(FT // 2 - 2 + n_), tiles=[t])
                if n_:
                    ins.then_inc(tok_done, 1)


_INS = ["x", "meta_tokens", "t5_bias", "g_pre_mix", "w_in", "b_in", "w_gla_a2", "b_gla_a", "g_gla_head", "w_br_gla",
        "g_dsa_q", "w_dsa_uq", "w_idx_q", "g_dsa_kv", "w_dsa_uv", "idx_ln_g", "idx_ln_b", "w_br_dsa", "ml_conv",
        "ml_f_bias", "g_ml_head", "w_br_ml", "w_out", "g_post_mix", "g_pre_mlp", "w_up", "w_down", "g_post_mlp"]


def bucket_onehot():
    import numpy as np
    import math
    n = np.maximum(LINE - 1 - (P - 1) - np.arange(LINE), 0)
    nf = np.maximum(n, 1).astype(np.float32)
    half = BUCKETS // 2
    large = half + (np.log(nf / np.float32(half)) / np.float32(math.log(128 / half)) * np.float32(half)).astype(np.int32)
    b = np.where(n < half, n, np.minimum(large, BUCKETS - 1))
    return (np.arange(BUCKETS)[:, None] == b[None, :]).astype(np.float32)


def kernel(**inputs):
    import numpy as _np
    import concourse.bacc as _bacc
    from concourse.bass_utils import run_bass_kernel_spmd as _run

    nc = _bacc.Bacc("TRN2", target_bir_lowering=False, num_devices=1)
    arrays, aps = {}, {}
    for name in _INS:
        v = _np.ascontiguousarray(inputs[name])
        arrays[f"in_{name}"] = v
        aps[name] = nc.dram_tensor(f"in_{name}", v.shape, FP32, kind="ExternalInput").ap()
    v = bucket_onehot()
    arrays["in_onehot"] = v
    aps["onehot"] = nc.dram_tensor("in_onehot", v.shape, FP32, kind="ExternalInput").ap()
    line = nc.dram_tensor("bias_line", (DSA_H, LINE), FP32).ap()
    scratch = nc.dram_tensor("line_rows", (P, DSA_H, LPITCH), FP32).ap()
    rows = nc.dram_tensor("gate_rows", (2, HEADS, ALL), FP32).ap()
    out = nc.dram_tensor("out_h", (1, SEQ, D), FP32, kind="ExternalOutput").ap()
    build(nc, aps, line, scratch, rows, out)
    r = _run(nc, [arrays], core_ids=[0])
    return r.results[0]["out_h"]
```
